# Optimizing a Trainium2 kernel written in Bass

```python
import jax
import jax.numpy as jnp
from jax import lax
import numpy as np

D_MODEL = 1024
BATCH = 1
SEQ = 256
DEPTH = 2

DN_ALPHA = (2.0 * DEPTH) ** 0.25
DN_BETA = (8.0 * DEPTH) ** -0.25
LN_EPS = 1e-5

RWKV_WIDTH = D_MODEL // 2
RWKV_HEAD = 64
RWKV_HEADS = RWKV_WIDTH // RWKV_HEAD
RWKV_W_RANK = 64
RWKV_A_RANK = 64
RWKV_G_RANK = 128
RWKV_GN_EPS = 1e-5 * RWKV_HEAD
RWKV_COLS = 3 * RWKV_WIDTH + RWKV_W_RANK + RWKV_A_RANK + RWKV_G_RANK

MLSTM_WIDTH = D_MODEL // 2
MLSTM_HEAD = 128
MLSTM_HEADS = MLSTM_WIDTH // MLSTM_HEAD
MLSTM_CONV = 4
MLSTM_CHUNK = 64
MLSTM_COLS = 4 * MLSTM_WIDTH + 2 * MLSTM_HEADS

FOX_HEAD = 64
FOX_HEADS = D_MODEL // FOX_HEAD
FOX_WIDTH = FOX_HEADS * FOX_HEAD
FOX_QBLOCK = 128
FOX_COLS = 4 * FOX_WIDTH + FOX_HEADS

PEER_HEADS = 8
PEER_NKEYS = 128
PEER_EXPERTS = PEER_NKEYS * PEER_NKEYS
PEER_TOPK = 16
PEER_DKEY = 256
PEER_DHALF = PEER_DKEY // 2
PEER_TOKBLOCK = 128

kernel_name = 'hybrid_rwkv7_mlstm_fox_peer'

def split_cols(p, sizes):
    out, start = [], 0
    for s in sizes:
        out.append(p[..., start:start + s])
        start += s
    return out

def layer_norm(x, g, b):
    xf = x.astype(jnp.float32)
    mu = jnp.mean(xf, -1, keepdims=True)
    var = jnp.mean(jnp.square(xf - mu), -1, keepdims=True)
    return ((xf - mu) * lax.rsqrt(var + LN_EPS) * g + b).astype(x.dtype)

def head_norm(y, g, b, eps):
    yf = y.astype(jnp.float32)
    mu = jnp.mean(yf, -1, keepdims=True)
    var = jnp.mean(jnp.square(yf - mu), -1, keepdims=True)
    return ((yf - mu) * lax.rsqrt(var + eps) * g + b).astype(y.dtype)

def rms_norm(y, g):
    yf = y.astype(jnp.float32)
    return (yf * lax.rsqrt(jnp.mean(yf * yf, -1, keepdims=True) + 1e-6) * g).astype(y.dtype)

def token_shift(z):
    return jnp.pad(z, ((0, 0), (1, 0), (0, 0)))[:, :-1]

def causal_conv(z, w, b):
    c = z.shape[-1]
    out = lax.conv_general_dilated(z, w[:, None, :].astype(z.dtype), window_strides=(1,),
                                   padding=((w.shape[0] - 1, 0),),
                                   dimension_numbers=('NWC', 'WIO', 'NWC'),
                                   feature_group_count=c)
    return out + b

def rwkv7_mix(p, mu, w0, w_up, a0, a_up, g_up, k_k, k_a, r_k, ln_g, ln_b):
    B, S, _ = p.shape
    H, N = RWKV_HEADS, RWKV_HEAD
    f32 = jnp.float32
    p = p + (token_shift(p) - p) * mu
    r, k, v, xw, xa, xg = split_cols(p, (RWKV_WIDTH, RWKV_WIDTH, RWKV_WIDTH,
                                         RWKV_W_RANK, RWKV_A_RANK, RWKV_G_RANK))
    log_w = -jnp.exp(-jax.nn.softplus(-(w0 + jnp.tanh(xw) @ w_up).astype(f32)) - 0.5)
    a = jax.nn.sigmoid((a0 + xa @ a_up).astype(f32))
    g = jax.nn.sigmoid(xg) @ g_up
    heads = lambda t: t.reshape(B, S, H, N)
    kk = heads(k * k_k).astype(f32)
    kk = kk / jnp.maximum(jnp.sqrt(jnp.sum(kk * kk, -1, keepdims=True)), 1e-12)
    k = k.astype(f32) * (1.0 + (a - 1.0) * k_a)
    r_h = heads(r).astype(f32)
    k_h = heads(k)
    v_h = heads(v).astype(f32)
    a_h = heads(a)
    w_h = jnp.exp(heads(log_w))

    def step(state, inp):
        r_t, w_t, k_t, v_t, kk_t, a_t = inp
        s_kk = jnp.einsum('bhvk,bhk->bhv', state, kk_t)
        state = (state * w_t[:, :, None, :]
                 - s_kk[..., None] * (kk_t * a_t)[:, :, None, :]
                 + v_t[..., None] * k_t[:, :, None, :])
        return state, jnp.einsum('bhvk,bhk->bhv', state, r_t)

    seq_first = lambda t: jnp.moveaxis(t, 1, 0)
    state0 = jnp.zeros((B, H, N, N), f32)
    _, y = lax.scan(step, state0, (seq_first(r_h), seq_first(w_h), seq_first(k_h),
                                   seq_first(v_h), seq_first(kk), seq_first(a_h)))
    y = jnp.moveaxis(y, 0, 1)
    y = head_norm(y, ln_g, ln_b, RWKV_GN_EPS)
    y = y + jnp.sum(r_h * k_h * r_k, -1, keepdims=True) * v_h
    return (y.reshape(B, S, RWKV_WIDTH) * g).astype(p.dtype)

def mlstm_chunkwise(q, k, v, ig, lf):
    B, S, H, D = q.shape
    L = MLSTM_CHUNK
    NC = S // L

    def to_chunks(t):
        t = t.reshape((B, NC, L, H) + t.shape[3:])
        return jnp.moveaxis(t, (1, 3), (0, 2))

    causal = jnp.tril(jnp.ones((L, L), dtype=bool))

    def body(carry, inp):
        C, n, m = carry
        qc, kc, vc, igc, lfc = inp
        b = jnp.cumsum(lfc, axis=-1)
        dmat = jnp.where(causal, b[..., :, None] - b[..., None, :] + igc[..., None, :], -jnp.inf)
        inter = b + m[..., None]
        m_t = jnp.maximum(inter, jnp.max(dmat, -1))
        weights = jnp.exp(dmat - m_t[..., None])
        sc = jnp.einsum('bhtd,bhsd->bhts', qc, kc) * weights
        carry_in = jnp.exp(inter - m_t)
        num = (jnp.einsum('bhts,bhsd->bhtd', sc, vc)
               + carry_in[..., None] * jnp.einsum('bhtk,bhkv->bhtv', qc, C))
        den = jnp.sum(sc, -1) + carry_in * jnp.einsum('bhtk,bhk->bht', qc, n)
        h = num / jnp.maximum(jnp.abs(den), jnp.exp(-m_t))[..., None]
        b_last = b[..., -1]
        gs = b_last[..., None] - b + igc
        m_new = jnp.maximum(b_last + m, jnp.max(gs, -1))
        ws = jnp.exp(gs - m_new[..., None])
        keep = jnp.exp(b_last + m - m_new)
        C = keep[..., None, None] * C + jnp.einsum('bhs,bhsk,bhsv->bhkv', ws, kc, vc)
        n = keep[..., None] * n + jnp.einsum('bhs,bhsk->bhk', ws, kc)
        return (C, n, m_new), h

    f32 = jnp.float32
    init = (jnp.zeros((B, H, D, D), f32), jnp.zeros((B, H, D), f32), jnp.zeros((B, H), f32))
    _, h = lax.scan(body, init, (to_chunks(q), to_chunks(k), to_chunks(v),
                                 to_chunks(ig), to_chunks(lf)))
    return jnp.moveaxis(h, (0, 2), (1, 3)).reshape(B, S, H, D)

def mlstm_mix(p, conv_w, conv_b, ig_b, fg_b, hn_g, hn_b):
    B, S, _ = p.shape
    H, N = MLSTM_HEADS, MLSTM_HEAD
    f32 = jnp.float32
    q, k, v, o, ig, fg = split_cols(p, (MLSTM_WIDTH, MLSTM_WIDTH, MLSTM_WIDTH, MLSTM_WIDTH, H, H))
    qk = jax.nn.silu(causal_conv(jnp.concatenate([q, k], -1), conv_w, conv_b))
    q, k = qk[..., :MLSTM_WIDTH], qk[..., MLSTM_WIDTH:]
    heads = lambda t: t.reshape(B, S, H, N).astype(f32)
    q = heads(q) * (N ** -0.5)
    ig = (ig + ig_b).astype(f32)
    lf = jax.nn.log_sigmoid((fg + fg_b).astype(f32))
    h = mlstm_chunkwise(q, heads(k), heads(v), ig, lf)
    h = head_norm(h, hn_g, hn_b, LN_EPS).reshape(B, S, MLSTM_WIDTH).astype(p.dtype)
    return jax.nn.sigmoid(o) * h

def even_mixer(x, w_in, mu, w0, w_up, a0, a_up, g_up, k_k, k_a, r_k, rln_g, rln_b,
               conv_w, conv_b, ig_b, fg_b, hn_g, hn_b, w_out):
    p = x @ w_in
    y_a = rwkv7_mix(p[..., :RWKV_COLS], mu, w0, w_up, a0, a_up, g_up, k_k, k_a, r_k, rln_g, rln_b)
    y_b = mlstm_mix(p[..., RWKV_COLS:], conv_w, conv_b, ig_b, fg_b, hn_g, hn_b)
    return jnp.concatenate([y_a, y_b], -1) @ w_out

def fox_attention(q, k, v, logf):
    B, S, H, D = q.shape
    NB = S // FOX_QBLOCK
    c = jnp.cumsum(logf, axis=1)
    c_key = jnp.transpose(c, (0, 2, 1))[:, :, None, :]
    q_blocks = jnp.moveaxis(q.reshape(B, NB, FOX_QBLOCK, H, D), 1, 0)
    c_blocks = jnp.moveaxis(c.reshape(B, NB, FOX_QBLOCK, H), 1, 0)
    key_pos = jnp.arange(S)
    scale = D ** -0.5

    def one_block(args):
        qb, cb, blk = args
        q_pos = blk * FOX_QBLOCK + jnp.arange(FOX_QBLOCK)
        logits = jnp.einsum('bqhd,bkhd->bhqk', qb, k).astype(jnp.float32) * scale
        logits = logits + jnp.transpose(cb, (0, 2, 1))[..., None] - c_key
        logits = jnp.where(key_pos[None, :] <= q_pos[:, None], logits, -jnp.inf)
        probs = jax.nn.softmax(logits, axis=-1).astype(v.dtype)
        return jnp.einsum('bhqk,bkhd->bqhd', probs, v)

    out = lax.map(one_block, (q_blocks, c_blocks, jnp.arange(NB)))
    return jnp.moveaxis(out, 0, 1).reshape(B, S, H, D)

def odd_mixer(x, w_in, qn_g, kn_g, f_b, w_out):
    B, S, _ = x.shape
    p = x @ w_in
    q, k, v, og, fl = split_cols(p, (FOX_WIDTH, FOX_WIDTH, FOX_WIDTH, FOX_WIDTH, FOX_HEADS))
    heads = lambda t: t.reshape(B, S, FOX_HEADS, FOX_HEAD)
    q = rms_norm(heads(q), qn_g)
    k = rms_norm(heads(k), kn_g)
    logf = jax.nn.log_sigmoid((fl + f_b).astype(jnp.float32))
    o = fox_attention(q, k, heads(v), logf).reshape(B, S, FOX_WIDTH)
    return (jax.nn.sigmoid(og) * o) @ w_out

def peer_ffn(x, w_q, sub_k1, sub_k2, u_tab, v_tab):
    B, S, Dm = x.shape
    K = PEER_TOPK
    xt = x.reshape((B * S) // PEER_TOKBLOCK, PEER_TOKBLOCK, Dm)

    def block(xb):
        T = xb.shape[0]
        q = (xb @ w_q).reshape(T, PEER_HEADS, 2, PEER_DHALF)
        s1 = jnp.einsum('thd,hnd->thn', q[:, :, 0], sub_k1)
        s2 = jnp.einsum('thd,hnd->thn', q[:, :, 1], sub_k2)
        v1, i1 = lax.top_k(s1, K)
        v2, i2 = lax.top_k(s2, K)
        cand = (v1[..., :, None] + v2[..., None, :]).reshape(T, PEER_HEADS, K * K)
        sc, ci = lax.top_k(cand, K)
        e1 = jnp.take_along_axis(i1, ci // K, axis=-1)
        e2 = jnp.take_along_axis(i2, ci % K, axis=-1)
        eid = e1 * PEER_NKEYS + e2
        gate = jax.nn.softmax(sc.astype(jnp.float32), axis=-1).astype(xb.dtype)
        act = jax.nn.gelu(jnp.einsum('td,thkd->thk', xb, u_tab[eid]), approximate=False)
        return jnp.einsum('thk,thkd->td', gate * act, v_tab[eid])

    return lax.map(block, xt).reshape(B, S, Dm)

def setup_inputs(seed: int = 0) -> dict:
    key = jax.random.key(seed)
    keys = iter(jax.random.split(key, 128))
    nk = lambda: next(keys)
    D = D_MODEL
    s_in = D ** -0.5
    nrm = lambda shape, scale: jax.random.normal(nk(), shape, jnp.float32) * scale
    uni = lambda shape, lo, hi: jax.random.uniform(nk(), shape, jnp.float32, minval=lo, maxval=hi)
    gain = lambda shape: 1.0 + 0.1 * jax.random.normal(nk(), shape, jnp.float32)
    bias = lambda shape: 0.01 * jax.random.normal(nk(), shape, jnp.float32)

    def peer_params():
        return (nrm((D, PEER_HEADS * PEER_DKEY), s_in),
                nrm((PEER_HEADS, PEER_NKEYS, PEER_DHALF), PEER_DHALF ** -0.5),
                nrm((PEER_HEADS, PEER_NKEYS, PEER_DHALF), PEER_DHALF ** -0.5),
                nrm((PEER_EXPERTS, D), s_in),
                nrm((PEER_EXPERTS, D), DN_BETA))

    x = jax.random.normal(nk(), (BATCH, SEQ, D), jnp.float32)
    l0_w_in = jnp.concatenate([
        nrm((D, RWKV_WIDTH), s_in), nrm((D, RWKV_WIDTH), s_in), nrm((D, RWKV_WIDTH), s_in * DN_BETA),
        nrm((D, RWKV_W_RANK), s_in), nrm((D, RWKV_A_RANK), s_in), nrm((D, RWKV_G_RANK), s_in),
        nrm((D, MLSTM_WIDTH), s_in), nrm((D, MLSTM_WIDTH), s_in), nrm((D, MLSTM_WIDTH), s_in * DN_BETA),
        nrm((D, MLSTM_WIDTH), s_in), nrm((D, MLSTM_HEADS), s_in), nrm((D, MLSTM_HEADS), s_in)], axis=1)
    l0_rwkv_mu = uni((RWKV_COLS,), 0.0, 1.0)
    l0_rwkv_w0 = uni((RWKV_WIDTH,), -6.0, 1.0)
    l0_rwkv_w_up = nrm((RWKV_W_RANK, RWKV_WIDTH), 0.1)
    l0_rwkv_a0 = nrm((RWKV_WIDTH,), 0.1)
    l0_rwkv_a_up = nrm((RWKV_A_RANK, RWKV_WIDTH), 0.1)
    l0_rwkv_g_up = nrm((RWKV_G_RANK, RWKV_WIDTH), RWKV_G_RANK ** -0.5)
    l0_rwkv_k_k = 0.85 + 0.05 * jax.random.normal(nk(), (RWKV_WIDTH,), jnp.float32)
    l0_rwkv_k_a = gain((RWKV_WIDTH,))
    l0_rwkv_r_k = nrm((RWKV_HEADS, RWKV_HEAD), 0.1)
    l0_rwkv_ln_g = gain((RWKV_HEADS, RWKV_HEAD))
    l0_rwkv_ln_b = bias((RWKV_HEADS, RWKV_HEAD))
    l0_mlstm_conv_w = nrm((MLSTM_CONV, 2 * MLSTM_WIDTH), MLSTM_CONV ** -0.5)
    l0_mlstm_conv_b = bias((2 * MLSTM_WIDTH,))
    l0_mlstm_ig_b = nrm((MLSTM_HEADS,), 0.1)
    l0_mlstm_fg_b = uni((MLSTM_HEADS,), 3.0, 6.0)
    l0_mlstm_hn_g = gain((MLSTM_HEADS, MLSTM_HEAD))
    l0_mlstm_hn_b = bias((MLSTM_HEADS, MLSTM_HEAD))
    l0_w_out = nrm((RWKV_WIDTH + MLSTM_WIDTH, D), (RWKV_WIDTH + MLSTM_WIDTH) ** -0.5 * DN_BETA)
    l0_ln1_g, l0_ln1_b = gain((D,)), bias((D,))
    l0_peer_wq, l0_peer_k1, l0_peer_k2, l0_peer_u, l0_peer_v = peer_params()
    l0_ln2_g, l0_ln2_b = gain((D,)), bias((D,))

    l1_w_in = jnp.concatenate([
        nrm((D, FOX_WIDTH), s_in), nrm((D, FOX_WIDTH), s_in), nrm((D, FOX_WIDTH), s_in * DN_BETA),
        nrm((D, FOX_WIDTH), s_in), nrm((D, FOX_HEADS), s_in)], axis=1)
    l1_fox_qn_g = gain((FOX_HEADS, FOX_HEAD))
    l1_fox_kn_g = gain((FOX_HEADS, FOX_HEAD))
    l1_fox_f_b = uni((FOX_HEADS,), 1.0, 6.0)
    l1_w_out = nrm((FOX_WIDTH, D), FOX_WIDTH ** -0.5 * DN_BETA)
    l1_ln1_g, l1_ln1_b = gain((D,)), bias((D,))
    l1_peer_wq, l1_peer_k1, l1_peer_k2, l1_peer_u, l1_peer_v = peer_params()
    l1_ln2_g, l1_ln2_b = gain((D,)), bias((D,))

    return {
        'x': x,
        'l0_w_in': l0_w_in, 'l0_rwkv_mu': l0_rwkv_mu, 'l0_rwkv_w0': l0_rwkv_w0,
        'l0_rwkv_w_up': l0_rwkv_w_up, 'l0_rwkv_a0': l0_rwkv_a0, 'l0_rwkv_a_up': l0_rwkv_a_up,
        'l0_rwkv_g_up': l0_rwkv_g_up, 'l0_rwkv_k_k': l0_rwkv_k_k, 'l0_rwkv_k_a': l0_rwkv_k_a,
        'l0_rwkv_r_k': l0_rwkv_r_k, 'l0_rwkv_ln_g': l0_rwkv_ln_g, 'l0_rwkv_ln_b': l0_rwkv_ln_b,
        'l0_mlstm_conv_w': l0_mlstm_conv_w, 'l0_mlstm_conv_b': l0_mlstm_conv_b,
        'l0_mlstm_ig_b': l0_mlstm_ig_b, 'l0_mlstm_fg_b': l0_mlstm_fg_b,
        'l0_mlstm_hn_g': l0_mlstm_hn_g, 'l0_mlstm_hn_b': l0_mlstm_hn_b,
        'l0_w_out': l0_w_out, 'l0_ln1_g': l0_ln1_g, 'l0_ln1_b': l0_ln1_b,
        'l0_peer_wq': l0_peer_wq, 'l0_peer_k1': l0_peer_k1, 'l0_peer_k2': l0_peer_k2,
        'l0_peer_u': l0_peer_u, 'l0_peer_v': l0_peer_v, 'l0_ln2_g': l0_ln2_g, 'l0_ln2_b': l0_ln2_b,
        'l1_w_in': l1_w_in, 'l1_fox_qn_g': l1_fox_qn_g, 'l1_fox_kn_g': l1_fox_kn_g,
        'l1_fox_f_b': l1_fox_f_b, 'l1_w_out': l1_w_out, 'l1_ln1_g': l1_ln1_g, 'l1_ln1_b': l1_ln1_b,
        'l1_peer_wq': l1_peer_wq, 'l1_peer_k1': l1_peer_k1, 'l1_peer_k2': l1_peer_k2,
        'l1_peer_u': l1_peer_u, 'l1_peer_v': l1_peer_v, 'l1_ln2_g': l1_ln2_g, 'l1_ln2_b': l1_ln2_b,
    }

def reference(x, l0_w_in, l0_rwkv_mu, l0_rwkv_w0, l0_rwkv_w_up, l0_rwkv_a0, l0_rwkv_a_up,
              l0_rwkv_g_up, l0_rwkv_k_k, l0_rwkv_k_a, l0_rwkv_r_k, l0_rwkv_ln_g, l0_rwkv_ln_b,
              l0_mlstm_conv_w, l0_mlstm_conv_b, l0_mlstm_ig_b, l0_mlstm_fg_b,
              l0_mlstm_hn_g, l0_mlstm_hn_b, l0_w_out, l0_ln1_g, l0_ln1_b,
              l0_peer_wq, l0_peer_k1, l0_peer_k2, l0_peer_u, l0_peer_v, l0_ln2_g, l0_ln2_b,
              l1_w_in, l1_fox_qn_g, l1_fox_kn_g, l1_fox_f_b, l1_w_out, l1_ln1_g, l1_ln1_b,
              l1_peer_wq, l1_peer_k1, l1_peer_k2, l1_peer_u, l1_peer_v, l1_ln2_g, l1_ln2_b):
    mixer_params = (
        (l0_w_in, l0_rwkv_mu, l0_rwkv_w0, l0_rwkv_w_up, l0_rwkv_a0, l0_rwkv_a_up, l0_rwkv_g_up,
         l0_rwkv_k_k, l0_rwkv_k_a, l0_rwkv_r_k, l0_rwkv_ln_g, l0_rwkv_ln_b,
         l0_mlstm_conv_w, l0_mlstm_conv_b, l0_mlstm_ig_b, l0_mlstm_fg_b,
         l0_mlstm_hn_g, l0_mlstm_hn_b, l0_w_out),
        (l1_w_in, l1_fox_qn_g, l1_fox_kn_g, l1_fox_f_b, l1_w_out),
    )
    norm_params = ((l0_ln1_g, l0_ln1_b, l0_ln2_g, l0_ln2_b),
                   (l1_ln1_g, l1_ln1_b, l1_ln2_g, l1_ln2_b))
    peer_params = ((l0_peer_wq, l0_peer_k1, l0_peer_k2, l0_peer_u, l0_peer_v),
                   (l1_peer_wq, l1_peer_k1, l1_peer_k2, l1_peer_u, l1_peer_v))
    for layer in range(DEPTH):
        mixer = even_mixer if layer % 2 == 0 else odd_mixer
        ln1_g, ln1_b, ln2_g, ln2_b = norm_params[layer]
        x = layer_norm(DN_ALPHA * x + mixer(x, *mixer_params[layer]), ln1_g, ln1_b)
        x = layer_norm(DN_ALPHA * x + peer_ffn(x, *peer_params[layer]), ln2_g, ln2_b)
    return x


_drawn_inputs = setup_inputs


def setup_inputs(seed=0):
    import zlib

    import numpy as np

    out = dict(_drawn_inputs(seed))
    spreads = {}
    factors = {'l0_rwkv_ln_b': 3.884,
     'l0_mlstm_conv_b': 4.372,
     'l0_mlstm_ig_b': 64.0,
     'l0_mlstm_hn_b': 4.183,
     'l1_fox_qn_g': 5.716,
     'l1_fox_kn_g': 6.014,
     'l1_ln2_b': 5.616,
     'l1_ln1_b': 2.722}
    for name, (base, spread) in spreads.items():
        noise = np.random.default_rng([zlib.crc32(name.encode()), seed]).standard_normal(out[name].shape)
        drawn = base * np.exp(spread * noise) if base else spread * noise
        out[name] = jnp.asarray(drawn.astype(out[name].dtype))
    for name, factor in factors.items():
        out[name] = (out[name] * factor).astype(out[name].dtype)
    return out
```

```python
from contextlib import ExitStack

import concourse.bass as bass
from concourse import mybir

F32 = mybir.dt.float32
U32 = mybir.dt.uint32
ALU = mybir.AluOpType
ACT = mybir.ActivationFunctionType
AX_X = mybir.AxisListType.X

P = 128
D = 1024
SEQ = 256
NB = SEQ // P
KT = D // P
ALPHA = 4.0 ** 0.25
LN_EPS = 1e-5

RW = 512
RH, RN = 8, 64
RT = RW // P
CH = 64
NCH = SEQ // CH
RWKV_COLS = 3 * RW + 64 + 64 + 128
MW = 512
MH, MN = 4, 128
LEVELS = [2, 4, 8, 16, 32]

FH, FN = 16, 64

EH = 8
NK = 128
TOPK = 16
SLOTS = EH * TOPK
RING = 8
UNROLL = 16
DIAGS = 4

STRIP = 256
WRING = 3
BIG = 3.0e38


def unit_heads():
    return [(b, 2 * q + odd) for b in range(NB) for odd in range(2) for q in range(RH // 2)]


UNITS = unit_heads()
UNIT = {bh: u for u, bh in enumerate(UNITS)}


def parameter_rows():
    rows, at = {}, 0
    for name, n in (("mu", RWKV_COLS // P), ("w0", RT), ("a0", RT), ("k_k", RT), ("k_a", RT), ("r_k", RT),
                    ("ln_g", RT), ("ln_b", RT), ("conv_w", 4 * 8), ("conv_b", 8), ("hn_g", MH), ("hn_b", MH),
                    ("qn_g", 8), ("kn_g", 8)):
        rows[name] = (at, n)
        at += n
    return rows, at


def attention_plan():
    units = FH * NB
    order = []
    for s in range(units + 3):
        if s < units:
            order.append(("att", s))
        if 2 <= s < units + 2:
            order.append(("att_turn", s - 2))
        if s >= 3 and (s - 3) % 2:
            order.append(("att_out", (s - 3) // 2))
    return order


def bank_plan():
    plan = [("params", 1), ("x_turn", 4), ("rwkv_in", 14), ("conv_in", 8), ("vo_in", 4), ("gates_in", 1),
            ("lora_w", 2), ("lora_a", 2), ("lora_g", 2), ("kk_norm", 2), ("bonus", 2), ("token_turn", 6),
            ("scores", 16), ("ab", 4)]
    for m in LEVELS:
        plan.append(("inv_t", 4))
        plan.append(("inv_d", 4 if m == LEVELS[-1] else 8))
    plan += [("mrow_turn", 1), ("mv_turn", 2), ("mx_row", 2), ("qk", 4), ("hnum", 4)]
    for c in range(NCH):
        plan += [("seq_x", 1), ("seq_u", 1), ("seq_y", 1)] + ([("seq_s", 1)] if c < NCH - 1 else [])
    plan += [("y_turn", 4), ("mix_out", 4)]
    peer = [("x_turn", 4), ("key_turn", 4), ("peer_q", 8), ("peer_s", 8), ("experts", 4)]
    plan += peer
    plan += [("x_turn", 4), ("fox_qk", 8), ("fox_v", 4), ("fox_og", 4), ("fox_f", 1), ("fox_rms", 8)]
    plan += [(name, 1) for name, _ in attention_plan()]
    plan += [("mix_out", 4)] + peer
    return plan


def build(nc, T, out, stop=None, dbg=None):
    ROWS, NROWS = parameter_rows()
    ctx = ExitStack()
    with ctx:
        def sb(name, shape, dt=F32):
            return ctx.enter_context(nc.sbuf_tensor(name, shape, dt))

        sems = {}

        def S(name):
            if name not in sems:
                sems[name] = ctx.enter_context(nc.semaphore(name))
            return sems[name]

        psum = ctx.enter_context(nc.psum_tensor("psum", [P, 8, 512], F32))
        order, ticket, seen = [], {}, {}
        for name, n in bank_plan():
            for _ in range(n):
                k = seen.get(name, 0)
                seen[name] = k + 1
                ticket[(name, k)] = len(order)
                order.append((name, k))

        def bank(name, k):
            return psum[:, ticket[(name, k)] % 8, :]

        def claim(pe, name, k):
            n = ticket[(name, k)]
            if n >= 8:
                before, i = order[n - 8]
                pe.wait_ge(S(before + "_taken"), i + 1)
            return bank(name, k)

        def await_filled(eng, name, k):
            eng.wait_ge(S("banks_filled"), ticket[(name, k)] + 1)

        def full(eng, name, k):
            await_filled(eng, name, k)
            return bank(name, k)

        ident = sb("ident", [P, P])
        ident_a = sb("ident_a", [P, P])
        pair_ones = sb("pair_ones", [P, P])
        ones = sb("ones", [P, SEQ])
        score_mask = sb("score_mask", [P, 2, P])
        level_mask = sb("level_mask", [P, 6, P])
        level_one = sb("level_one", [P, P])
        causal_st = sb("causal_st", [P, 3 * P])
        causal_ts = sb("causal_ts", [P, SEQ + P])
        iota16 = sb("iota16", [P, TOPK])
        pars = sb("pars", [P, P])
        one_mu = sb("one_mu", [P, RWKV_COLS // P])
        kn8 = sb("kn8", [P, 8])
        small = sb("small", [P, 4])
        cexp = sb("cexp", [P, 6])

        def par(name, i=0):
            at, n = ROWS[name]
            return pars[:, at + i:at + i + 1]

        xres = sb("xres", [P, NB, D])
        xT = sb("xT", [P, KT, SEQ])
        ln_par = sb("ln_par", [P, 2, D])
        lnst = sb("lnst", [P, NB, 12])
        lnmv = sb("lnmv", [P, NB, 2])
        lnrs = sb("lnrs", [P, NB])
        wring = sb("wring", [P, WRING, KT, STRIP])
        ARENA = 36352
        A = sb("arena", [P, ARENA])

        def cut(at, n):
            assert at + n <= ARENA, (at, n)
            return A[:, at:at + n]

        strips = []

        def add_strips(w, c0, c1, name, first, per):
            for i, c in enumerate(range(c0, c1, STRIP)):
                strips.append((T[w][:, c:min(c + STRIP, c1)].rearrange("(k p) n -> p k n", p=P),
                               min(STRIP, c1 - c), name, first + (i + 1) * per - 1))

        def peer_strips(l):
            add_strips(f"l{l}_peer_wq", 0, 2048, "peer_q", 8 * l, 1)

        M0 = RWKV_COLS
        add_strips("l0_w_in", 0, M0, "rwkv_in", 0, 2)
        add_strips("l0_w_in", M0, M0 + 2 * MW, "conv_in", 0, 2)
        add_strips("l0_w_in", M0 + 2 * MW, M0 + 4 * MW, "vo_in", 0, 1)
        add_strips("l0_w_in", M0 + 4 * MW, M0 + 4 * MW + 2 * MH, "gates_in", 0, 1)
        add_strips("l0_w_out", 0, D, "mix_out", 0, 1)
        peer_strips(0)
        add_strips("l1_w_in", 0, 2 * D, "fox_qk", 0, 1)
        add_strips("l1_w_in", 2 * D, 3 * D, "fox_v", 0, 1)
        add_strips("l1_w_in", 3 * D, 4 * D, "fox_og", 0, 1)
        strips_before_f = len(strips)
        add_strips("l1_w_in", 4 * D, 4 * D + FH, "fox_f", 0, 1)
        add_strips("l1_w_out", 0, D, "mix_out", 4, 1)
        peer_strips(1)

        strip_at = [0]

        def next_strip(pe):
            n = strip_at[0]
            strip_at[0] += 1
            pe.wait_ge(S(f"strip_loaded{n % WRING}"), 16 * (n // WRING + 1))
            return wring[:, n % WRING]

        prows = cut(24064, P)
        R = cut(0, 14 * SEQ)
        r_all, k_all, v_all = cut(0, 1024), cut(1024, 1024), cut(2048, 1024)
        xwa, xg = cut(3072, SEQ), cut(3328, SEQ)
        waup, gup = cut(3584, RW), cut(4096, RW)
        mq_all, mk_all, mv_all, mo_all = (cut(4608 + 1024 * i, 1024) for i in range(4))
        AR = cut(8704, 2048).rearrange("p (t b two n) -> p t b two n", t=RT, b=NB, two=2)
        beta_all, kappa_all, g_all, bonus_all = (cut(10752 + 1024 * i, 1024) for i in range(4))
        v_tok = cut(14848, 1024).rearrange("p (b c) -> p b c", b=NB)
        beta_tok = cut(0, 1024).rearrange("p (b c) -> p b c", b=NB)
        kappa_tok = cut(1024, 1024).rearrange("p (b c) -> p b c", b=NB)
        y_tok = cut(2048, 1024)
        SC = cut(15872, 8192).rearrange("p (u f n) -> p u f n", u=16, f=4)
        a_all, logw, cumw, pinv, pprev, pfull, kk_all, tmp = (cut(24064 + 1024 * i, 1024) for i in range(8))
        Dm, DT, Tm, LM = (cut(24064 + 2048 * i, 2048).rearrange("p (u n) -> p u n", u=16) for i in range(4))
        vaug = cut(32256, NB * MH * 132).rearrange("p (b h n) -> p b h n", b=NB, h=MH)
        scT = cut(33312, MH * 384).rearrange("p (h n) -> p h n", h=MH)
        seq_x, seq_u = cut(34848, RW), cut(35360, RW)
        state = cut(35872, RT * RN).rearrange("p (t n) -> p t n", t=RT)
        h_tok = mq_all
        yT = cut(8704, 2048).rearrange("p (k n) -> p k n", k=KT)
        mr = sb("mrows", [MH, 6, SEQ])
        pend = sb("pend", [P, RT, NCH])
        gcol = sb("gcol", [P, 4 * MH])
        stat = sb("stat", [P, 4, 16])
        dcol = sb("dcol", [P, 8])

        ring_u = cut(0, RING * D).rearrange("p (j n) -> p j n", j=RING)
        ring_v = cut(8192, RING * D).rearrange("p (j n) -> p j n", j=RING)
        keyT = cut(16384, 2048).rearrange("p (i n) -> p i n", i=16)
        keys = cut(18432, 2048).rearrange("p (i n) -> p i n", i=16)
        cand = cut(18432, 2048).rearrange("p (h n) -> p h n", h=EH)
        qT = cut(20480, 4096).rearrange("p (i n) -> p i n", i=16)
        sc = cut(24576, 4096).rearrange("p (b i n) -> p b i n", b=NB, i=16)
        scr = cut(28672, 2048)
        onehot = cut(30720, 2048).rearrange("p (h k j) -> p h k j", h=EH, k=TOPK)
        v16 = cut(32768, 256).rearrange("p (i k) -> p i k", i=16)
        i16f = cut(33024, 256).rearrange("p (h two k) -> p h two k", h=EH, two=2)
        csc = cut(33280, SLOTS).rearrange("p (h k) -> p h k", h=EH)
        hilo = cut(33408, 2 * SLOTS).rearrange("p (w h k) -> p w h k", w=2, h=EH)
        e12 = cut(33664, 2 * SLOTS).rearrange("p (w h k) -> p w h k", w=2, h=EH)
        eidf = cut(33920, SLOTS)
        gate = cut(34048, NB * SLOTS).rearrange("p (b s) -> p b s", b=NB)
        hid = cut(34304, NB * SLOTS).rearrange("p (b s) -> p b s", b=NB)
        ga = cut(34560, NB * SLOTS).rearrange("p (b s) -> p b s", b=NB)
        diag = cut(34816, DIAGS * P).rearrange("p (j n) -> p j n", j=DIAGS)
        gsum = cut(35328, 2 * EH)
        hstage = cut(35344, 2 * RING).rearrange("p (k j) -> p k j", k=2)
        gstage = cut(35360, 2 * RING).rearrange("p (k j) -> p k j", k=2)
        uints = cut(35376, 944).bitcast(U32)
        i16 = uints[:, 0:256].rearrange("p (i k) -> p i k", k=TOPK)
        pos = uints[:, 256:384].rearrange("p (h k) -> p h k", k=TOPK)
        hilo_u = uints[:, 384:640].rearrange("p (w s) -> p w s", w=2)
        eid = uints[:, 640:896].rearrange("p (b s) -> p b s", b=NB)
        ustage = uints[:, 896:912].rearrange("p (k j) -> p k j", k=2)
        vstage = uints[:, 912:928].rearrange("p (k j) -> p k j", k=2)

        QK = cut(0, 4096).rearrange("p (t n) -> p t n", t=16)
        SQ = cut(4096, 4096).rearrange("p (t n) -> p t n", t=16)
        RS = cut(8192, 4096).rearrange("p (t n) -> p t n", t=16)
        lg = cut(4096, 4 * SEQ).rearrange("p (j n) -> p j n", j=4)
        prob = cut(5120, 4 * SEQ).rearrange("p (j n) -> p j n", j=4)
        probT = cut(6144, 4 * SEQ).rearrange("p (j s n) -> p j s n", j=4, s=2)
        fv = cut(12288, 2048).rearrange("p (b n) -> p b n", b=NB)
        ogT = cut(14336, 2048).rearrange("p (t n) -> p t n", t=KT)
        oT = cut(16384, 2048).rearrange("p (t n) -> p t n", t=KT)
        frow = cut(18432, 4 * SEQ).rearrange("p (j n) -> p j n", j=4)
        fw = cut(20480, KT * P).rearrange("p (k n) -> p k n", k=KT)
        amax = cut(19456, 32)
        asum = cut(19488, 32)
        arec = cut(19520, 32)

        class Steps:

            def __init__(self, eng, name):
                self.eng, self.sem, self.n = eng, S(name), 0

            def then(self, ins):
                ins.then_inc(self.sem, 1)
                self.n += 1

            def settle(self):
                self.eng.wait_ge(self.sem, self.n)

        block = ctx.enter_context(nc.Block())
        R2 = lambda ap: ap.rearrange("(r c) -> r c", c=P)

        @block.sync
        def _(sp):
            used = [0]

            def load_strips(n):
                for _ in range(n):
                    i = used[0]
                    used[0] += 1
                    src, w, _, _ = strips[i]
                    if i >= WRING:
                        await_filled(sp, strips[i - WRING][2], strips[i - WRING][3])
                    sp.dma_start(wring[:, i % WRING, :, 0:w], src).then_inc(S(f"strip_loaded{i % WRING}"), 16)

            sp.dma_start(xres[:], T["x"].rearrange("o (b p) d -> p (o b) d", p=P)).then_inc(S("x_loaded"), 16)
            load_strips(2)
            srcs = [("mu", T["l0_rwkv_mu"]), ("w0", T["l0_rwkv_w0"]), ("a0", T["l0_rwkv_a0"]), ("k_k", T["l0_rwkv_k_k"]),
                    ("k_a", T["l0_rwkv_k_a"])]
            for name, src in srcs:
                at, n = ROWS[name]
                sp.dma_start(prows[at:at + n, :], R2(src)).then_inc(S("params_loaded"), 16)
            for name, src in (("r_k", "l0_rwkv_r_k"), ("ln_g", "l0_rwkv_ln_g"), ("ln_b", "l0_rwkv_ln_b"),
                              ("qn_g", "l1_fox_qn_g"), ("kn_g", "l1_fox_kn_g")):
                at, n = ROWS[name]
                sp.dma_start(prows[at:at + n, :], T[src].rearrange("(t h) n -> t (h n)", h=2)).then_inc(S("params_loaded"), 16)
            at, n = ROWS["conv_w"]
            sp.dma_start(prows[at:at + n, :], T["l0_mlstm_conv_w"].rearrange("j (t c) -> (j t) c", c=P)).then_inc(S("params_loaded"), 16)
            at, n = ROWS["conv_b"]
            sp.dma_start(prows[at:at + n, :], R2(T["l0_mlstm_conv_b"])).then_inc(S("params_loaded"), 16)
            for name in ("hn_g", "hn_b"):
                at, n = ROWS[name]
                sp.dma_start(prows[at:at + n, :], T["l0_mlstm_" + name]).then_inc(S("params_loaded"), 16)
            sp.wait_ge(S("constants"), 1)
            for i, lo, name, n in ((0, 0, "l0_mlstm_ig_b", MH), (1, 0, "l0_mlstm_fg_b", MH), (2, 0, "l1_fox_f_b", FH),
                                   (2, 64, "l1_fox_f_b", FH)):
                sp.dma_start(small[lo:lo + n, i:i + 1], T[name].rearrange("(h o) -> h o", o=1)).then_inc(S("small_loaded"), 16)
            sp.dma_start(waup[0:64, :], T["l0_rwkv_w_up"]).then_inc(S("ups_loaded"), 16)
            sp.dma_start(waup[64:128, :], T["l0_rwkv_a_up"]).then_inc(S("ups_loaded"), 16)
            sp.dma_start(gup, T["l0_rwkv_g_up"]).then_inc(S("ups_loaded"), 16)

            def load_ln(i, g, b):
                if i:
                    sp.wait_ge(S("x_normed"), 2 * i)
                sp.dma_start(ln_par[:, 0, :], T[g].partition_broadcast(P)).then_inc(S("ln_loaded"), 16)
                sp.dma_start(ln_par[:, 1, :], T[b].partition_broadcast(P)).then_inc(S("ln_loaded"), 16)

            def load_keys(l):
                sp.wait_ge(S("x_normed"), 4 * l + 2)
                for half in range(2):
                    sp.dma_start(keys[:, half * EH:half * EH + EH, :],
                                 T[f"l{l}_peer_k{half + 1}"].rearrange("h n d -> n h d")).then_inc(S("keys_loaded"), 16)

            load_ln(0, "l0_ln1_g", "l0_ln1_b")
            load_strips(16 - 2)
            if stop == "mix0":
                load_strips(4)
            else:
                load_strips(4)
                load_keys(0)
                load_ln(1, "l0_ln2_g", "l0_ln2_b")
                load_strips(8)
            if stop is None:
                load_ln(2, "l1_ln1_g", "l1_ln1_b")
                load_strips(17 + 4)
                load_keys(1)
                load_ln(3, "l1_ln2_g", "l1_ln2_b")
                load_strips(8)
            last = {"mix0": 2, "peer0": 4, None: 8}[stop]
            for b in range(NB):
                sp.wait_ge(S("x_normed"), last - 1 + b)
                sp.dma_start(out[0, b * P:(b + 1) * P, :], xres[:, b, :]).then_inc(S("stored"), 16)
            if dbg is not None:
                if dbg[1] == "seq":
                    pass
                sp.dma_start(dbg[0], dbg_src(dbg[1])).then_inc(S("stored"), 16)
                sp.wait_ge(S("stored"), 16 * 3)
            sp.wait_ge(S("stored"), 16 * NB)

        def dbg_src(name):
            return {"hid": hid, "eid": eid, "gate": gate}[name]

        @block.gpsimd
        def _(pool):
            st = Steps(pool, "pool_step")
            for t, v in ((ident, 1.0), (ident_a, ALPHA / 2), (pair_ones, 1.0), (ones, 1.0), (score_mask, 1.0),
                         (level_mask, 1.0), (level_one, 1.0), (small, 0.0), (causal_st, 1.0), (causal_ts, 0.0), (cexp, 1.0)):
                st.then(pool.memset(t[:], v))
            st.then(pool.memset(vaug, 1.0))
            st.settle()
            for i, eps in enumerate((LN_EPS, 1e-5 * RN, FN * 1e-6)):
                st.then(pool.memset(cexp[:, 2 + i:3 + i], eps))
            st.then(pool.iota(iota16[:], pattern=[[1, TOPK]], base=0, channel_multiplier=0,
                              allow_small_or_imprecise_dtypes=True))
            st.settle()

            def keep(ap, pattern, base, mult, op=ALU.is_ge, fill=0.0):
                st.then(pool.affine_select(out=ap, in_=ap, compare_op=op, fill=fill, base=base, pattern=pattern,
                                           channel_multiplier=mult))

            keep(ident[:], [[1, P]], 0, -1, ALU.is_equal)
            keep(ident_a[:], [[1, P]], 0, -1, ALU.is_equal)
            keep(pair_ones[:, 0:64], [[0, 64]], 63, -1)
            keep(pair_ones[:, 64:128], [[0, 64]], -64, 1)
            for i in range(2):
                keep(score_mask[:, i, :], [[1, P]], -1 if i % 2 == 0 else 0, -1)
            keep(causal_st[:, 0:P], [[1, P]], 0, -1)
            keep(causal_st[:, 2 * P:3 * P], [[1, P]], 0, -1)
            keep(causal_ts[:, SEQ:SEQ + P], [[-1, P]], 0, 1, ALU.is_ge, -1e30)
            keep(cexp[:, 0:1], [[0, 1]], -1000, 1)
            for i, m in enumerate([1] + LEVELS):
                v = level_mask[:, i, :].rearrange("p (g two m) -> p g two m", two=2, m=m)
                st.then(pool.memset(v[:, :, 0, :], 0.0))
            v = level_one[:].rearrange("p (g two) -> p g two", two=2)
            st.then(pool.memset(v[:, :, 1], 0.0))
            st.settle()
            for i in range(2):
                keep(score_mask[:, i, CH:P], [[0, CH]], -CH, 1)
            for i, m in enumerate([1] + LEVELS):
                v = level_mask[:, i, :].rearrange("p (g two m) -> p g two m", two=2, m=m)[:, :, 1, :]
                keep(v, [[-2 * m, P // (2 * m)], [0, m]], 0, 1)
            v = level_one[:].rearrange("p (g two) -> p g two", two=2)[:, :, 0]
            keep(v, [[-2, P // 2]], -1, 1)
            st.settle()
            for i, m in enumerate([1] + LEVELS):
                v = level_mask[:, i, :].rearrange("p (g two m) -> p g two m", two=2, m=m)[:, :, 1, :]
                keep(v, [[2 * m, P // (2 * m)], [0, m]], m - 1, -1)
            v = level_one[:].rearrange("p (g two) -> p g two", two=2)[:, :, 0]
            keep(v, [[2, P // 2]], 1, -1)
            st.settle()
            pool.sem_inc(S("constants"), 1)

            def gather(tab, ring, stage, j, k, sem, free, g):
                pool.wait_ge(free, g + 1)
                pool.sem_inc(S("gathers_issued"), 1)
                pool.indirect_dma_start(out=ring[:, j, :], out_offset=None, in_=tab,
                                        in_offset=bass.IndirectOffsetOnAxis(ap=stage[:, k, j:j + 1], axis=0)
                                        ).then_inc(S(f"{sem}{j}"), 16)

            staged = [0]

            def gathers(l, u, v):
                if u is not None:
                    pool.wait_ge(S("experts_chosen"), 2 * l + u + 1)
                nt = (u is not None) + (v is not None)
                base = staged[0]
                with pool.Fori(0, SLOTS // UNROLL) as i:
                    for k in range(UNROLL // RING):
                        n = 0
                        for which, tab, ring, stage, free in (
                                (u, T[f"l{l}_peer_u"], ring_u, ustage, S("u_rows_done")),
                                (v, T[f"l{l}_peer_v"], ring_v, vstage, S("v_rows_done"))):
                            if which is None:
                                continue
                            g0 = SLOTS * (2 * l + which) + RING * k
                            pool.wait_ge(free, i * UNROLL + g0 + 1)
                            pool.tensor_copy(stage[:, k, :], eid[:, which, bass.ds(i * UNROLL + RING * k, RING)]
                                             ).then_inc(S("indices_staged"), 1)
                            n += 1
                        pool.wait_ge(S("indices_staged"), i * (nt * UNROLL // RING) + (base + nt * (k + 1)))
                        for j in range(RING):
                            if u is not None:
                                gather(T[f"l{l}_peer_u"], ring_u, ustage, j, k, "u_row", S("u_rows_done"),
                                       i * UNROLL + (SLOTS * (2 * l + u) + RING * k + j))
                            if v is not None:
                                gather(T[f"l{l}_peer_v"], ring_v, vstage, j, k, "v_row", S("v_rows_done"),
                                       i * UNROLL + (SLOTS * (2 * l + v) + RING * k + j))
                staged[0] += nt * SLOTS // RING

            for l in range({"mix0": 0, "peer0": 1, None: 2}[stop]):
                gathers(l, 0, None)
                gathers(l, 1, 0)
                gathers(l, None, 1)

        @block.tensor
        def _(pe):
            mm, tp = nc.tensor.matmul, nc.tensor.transpose

            filled = [0]

            def done(ins, name):
                assert order[filled[0]][0] == name
                filled[0] += 1
                ins.then_inc(S("banks_filled"), 1)

            def turn_x(first, b, i):
                for half in range(2):
                    ps = claim(pe, "x_turn", first + half).rearrange("p (k n) -> p k n", k=4)
                    for q in range(4):
                        c = (4 * half + q) * P
                        last = tp(ps[:, q, :], xres[:, b, c:c + P], ident[:])
                    done(last, "x_turn")

            def project(ps, w, c0, cols):
                for k in range(KT):
                    last = mm(ps, w[:, k, c0:c0 + cols], xT[:, k, :], start=(k == 0), stop=(k == KT - 1))
                return last

            def mixer0():
                pe.wait_ge(S("constants"), 1)
                pe.wait_ge(S("params_loaded"), 16 * 14)
                done(tp(claim(pe, "params", 0)[:, 0:NROWS], prows[0:NROWS, :], ident[0:NROWS, 0:NROWS]), "params")
                pe.wait_ge(S("x_loaded"), 16)
                for b in range(NB):
                    turn_x(2 * b, b, 0)
                pe.wait_ge(S("x_turn_taken"), 4)
                for name, n in (("rwkv_in", 14), ("conv_in", 8)):
                    for t in range(n):
                        if t % 2 == 0:
                            w = next_strip(pe)
                        done(project(claim(pe, name, t)[:, 0:SEQ], w, P * (t % 2), P), name)
                for t in range(4):
                    w = next_strip(pe)
                    ps = claim(pe, "vo_in", t)
                    for q in range(2):
                        last = project(ps[:, q * SEQ:(q + 1) * SEQ], w, P * q, P)
                    done(last, "vo_in")
                w = next_strip(pe)
                ps = claim(pe, "gates_in", 0)
                project(ps[0:MH, 0:SEQ], w, 0, MH)
                done(project(ps[0:MH, SEQ:2 * SEQ], w, MH, MH), "gates_in")

                pe.wait_ge(S("ups_loaded"), 48)
                pe.wait_ge(S("lora_squashed"), 1)
                for name, lo, hi, up, low in (("lora_w", 0, 64, waup, xwa), ("lora_a", 64, 128, waup, xwa),
                                              ("lora_g", 0, 128, gup, xg)):
                    if name == "lora_g":
                        pe.wait_ge(S("lora_squashed"), 2)
                    for half in range(2):
                        ps = claim(pe, name, half)
                        for q in range(2):
                            t = 2 * half + q
                            last = mm(ps[:, q * SEQ:(q + 1) * SEQ], up[lo:hi, t * P:(t + 1) * P], low[lo:hi, :],
                                      start=True, stop=True)
                        done(last, name)
                for name, ready in (("kk_norm", 1), ("bonus", 2)):
                    pe.wait_ge(S("head_products"), ready)
                    for half in range(2):
                        done(mm(claim(pe, name, half), pair_ones[:], tmp[:, half * 512:(half + 1) * 512],
                                start=True, stop=True), name)
                pe.wait_ge(S("scan_operands"), 1)
                for i, src in enumerate((v_all, beta_all, kappa_all)):
                    for b in range(NB):
                        ps = claim(pe, "token_turn", NB * i + b).rearrange("p (t n) -> p t n", t=RT)
                        for t in range(RT):
                            last = tp(ps[:, t, :], src[:, t * SEQ + b * P:t * SEQ + (b + 1) * P], ident[:])
                        done(last, "token_turn")
                for u in range(16):
                    b, h = UNITS[u]
                    t, lo = h // 2, 64 * (h % 2)
                    ps = claim(pe, "scores", u)
                    ar = AR[lo:lo + 64, t, b, :, :].rearrange("p two n -> p (two n)")
                    c = t * SEQ + b * P
                    mm(ps[:, 0:256], beta_all[lo:lo + 64, c:c + P], ar, start=True, stop=True)
                    done(mm(ps[:, 256:512], kappa_all[lo:lo + 64, c:c + P], ar, start=True, stop=True), "scores")
                for g in range(4):
                    ps = claim(pe, "ab", g).rearrange("p (u n) -> p u n", u=4)
                    for q in range(4):
                        u = 4 * g + q
                        b, h = UNITS[u]
                        t, lo = h // 2, 64 * (h % 2)
                        c = t * SEQ + b * P
                        last = mm(ps[:, q, :], AR[lo:lo + 64, t, b, 0, :], beta_all[lo:lo + 64, c:c + P],
                                  start=True, stop=True)
                    done(last, "ab")
                nt = nd = 0
                for i, m in enumerate(LEVELS):
                    last_level = m == LEVELS[-1]
                    for g in range(4):
                        pe.wait_ge(S("merge_ready"), 4 * i + g + 1)
                        ps = claim(pe, "inv_t", nt).rearrange("p (u n) -> p u n", u=4)
                        for q in range(4):
                            last = mm(ps[:, q, :], LM[:, 4 * g + q, :], Dm[:, 4 * g + q, :], start=True, stop=True)
                        done(last, "inv_t")
                        nt += 1
                    for g in range(4):
                        pe.wait_ge(S("inv_t_taken"), 4 * i + g + 1)
                        if not last_level:
                            ps = claim(pe, "inv_d", nd).rearrange("p (u n) -> p u n", u=4)
                            for q in range(4):
                                last = mm(ps[:, q, :], DT[:, 4 * g + q, :], Tm[:, 4 * g + q, :], start=True, stop=True)
                            done(last, "inv_d")
                            nd += 1
                        ps = claim(pe, "inv_d", nd).rearrange("p (u n) -> p u n", u=4)
                        for q in range(4):
                            last = mm(ps[:, q, :], Tm[:, 4 * g + q, :], DT[:, 4 * g + q, :], start=True, stop=True)
                        done(last, "inv_d")
                        nd += 1

                pe.wait_ge(S("m_rows"), 1)
                ps = claim(pe, "mrow_turn", 0)
                for i, row in enumerate((2, 5)):
                    for b in range(NB):
                        c = (2 * i + b) * MH
                        last = tp(ps[:, c:c + MH], mr[0:MH, row, b * P:(b + 1) * P], ident[0:MH, 0:MH])
                done(last, "mrow_turn")
                for b in range(NB):
                    ps = claim(pe, "mv_turn", b).rearrange("p (h n) -> p h n", h=MH)
                    for h in range(MH):
                        last = tp(ps[:, h, :], mv_all[:, h * SEQ + b * P:h * SEQ + (b + 1) * P], ident[:])
                    done(last, "mv_turn")
                for i in range(2):
                    ps = claim(pe, "mx_row", i)
                    for q in range(2):
                        h = 2 * i + q
                        last = mm(ps[:, q * SEQ:(q + 1) * SEQ], ident[0:MH, h:h + 1].to_broadcast([MH, P]),
                                  mr[0:MH, 4, :], start=True, stop=True)
                    done(last, "mx_row")
                for h in range(MH):
                    ps = claim(pe, "qk", h)
                    q, k = mq_all[:, h * SEQ:(h + 1) * SEQ], mk_all[:, h * SEQ:(h + 1) * SEQ]
                    mm(ps[:, 0:SEQ], k[:, 0:P], q, start=True, stop=True)
                    done(mm(ps[:, SEQ:SEQ + P], k[:, P:SEQ], q[:, P:SEQ], start=True, stop=True), "qk")
                for b in range(NB):
                    for i in range(2):
                        pe.wait_ge(S("qk_taken"), 2 * i + 2)
                        ps = claim(pe, "hnum", 2 * b + i).rearrange("p (q n) -> p q n", q=2)
                        for q in range(2):
                            h = 2 * i + q
                            for s in range(b + 1):
                                c = b * P if s == 0 else SEQ
                                last = mm(ps[:, q, 0:MN + 1], scT[:, h, c:c + P], vaug[:, s, h, 0:MN + 1],
                                          start=(s == 0), stop=(s == b))
                        done(last, "hnum")

                pe.wait_ge(S("inv_d_taken"), nd)
                for c in range(NCH):
                    b, lo = c // 2, CH * (c % 2)
                    rows = slice(lo, lo + CH)
                    if c:
                        pe.wait_ge(S("state_ready"), c)
                    ps = claim(pe, "seq_x", c)
                    chunk_rows(c, ps, 0, [(2, v_tok[:, b, :])], "seq_x")
                    ps = claim(pe, "seq_u", c)
                    pe.wait_ge(S("seq_x_taken"), c + 1)
                    for h in range(RH):
                        last = mm(ps[rows, h * RN:(h + 1) * RN], DT[rows, UNIT[(b, h)], rows],
                                  seq_x[rows, h * RN:(h + 1) * RN], start=True, stop=True)
                    done(last, "seq_u")
                    ps = claim(pe, "seq_y", c)
                    pe.wait_ge(S("seq_u_taken"), c + 1)
                    chunk_rows(c, ps, 1, [(3, v_tok[:, b, :]), (1, seq_u)], "seq_y")
                    if c < NCH - 1:
                        ps = claim(pe, "seq_s", c).rearrange("p (t n) -> p t n", n=RN)
                        for h in range(RH):
                            t, hp = h // 2, 64 * (h % 2)
                            cols = slice(h * RN, (h + 1) * RN)
                            mm(ps[hp:hp + 64, t, :], kappa_tok[rows, b, cols], v_tok[rows, b, cols], start=True, stop=False)
                            last = mm(ps[hp:hp + 64, t, :], beta_tok[rows, b, cols], seq_u[rows, cols], start=False, stop=True)
                        done(last, "seq_s")
                for i, (src, sem) in enumerate(((y_tok, "y_normed"), (h_tok, "h_normed"))):
                    pe.wait_ge(S(sem), 1)
                    for b in range(NB):
                        ps = claim(pe, "y_turn", NB * i + b).rearrange("p (t n) -> p t n", t=RT)
                        for t in range(RT):
                            last = tp(ps[:, t, :], src[:, b * 512 + t * P:b * 512 + (t + 1) * P], ident[:])
                        done(last, "y_turn")
                mix_out(0, yT)

            def chunk_rows(c, ps, which, products, name):
                b, lo = c // 2, CH * (c % 2)
                rows = slice(lo, lo + CH)

                def on_state(h, start, stop):
                    hp = 64 * (h % 2)
                    return mm(ps[rows, h * RN:(h + 1) * RN], AR[hp:hp + 64, h // 2, b, which, rows],
                              state[hp:hp + 64, h // 2, :], start=start, stop=stop, skip_group_check=True)

                last_far = max(h for h in range(RH) if 64 * (h % 2) != lo)
                opened = False

                for h in range(RH):
                    near = c > 0 and 64 * (h % 2) == lo
                    if near:
                        on_state(h, not opened, False)
                        opened = True
                    for i, (f, rhs) in enumerate(products):
                        last = mm(ps[rows, h * RN:(h + 1) * RN], SC[rows, UNIT[(b, h)], f, rows],
                                  rhs[rows, h * RN:(h + 1) * RN], start=not opened,
                                  stop=(c == 0 and h == RH - 1 and i == len(products) - 1), skip_group_check=True)
                        opened = True
                if c:
                    last.then_inc(S("row_tile_done"), 1)
                    far_waits[0] += 1
                    pe.wait_ge(S("row_tile_done"), far_waits[0])
                    for h in range(RH):
                        if 64 * (h % 2) != lo:
                            last = on_state(h, False, h == last_far)
                done(last, name)

            far_waits = [0]

            def mix_out(l, y):
                pe.wait_ge(S("mixed"), l + 1)
                for i in range(4):
                    w = next_strip(pe)
                    ps = claim(pe, "mix_out", 4 * l + i)
                    for b in range(NB):
                        for k in range(KT):
                            last = mm(ps[:, b * STRIP:(b + 1) * STRIP], y[:, k, b * P:(b + 1) * P], w[:, k, :],
                                      start=(k == 0), stop=(k == KT - 1))
                    done(last, "mix_out")

            def peer(l):
                for b in range(NB):
                    pe.wait_ge(S("x_normed"), 4 * l + 1 + b)
                    turn_x(4 + 8 * l + 2 * b, b, 0)
                pe.wait_ge(S("keys_loaded"), 32 * (l + 1))
                for i in range(4):
                    ps = claim(pe, "key_turn", 4 * l + i).rearrange("p (q n) -> p q n", q=4)
                    for q in range(4):
                        last = tp(ps[:, q, :], keys[:, 4 * i + q, :], ident[:])
                    done(last, "key_turn")
                pe.wait_ge(S("x_turn_taken"), 8 + 8 * l)
                for i in range(8):
                    w = next_strip(pe)
                    ps = claim(pe, "peer_q", 8 * l + i)
                    for q in range(2):
                        last = project(ps[:, q * SEQ:(q + 1) * SEQ], w, P * q, P)
                    done(last, "peer_q")
                pe.wait_ge(S("key_turn_taken"), 4 * (l + 1))
                pe.wait_ge(S("peer_q_taken"), 8 * (l + 1))
                for b in range(NB):
                    for i in range(4):
                        ps = claim(pe, "peer_s", 8 * l + 4 * b + i).rearrange("p (q n) -> p q n", q=4)
                        for q in range(4):
                            j = 4 * i + q
                            last = mm(ps[:, q, :], qT[:, j, b * P:(b + 1) * P], keyT[:, (j % 2) * EH + j // 2, :],
                                      start=True, stop=True)
                        done(last, "peer_s")
                for b in range(NB):
                    n = 2 * l + b
                    ps = [claim(pe, "experts", 2 * n + c) for c in range(2)]
                    for c in range(2):
                        mm(ps[c], ident_a[:], xres[:, b, c * 512:(c + 1) * 512], start=True, stop=False)
                    with pe.Fori(0, SLOTS // UNROLL) as i:
                        for s in range(UNROLL):
                            j = s % RING
                            pe.wait_ge(S("diags_made"), i * UNROLL + (SLOTS * n + s + 1))
                            pe.wait_ge(S(f"v_row{j}"), i * (16 * UNROLL // RING) + 16 * (SLOTS // RING * n + s // RING + 1))
                            mm(ps[0], diag[:, s % DIAGS, :], ring_v[:, j, 0:512], start=False, stop=False)
                            mm(ps[1], diag[:, s % DIAGS, :], ring_v[:, j, 512:1024], start=False, stop=False
                               ).then_inc(S("v_rows_done"), 1)
                    for c in range(2):
                        done(mm(ps[c], ident_a[:], xres[:, b, c * 512:(c + 1) * 512], start=False, stop=True), "experts")

            def mixer1():
                for b in range(NB):
                    pe.wait_ge(S("x_normed"), 3 + b)
                    turn_x(8 + 2 * b, b, 0)
                pe.wait_ge(S("x_turn_taken"), 12)
                for name, n in (("fox_qk", 8), ("fox_v", 4), ("fox_og", 4)):
                    for i in range(n):
                        w = next_strip(pe)
                        ps = claim(pe, name, i)
                        if name == "fox_v":
                            for b in range(NB):
                                for k in range(KT):
                                    last = mm(ps[:, b * STRIP:(b + 1) * STRIP], xT[:, k, b * P:(b + 1) * P], w[:, k, :],
                                              start=(k == 0), stop=(k == KT - 1))
                        else:
                            for q in range(2):
                                last = project(ps[:, q * SEQ:(q + 1) * SEQ], w, P * q, P)
                        done(last, name)
                strip_at[0] += 1
                pe.wait_ge(S("f_weights"), 1)
                done(project(claim(pe, "fox_f", 0)[:, 0:SEQ], fw, 0, P), "fox_f")
                for i in range(8):
                    pe.wait_ge(S("squares"), i + 1)
                    done(mm(claim(pe, "fox_rms", i), pair_ones[:], SQ[:, 2 * i:2 * i + 2, :].rearrange("p t n -> p (t n)"),
                            start=True, stop=True), "fox_rms")
                pe.wait_ge(S("qk_normed"), 1)
                pe.wait_ge(S("decay_rows"), 1)
                for name, u in attention_plan():
                    if name == "att":
                        h, b = u % FH, u // FH
                        t, lo, w = h // 2, 64 * (h % 2), P * (b + 1)
                        ps = claim(pe, "att", u)[:, 0:w]
                        mm(ps, QK[lo:lo + 64, t, b * P:(b + 1) * P], QK[lo:lo + 64, 8 + t, 0:w], start=True, stop=False)
                        done(mm(ps, ident[lo:lo + 64, lo + h:lo + h + 1].to_broadcast([64, P]), frow[lo:lo + 64, 3, 0:w],
                                start=False, stop=True), "att")
                    elif name == "att_turn":
                        b = u // FH
                        pe.wait_ge(S("probs_ready"), u + 1)
                        ps = claim(pe, "att_turn", u)
                        for s in range(b + 1):
                            last = tp(ps[:, s * P:(s + 1) * P], prob[:, u % 4, s * P:(s + 1) * P], ident[:])
                        done(last, "att_turn")
                    else:
                        ps = claim(pe, "att_out", u)
                        for q in range(2):
                            n = 2 * u + q
                            h, b = n % FH, n // FH
                            lo = 64 * (h % 2)
                            pe.wait_ge(S("att_turn_taken"), n + 1)
                            for s in range(b + 1):
                                last = mm(ps[lo:lo + 64, 0:P], fv[:, s, h * FN:(h + 1) * FN], probT[:, n % 4, s, :],
                                          start=(s == 0), stop=(s == b))
                        done(last, "att_out")
                mix_out(1, oT)

            pe.sem_inc(S("v_rows_done"), RING)
            mixer0()
            if stop != "mix0":
                peer(0)
            if stop is None:
                mixer1()
                peer(1)

        @block.scalar
        def _(act):
            st = Steps(act, "scalar_step")
            af = nc.scalar.activation

            def taken(ins, name):
                ins.then_inc(S(name + "_taken"), 1)

            def copy(out_, in_):
                return nc.scalar.copy(out_, in_)

            ZERO, ONE, EPS_LN, EPS_RWKV, EPS_FOX = (cexp[:, i:i + 1] for i in range(5))

            def root(ready, n, ap, bias, scale, sem):
                act.wait_ge(S(ready), n)
                af(ap, ap, ACT.Sqrt, bias=bias, scale=scale).then_inc(S(sem), 1)

            def ln_root(i):
                for b in range(NB):
                    root("ln_var", 2 * i + b + 1, lnmv[:, b, 1:2], EPS_LN, 1.0, "ln_std")

            def take_x(first, b):
                for half in range(2):
                    ps = full(act, "x_turn", first + half)
                    taken(copy(xT[:, 4 * half:4 * half + 4, b * P:(b + 1) * P], ps.rearrange("p (k n) -> p k n", k=4)),
                          "x_turn")

            def mixer0():
                act.wait_ge(S("constants"), 1)
                for b in range(NB):
                    take_x(2 * b, b)
                act.wait_ge(S("params_taken"), 1)
                act.wait_ge(S("one_mu"), 1)
                for t in range(14):
                    ps = full(act, "rwkv_in", t)[:, 0:SEQ]
                    af(R[:, t * SEQ:(t + 1) * SEQ], ps, ACT.Identity, bias=ZERO, scale=one_mu[:, t:t + 1]
                       ).then_inc(S("rwkv_scaled"), 1)
                for t in range(8):
                    ps = full(act, "conv_in", t)[:, 0:SEQ]
                    dst = cut(4608 + t * SEQ, SEQ)
                    af(dst, ps, ACT.Identity, bias=par("conv_b", t), scale=par("conv_w", 24 + t)).then_inc(S("conv_scaled"), 1)
                for t in range(2):
                    taken(copy(mv_all[:, t * 512:(t + 1) * 512], full(act, "vo_in", t)), "vo_in")
                for t in range(2):
                    taken(af(mo_all[:, t * 512:(t + 1) * 512], full(act, "vo_in", 2 + t), ACT.Sigmoid), "vo_in")
                act.wait_ge(S("conv_in_taken"), 8)
                for t in range(2):
                    c = cut(4608 + t * 1024, 1024)
                    af(SC_flat(t), c, ACT.Sigmoid).then_inc(S("conv_sigmoid"), 1)
                act.wait_ge(S("small_loaded"), 64)
                ps = full(act, "gates_in", 0)
                af(mr[0:MH, 0, :], ps[0:MH, 0:SEQ], ACT.Identity, bias=small[0:MH, 0:1], scale=1.0)
                taken(af(mr[0:MH, 1, :], ps[0:MH, SEQ:2 * SEQ], ACT.Identity, bias=small[0:MH, 1:2], scale=1.0), "gates_in")
                act.wait_ge(S("rwkv_in_taken"), 14)
                af(xg, xg, ACT.Sigmoid)
                af(xwa[0:64, :], xwa[0:64, :], ACT.Tanh).then_inc(S("lora_squashed"), 2)
                for name, dst, bias in (("lora_w", logw, "w0"), ("lora_a", a_all, "a0")):
                    for half in range(2):
                        ps = full(act, name, half)
                        for q in range(2):
                            t = 2 * half + q
                            last = af(dst[:, t * SEQ:(t + 1) * SEQ], ps[:, q * SEQ:(q + 1) * SEQ], ACT.Sigmoid,
                                      bias=par(bias, t), scale=1.0)
                        taken(last, name)
                for half in range(2):
                    taken(copy(g_all[:, half * 512:(half + 1) * 512], full(act, "lora_g", half)), "lora_g")
                for half in range(2):
                    taken(af(tmp[:, half * 512:(half + 1) * 512], full(act, "kk_norm", half), ACT.Sqrt, bias=ZERO), "kk_norm")
                act.wait_ge(S("m_abs"), 1)
                st.then(af(mr[0:MH, 3, :], mr[0:MH, 3, :], ACT.Exp, scale=-1.0))
                st.settle()
                af(mr[0:MH, 3, :], mr[0:MH, 3, :], ACT.Ln, bias=ONE[0:MH]).then_inc(S("m_log"), 1)
                act.wait_ge(S("cum_ready"), 1)
                af(pfull, cumw, ACT.Exp)
                af(pinv, cumw, ACT.Exp, scale=-1.0)
                act.wait_ge(S("cum_ready"), 2)
                af(pprev, pprev, ACT.Exp).then_inc(S("decays"), 1)
                for i, dst in enumerate((v_tok, beta_tok, kappa_tok)):
                    for b in range(NB):
                        taken(copy(dst[:, b, :], full(act, "token_turn", NB * i + b)), "token_turn")
                act.wait_ge(S("m_neg"), 1)
                af(mr[0:MH, 5, :], mr[0:MH, 5, :], ACT.Exp).then_inc(S("m_rows"), 1)
                for i in range(len(LEVELS)):
                    for g in range(4):
                        taken(copy(Tm[:, 4 * g:4 * g + 4, :], full(act, "inv_t", 4 * i + g).rearrange("p (u n) -> p u n", u=4)),
                              "inv_t")
                for b in range(NB):
                    taken(copy(vaug[:, b, :, 0:MN], full(act, "mv_turn", b).rearrange("p (h n) -> p h n", h=MH)), "mv_turn")
                for h in range(MH):
                    act.wait_ge(S("mx_clamped"), h + 1)
                    af(scT[:, h, :], scT[:, h, :], ACT.Exp).then_inc(S("m_weights"), 1)
                root("head_var", 1, stat[:, 1, 0:NB * MH], EPS_LN, 1.0 / MN, "head_std")
                for c in range(NCH):
                    rows = slice(CH * (c % 2), CH * (c % 2) + CH)
                    taken(copy(seq_x[rows, :], full(act, "seq_x", c)[rows, :]), "seq_x")
                    taken(af(seq_u[rows, :], full(act, "seq_u", c)[rows, :], ACT.Copy, scale=-1.0), "seq_u")
                root("head_var", 2, stat[:, 1, 0:NB * RH], EPS_RWKV, 1.0 / RN, "head_std")
                for i, (g, bb) in enumerate((("ln_g", "ln_b"), ("hn_g", "hn_b"))):
                    for b in range(NB):
                        ps = full(act, "y_turn", NB * i + b)
                        for t in range(RT):
                            last = af(yT[:, 4 * i + t, b * P:(b + 1) * P], ps[:, t * P:(t + 1) * P], ACT.Identity,
                                      bias=par(bb, t), scale=par(g, t))
                        taken(last, "y_turn")
                ln_root(0)

            def SC_flat(t):
                return cut(24064 + 4096 + 1024 * t, 1024)

            def peer(l):
                for b in range(NB):
                    take_x(4 + 8 * l + 2 * b, b)
                for i in range(4):
                    taken(copy(keyT[:, 4 * i:4 * i + 4, :], full(act, "key_turn", 4 * l + i).rearrange("p (q n) -> p q n", q=4)),
                          "key_turn")
                for i in range(8):
                    taken(copy(qT[:, 2 * i:2 * i + 2, :], full(act, "peer_q", 8 * l + i).rearrange("p (q n) -> p q n", q=2)),
                          "peer_q")
                for b in range(NB):
                    for i in range(4):
                        ps = full(act, "peer_s", 8 * l + 4 * b + i).rearrange("p (q n) -> p q n", q=4)
                        taken(copy(sc[:, b, 4 * i:4 * i + 4, :], ps), "peer_s")
                def gate_exp(b):
                    act.wait_ge(S("gate_shifted"), 2 * l + b + 1)
                    g = gate[:, b, :]
                    af(g, g, ACT.Exp).then_inc(S("gate_exp"), 1)

                def gelu(b):
                    act.wait_ge(S("hidden"), 2 * l + b + 1)
                    af(ga[:, b, :], hid[:, b, :], ACT.Gelu).then_inc(S("gelued"), 1)

                def diags(b):
                    n = 2 * l + b
                    act.wait_ge(S("weights"), n + 1)
                    with act.Fori(0, SLOTS // UNROLL) as i:
                        for k in range(UNROLL // RING):
                            act.wait_ge(S("v_rows_done"), i * UNROLL + (SLOTS * n + RING * k + 1))
                            copy(gstage[:, k, :], ga[:, b, bass.ds(i * UNROLL + RING * k, RING)]).then_inc(S("weights_staged"), 1)
                            act.wait_ge(S("weights_staged"), i * (UNROLL // RING) + (SLOTS // RING * n + k + 1))
                            for j in range(RING):
                                s = RING * k + j
                                act.wait_ge(S("v_rows_done"), i * UNROLL + (SLOTS * n + s + 1 + RING - DIAGS))
                                af(diag[:, s % DIAGS, :], ident[:], ACT.Copy, scale=gstage[:, k, j:j + 1]
                                   ).then_inc(S("diags_made"), 1)

                gate_exp(0)
                gelu(0)
                gate_exp(1)
                diags(0)
                gelu(1)
                diags(1)
                ln_root(2 * l + 1)

            def mixer1():
                for b in range(NB):
                    take_x(8 + 2 * b, b)
                for i in range(8):
                    taken(copy(QK[:, 2 * i:2 * i + 2, :], full(act, "fox_qk", i).rearrange("p (q n) -> p q n", q=2)), "fox_qk")
                for i in range(4):
                    taken(copy(fv[:, :, i * STRIP:(i + 1) * STRIP], full(act, "fox_v", i).rearrange("p (b n) -> p b n", b=NB)),
                          "fox_v")
                for i in range(4):
                    taken(af(ogT[:, 2 * i:2 * i + 2, :], full(act, "fox_og", i).rearrange("p (q n) -> p q n", q=2), ACT.Sigmoid),
                          "fox_og")
                n = strips_before_f
                act.wait_ge(S(f"strip_loaded{n % WRING}"), 16 * (n // WRING + 1))
                act.wait_ge(S("f_zeroed"), 1)
                copy(fw[:, :, 0:FH], wring[:, n % WRING, :, 0:FH])
                copy(fw[:, :, 64:64 + FH], wring[:, n % WRING, :, 0:FH]).then_inc(S("f_weights"), 1)
                taken(af(frow[:, 0, :], full(act, "fox_f", 0)[:, 0:SEQ], ACT.Identity, bias=small[:, 2:3], scale=1.0),
                      "fox_f")
                act.wait_ge(S("f_abs"), 1)
                st.then(af(frow[:, 1, :], frow[:, 1, :], ACT.Exp, scale=-1.0))
                st.settle()
                af(frow[:, 1, :], frow[:, 1, :], ACT.Ln, bias=ONE).then_inc(S("f_log"), 1)
                for i in range(8):
                    taken(af(RS[:, 2 * i:2 * i + 2, :], full(act, "fox_rms", i).rearrange("p (t n) -> p t n", t=2), ACT.Sqrt,
                             bias=EPS_FOX), "fox_rms")
                units = FH * NB
                for s in range(units + 2):
                    if s < units:
                        u, w = s, P * (s // FH + 1)
                        act.wait_ge(S("logits_max"), u + 1)
                        if u >= 4:
                            await_filled(act, "att_turn", u - 4)
                        af(prob[:, u % 4, 0:w], lg[:, u % 4, 0:w], ACT.Exp, bias=amax[:, u:u + 1], scale=1.0,
                           accum_out=asum[:, u:u + 1]).then_inc(S("exped"), 1)
                    if s >= 2:
                        u, w = s - 2, P * ((s - 2) // FH + 1)
                        ps = full(act, "att_turn", u)
                        if u >= 4:
                            await_filled(act, "att_out", (u - 4) // 2)
                        taken(copy(probT[:, u % 4, 0:w // P, :], ps[:, 0:w].rearrange("p (s n) -> p s n", n=P)), "att_turn")
                ln_root(2)

            mixer0()
            if stop != "mix0":
                peer(0)
            if stop is None:
                mixer1()
                peer(1)

        @block.vector
        def _(dve):
            v = nc.vector
            st = Steps(dve, "vector_step")
            tt, ts, stt = v.tensor_tensor, v.tensor_scalar, v.scalar_tensor_tensor

            def go(ins):
                st.then(ins)
                st.settle()

            def taken(ins, name):
                ins.then_inc(S(name + "_taken"), 1)

            def layer_norm(i, b, parts):
                dve.wait_ge(S("ln_loaded"), 32 * (i + 1))
                for c, part in enumerate(parts):
                    st.then(v.bn_stats(lnst[:, b, 6 * c:6 * c + 6], part))
                st.settle()
                v.bn_aggr(lnmv[:, b, :], lnst[:, b, :]).then_inc(S("ln_var"), 1)
                dve.wait_ge(S("ln_std"), 2 * i + b + 1)
                go(v.reciprocal(lnrs[:, b:b + 1], lnmv[:, b, 1:2]))
                for c, part in enumerate(parts):
                    ins = ts(xres[:, b, c * 512:(c + 1) * 512], part, lnmv[:, b, 0:1], lnrs[:, b:b + 1],
                             ALU.subtract, ALU.mult)
                    if i % 2:
                        taken(ins, "experts")
                    else:
                        st.then(ins)
                if i % 2:
                    dve.wait_ge(S("experts_taken"), 2 * (2 * (i // 2) + b + 1))
                st.settle()
                go(tt(xres[:, b, :], xres[:, b, :], ln_par[:, 0, :], ALU.mult))
                tt(xres[:, b, :], xres[:, b, :], ln_par[:, 1, :], ALU.add).then_inc(S("x_normed"), 1)
                dve.wait_ge(S("x_normed"), 2 * i + b + 1)

            def head_norm(x, scratch, groups, n, norms, sem):
                g = x.rearrange("p (g n) -> p g n", n=n)
                q = scratch.rearrange("p (g n) -> p g n", n=n)
                mean, ss = stat[:, 0, 0:groups], stat[:, 1, 0:groups]
                wide = lambda s: s.rearrange("p (g o) -> p g o", o=1).to_broadcast([P, groups, n])
                go(v.tensor_reduce(mean, g, AX_X, ALU.add))
                go(ts(mean, mean, 1.0 / n, None, ALU.mult))
                go(tt(g, g, wide(mean), ALU.subtract))
                go(tt(q, g, g, ALU.mult))
                v.tensor_reduce(ss, q, AX_X, ALU.add).then_inc(S("head_var"), 1)
                dve.wait_ge(S("head_std"), norms)
                go(v.reciprocal(ss, ss))
                tt(g, g, wide(ss), ALU.mult).then_inc(S(sem), 1)

            def log_sigmoid(z, t, o, ready, logged):
                stt(t, z, -1.0, z, ALU.mult, ALU.max).then_inc(S(ready), 1)
                dve.wait_ge(S(logged), 1)
                go(stt(o, z, 0.0, t, ALU.min, ALU.subtract))

            def mixer0():
                dve.wait_ge(S("constants"), 1)
                taken(v.tensor_copy(pars[:, 0:NROWS], full(dve, "params", 0)[:, 0:NROWS]), "params")
                dve.wait_ge(S("params_taken"), 1)
                st.then(ts(kn8[:], pars[:, ROWS["kn_g"][0]:ROWS["kn_g"][0] + 8], float(FN) ** 0.5, None, ALU.mult))
                ts(one_mu[:], pars[:, 0:14], -1.0, 1.0, ALU.mult, ALU.add).then_inc(S("one_mu"), 1)
                for t in range(14):
                    dve.wait_ge(S("rwkv_scaled"), t + 1)
                    ps = full(dve, "rwkv_in", t)
                    dst = R[:, t * SEQ + 1:(t + 1) * SEQ]
                    taken(stt(dst, ps[:, 0:SEQ - 1], par("mu", t), dst, ALU.mult, ALU.add), "rwkv_in")
                for t in range(8):
                    dve.wait_ge(S("conv_scaled"), t + 1)
                    ps = full(dve, "conv_in", t)
                    for back in (1, 2, 3):
                        dst = cut(4608 + t * SEQ, SEQ)[:, back:SEQ]
                        ins = stt(dst, ps[:, 0:SEQ - back], par("conv_w", 8 * (3 - back) + t), dst, ALU.mult, ALU.add)
                        if back < 3:
                            go(ins)
                        else:
                            taken(ins, "conv_in")
                dve.wait_ge(S("rwkv_in_taken"), 14)
                for t in range(RT):
                    st.then(ts(kk_all[:, t * SEQ:(t + 1) * SEQ], k_all[:, t * SEQ:(t + 1) * SEQ], par("k_k", t), None, ALU.mult))
                st.settle()
                tt(tmp, kk_all, kk_all, ALU.mult).then_inc(S("head_products"), 1)
                dve.wait_ge(S("conv_sigmoid"), 1)
                stt(mq_all, mq_all, float(MN) ** -0.5, cut(28160, 1024), ALU.mult, ALU.mult).then_inc(S("silu"), 1)
                dve.wait_ge(S("conv_sigmoid"), 2)
                tt(mk_all, mk_all, cut(29184, 1024), ALU.mult).then_inc(S("silu"), 1)
                dve.wait_ge(S("silu"), 2)
                dve.wait_ge(S("gates_in_taken"), 1)
                rows = [mr[0:MH, i, :] for i in range(6)]
                log_sigmoid(rows[1], rows[3], rows[1], "m_abs", "m_log")
                go(v.tensor_tensor_scan(rows[3], ones[0:MH, :], rows[1], 0.0, ALU.mult, ALU.add))
                go(tt(rows[2], rows[0], rows[3], ALU.subtract))
                go(v.tensor_tensor_scan(rows[4], rows[2], rows[2], 0.0, ALU.max, ALU.max))
                go(tt(rows[5], rows[3], rows[4], ALU.add))
                go(ts(rows[5], rows[5], -1.0, None, ALU.mult))
                ts(rows[4], rows[4], -1.0, None, ALU.mult).then_inc(S("m_neg"), 1)
                dve.wait_ge(S("lora_w_taken"), 2)
                go(ts(logw, logw, -float(2.718281828459045 ** -0.5), None, ALU.mult))
                for i in range(RT * NCH):
                    ins = v.tensor_tensor_scan(cumw[:, i * CH:(i + 1) * CH], ones[:, 0:CH], logw[:, i * CH:(i + 1) * CH], 0.0,
                                               ALU.mult, ALU.add)
                    if i < RT * NCH - 1:
                        st.then(ins)
                ins.then_inc(S("cum_ready"), 1)
                dve.wait_ge(S("cum_ready"), 1)
                tt(pprev, cumw, logw, ALU.subtract).then_inc(S("cum_ready"), 1)
                dve.wait_ge(S("kk_norm_taken"), 2)
                go(ts(tmp, tmp, 1e-12, None, ALU.max))
                go(v.reciprocal(tmp, tmp))
                go(tt(kk_all, kk_all, tmp, ALU.mult))
                dve.wait_ge(S("lora_a_taken"), 2)
                for t in range(RT):
                    c = slice(t * SEQ, (t + 1) * SEQ)
                    st.then(ts(tmp[:, c], a_all[:, c], 1.0, par("k_a", t), ALU.subtract, ALU.mult))
                st.settle()
                go(stt(k_all, tmp, 1.0, k_all, ALU.add, ALU.mult))
                for t in range(RT):
                    c = slice(t * SEQ, (t + 1) * SEQ)
                    ins = stt(tmp[:, c], r_all[:, c], par("r_k", t), k_all[:, c], ALU.mult, ALU.mult)
                ins.then_inc(S("head_products"), 1)
                dve.wait_ge(S("decays"), 1)
                view = lambda x: x.rearrange("p (t b n) -> p t b n", t=RT, b=NB)
                st.then(v.tensor_copy(pend[:], pfull.rearrange("p (t c n) -> p t c n", t=RT, c=NCH)[:, :, :, CH - 1]))
                st.then(tt(AR[:, :, :, 0, :], view(kk_all), view(pprev), ALU.mult))
                st.then(tt(AR[:, :, :, 1, :], view(r_all), view(pfull), ALU.mult))
                go(tt(beta_all, kk_all, a_all, ALU.mult))
                st.then(tt(beta_all, beta_all, pinv, ALU.mult))
                tt(kappa_all, k_all, pinv, ALU.mult).then_inc(S("scan_operands"), 1)
                for half in range(2):
                    c = slice(half * 512, (half + 1) * 512)
                    taken(tt(bonus_all[:, c], full(dve, "bonus", half), v_all[:, c], ALU.mult), "bonus")
                for u in range(16):
                    ps = full(dve, "scores", u).rearrange("p (f n) -> p f n", f=2)
                    taken(tt(SC[:, u, :, :].rearrange("p (f g) n -> p f (g n)", f=2), ps,
                             score_mask[:].rearrange("p g n -> p (g n)").unsqueeze(1).to_broadcast([P, 2, 2 * P]), ALU.mult),
                          "scores")
                dve.wait_ge(S("scores_taken"), 16)
                wide = lambda m: m.unsqueeze(1).to_broadcast([P, 4, P])
                for g in range(4):
                    us = slice(4 * g, 4 * g + 4)
                    ps = full(dve, "ab", g).rearrange("p (u n) -> p u n", u=4)
                    taken(stt(Dm[:, us, :], ps, -1.0, wide(level_one[:]), ALU.mult, ALU.mult), "ab")
                    st.then(stt(DT[:, us, :], SC[:, us, 0, :], -1.0, wide(level_mask[:, 0, :]), ALU.mult, ALU.mult))
                dve.wait_ge(S("ab_taken"), 4)
                st.settle()
                nd = 0
                for g in range(4):
                    us = slice(4 * g, 4 * g + 4)
                    st.then(tt(Dm[:, us, :], Dm[:, us, :], wide(ident[:]), ALU.add))
                    st.then(tt(DT[:, us, :], DT[:, us, :], wide(ident[:]), ALU.add))
                for i, m in enumerate(LEVELS):
                    for g in range(4):
                        us = slice(4 * g, 4 * g + 4)
                        if i:
                            await_filled(dve, "inv_t", 4 * (i - 1) + g)
                        tt(LM[:, us, :], SC[:, us, 0, :], wide(level_mask[:, i + 1, :]), ALU.mult).then_inc(S("merge_ready"), 1)
                    for g in range(4):
                        us = slice(4 * g, 4 * g + 4)
                        for which in ((DT,) if m == LEVELS[-1] else (Dm, DT)):
                            if which is Dm:
                                await_filled(dve, "inv_d", nd + 1)
                            ps = full(dve, "inv_d", nd).rearrange("p (u n) -> p u n", u=4)
                            if i == 0:
                                st.settle()
                            taken(tt(which[:, us, :], which[:, us, :], ps, ALU.subtract), "inv_d")
                            nd += 1
                    dve.wait_ge(S("inv_d_taken"), nd)
                taken(v.tensor_copy(gcol[:], full(dve, "mrow_turn", 0)[:, 0:16]), "mrow_turn")
                dve.wait_ge(S("mrow_turn_taken"), 1)
                for i in range(2):
                    ps = full(dve, "mx_row", i)
                    for q in range(2):
                        h = 2 * i + q
                        st.then(ts(scT[:, h, 0:SEQ], ps[:, q * SEQ:(q + 1) * SEQ], gcol[:, h:h + 1], 0.0, ALU.add, ALU.min))
                        ins = ts(scT[:, h, SEQ:SEQ + P], ps[:, q * SEQ + P:(q + 1) * SEQ], gcol[:, MH + h:MH + h + 1], 0.0,
                                 ALU.add, ALU.min)
                        if q == 0:
                            st.then(ins)
                    taken(ins, "mx_row")
                    dve.wait_ge(S("mx_row_taken"), i + 1)
                    dve.sem_inc(S("mx_clamped"), 2)
                for h in range(MH):
                    dve.wait_ge(S("m_weights"), h + 1)
                    go(tt(scT[:, h, :], scT[:, h, :], causal_st[:], ALU.mult))
                    taken(tt(scT[:, h, :], full(dve, "qk", h)[:, 0:384], scT[:, h, :], ALU.mult), "qk")
                for n in range(4):
                    b, i = n // 2, n % 2
                    ps = full(dve, "hnum", n).rearrange("p (q n) -> p q n", q=2)
                    d = dcol[:, 2 * n:2 * n + 2]
                    go(v.tensor_copy(d, ps[:, :, MN]))
                    go(stt(d, d, -1.0, d, ALU.mult, ALU.max))
                    go(tt(d, d, gcol[:, 2 * MH + MH * b + 2 * i:2 * MH + MH * b + 2 * i + 2], ALU.max))
                    go(v.reciprocal(d, d))
                    for q in range(2):
                        c = b * 512 + (2 * i + q) * MN
                        ins = ts(h_tok[:, c:c + MN], ps[:, q, 0:MN], d[:, q:q + 1], None, ALU.mult)
                        if q == 0:
                            st.then(ins)
                    taken(ins, "hnum")
                dve.wait_ge(S("hnum_taken"), 4)
                head_norm(h_tok, mk_all, NB * MH, MN, 1, "h_normed")
                for c in range(NCH):
                    b, rows = c // 2, slice(CH * (c % 2), CH * (c % 2) + CH)
                    if c < NCH - 1:
                        ps = full(dve, "seq_s", c).rearrange("p (t n) -> p t n", n=RN)
                        if c == 0:
                            taken(v.tensor_copy(state, ps[:, 0:RT, :]), "seq_s")
                        else:
                            taken(tt(state, state, ps[:, 0:RT, :], ALU.add), "seq_s")
                        dve.wait_ge(S("seq_s_taken"), c + 1)
                        tt(state, state, pend[:, :, c:c + 1].to_broadcast([P, RT, RN]), ALU.mult).then_inc(S("state_ready"), 1)
                        dve.wait_ge(S("state_ready"), c + 1)
                    taken(v.tensor_copy(y_tok[rows, b * 512:(b + 1) * 512], full(dve, "seq_y", c)[rows, :]), "seq_y")
                dve.wait_ge(S("seq_y_taken"), NCH)
                head_norm(y_tok, kk2, NB * RH, RN, 2, "y_normed")
                yr = cut(8704, 1024)
                dve.wait_ge(S("y_turn_taken"), 2)
                go(tt(yr, yr, bonus_all, ALU.add))
                go(tt(yr, yr, g_all, ALU.mult))
                dve.wait_ge(S("y_turn_taken"), 4)
                ym = cut(9728, 1024)
                tt(ym, ym, mo_all, ALU.mult).then_inc(S("mixed"), 1)
                residual(0)

            kk2 = cut(24064, 1024)

            def residual(l):
                for i in range(4):
                    ps = full(dve, "mix_out", 4 * l + i).rearrange("p (b n) -> p b n", b=NB)
                    x = xres[:, :, i * STRIP:(i + 1) * STRIP]
                    taken(stt(x, x, ALPHA, ps, ALU.mult, ALU.add), "mix_out")
                dve.wait_ge(S("mix_out_taken"), 4 * (l + 1))
                for b in range(NB):
                    layer_norm(2 * l, b, [xres[:, b, c * 512:(c + 1) * 512] for c in range(2)])

            def top16(src, scratch, vals, idx, n):
                for i in range(n):
                    st.then(v.max(vals[:, i, 0:8], src[:, i, :]))
                st.settle()
                for i in range(n):
                    st.then(v.max_index(idx[:, i, 0:8], vals[:, i, 0:8], src[:, i, :]))
                    st.then(v.match_replace(scratch[:, i, :], vals[:, i, 0:8], src[:, i, :], -BIG))
                st.settle()
                for i in range(n):
                    st.then(v.max(vals[:, i, 8:16], scratch[:, i, :]))
                st.settle()
                for i in range(n):
                    st.then(v.max_index(idx[:, i, 8:16], vals[:, i, 8:16], scratch[:, i, :]))
                st.settle()

            def route(l, b):
                dve.wait_ge(S("peer_s_taken"), 8 * (l + 1) if b else 8 * l + 4)
                top16(sc[:, b, :, :], scr.rearrange("p (i n) -> p i n", i=16), v16, i16, 16)
                vv = v16.rearrange("p (h two) k -> p h two k", two=2)
                cv = cand.rearrange("p h (i j) -> p h i j", i=TOPK)
                go(v.tensor_copy(i16f, i16.rearrange("p (h two) k -> p h two k", two=2)))
                for h in range(EH):
                    st.then(tt(cv[:, h], vv[:, h, 0, :].unsqueeze(2).to_broadcast([P, TOPK, TOPK]),
                               vv[:, h, 1, :].unsqueeze(1).to_broadcast([P, TOPK, TOPK]), ALU.add))
                st.settle()
                top16(cand, scr.rearrange("p (h n) -> p h n", h=EH), csc, pos, EH)
                pf = pos.rearrange("p h k -> p (h k)")
                st.then(ts(hilo_u[:, 0, :], pf, 4, None, ALU.logical_shift_right))
                go(ts(hilo_u[:, 1, :], pf, 15, None, ALU.bitwise_and))
                go(v.tensor_copy(hilo.rearrange("p w h k -> p w (h k)"), hilo_u))
                for w in range(2):
                    for h in range(EH):
                        st.then(tt(onehot[:, h], hilo[:, w, h, :].unsqueeze(2).to_broadcast([P, TOPK, TOPK]),
                                   iota16[:].unsqueeze(1).to_broadcast([P, TOPK, TOPK]), ALU.is_equal))
                    st.settle()
                    for h in range(EH):
                        st.then(tt(onehot[:, h], onehot[:, h], i16f[:, h, w, :].unsqueeze(1).to_broadcast([P, TOPK, TOPK]),
                                   ALU.mult))
                    st.settle()
                    go(v.tensor_reduce(e12[:, w].rearrange("p h k -> p (h k)"), onehot.rearrange("p h k j -> p (h k) j"),
                                       AX_X, ALU.add))
                ef = e12.rearrange("p w h k -> p w (h k)")
                go(stt(eidf, ef[:, 0, :], float(NK), ef[:, 1, :], ALU.mult, ALU.add))
                v.tensor_copy(eid[:, b, :], eidf).then_inc(S("experts_chosen"), 1)
                g = gate[:, b, :].rearrange("p (h k) -> p h k", h=EH)
                tt(g, csc, csc[:, :, 0:1].to_broadcast([P, EH, TOPK]), ALU.subtract).then_inc(S("gate_shifted"), 1)
                dve.wait_ge(S("gate_exp"), 2 * l + b + 1)
                go(v.tensor_reduce(gsum[:, 0:EH], g, AX_X, ALU.add))
                go(v.reciprocal(gsum[:, EH:2 * EH], gsum[:, 0:EH]))
                go(tt(g, g, gsum[:, EH:2 * EH].unsqueeze(2).to_broadcast([P, EH, TOPK]), ALU.mult))

            def dots(l, b):
                n = 2 * l + b
                with dve.Fori(0, SLOTS // UNROLL) as i:
                    for k in range(UNROLL // RING):
                        if True:
                            dve.wait_ge(S("dots_kept"), i * (UNROLL // RING) + (SLOTS // RING * n + k + 1))
                        for j in range(RING):
                            dve.wait_ge(S(f"u_row{j}"), i * (16 * UNROLL // RING) + 16 * (SLOTS // RING * n + k + 1))
                            v.tensor_tensor_reduce(out=ring_u[:, j, :], in0=ring_u[:, j, :], in1=xres[:, b, :], scale=1.0,
                                                   scalar=0.0, op0=ALU.mult, op1=ALU.add, accum_out=hstage[:, k, j:j + 1]
                                                   ).then_inc(S("u_rows_done"), 1)
                        dve.wait_ge(S("u_rows_done"), i * UNROLL + (SLOTS * n + RING * (k + 1) + RING))
                        v.tensor_copy(hid[:, b, bass.ds(i * UNROLL + RING * k, RING)], hstage[:, k, :]
                                      ).then_inc(S("dots_kept"), 1)
                dve.wait_ge(S("dots_kept"), SLOTS // RING * (n + 1) + 2)
                dve.sem_inc(S("hidden"), 1)

            def weigh(l, b):
                dve.wait_ge(S("gelued"), 2 * l + b + 1)
                tt(ga[:, b, :], ga[:, b, :], gate[:, b, :], ALU.mult).then_inc(S("weights"), 1)

            def peer(l):
                route(l, 0)
                dots(l, 0)
                weigh(l, 0)
                route(l, 1)
                dots(l, 1)
                weigh(l, 1)
                for b in range(NB):
                    layer_norm(2 * l + 1, b, [full(dve, "experts", 4 * l + 2 * b + c) for c in range(2)])

            def mixer1():
                v.memset(fw, 0.0).then_inc(S("f_zeroed"), 1)
                for i in range(8):
                    dve.wait_ge(S("fox_qk_taken"), i + 1)
                    c = slice(2 * i, 2 * i + 2)
                    tt(SQ[:, c, :], QK[:, c, :], QK[:, c, :], ALU.mult).then_inc(S("squares"), 1)
                dve.wait_ge(S("fox_f_taken"), 1)
                z, t, c, neg = (frow[:, i, :] for i in range(4))
                log_sigmoid(z, t, z, "f_abs", "f_log")
                go(v.tensor_tensor_scan(c, ones[:], z, 0.0, ALU.mult, ALU.add))
                ts(neg, c, -1.0, None, ALU.mult).then_inc(S("decay_rows"), 1)
                for i in range(8):
                    dve.wait_ge(S("fox_rms_taken"), i + 1)
                    c = slice(2 * i, 2 * i + 2)
                    st.then(v.reciprocal(RS[:, c, :], RS[:, c, :]))
                st.settle()
                for t in range(16):
                    gain = par("qn_g", t) if t < 8 else kn8[:, t - 8:t - 7]
                    ins = stt(QK[:, t, :], QK[:, t, :], gain, RS[:, t, :], ALU.mult, ALU.mult)
                    if t < 15:
                        st.then(ins)
                ins.then_inc(S("qk_normed"), 1)
                units = FH * NB
                for s in range(units + 4):
                    if s < units:
                        u, b = s, s // FH
                        w = P * (b + 1)
                        ps = full(dve, "att", u)[:, 0:w]
                        if u >= 4:
                            dve.wait_ge(S("exped"), u - 3)
                        taken(v.tensor_tensor_reduce(out=lg[:, u % 4, 0:w], in0=ps, in1=causal_ts[:, SEQ + P - w:SEQ + P],
                                                     scale=1.0, scalar=-BIG, op0=ALU.add, op1=ALU.max,
                                                     accum_out=arec[:, u:u + 1]), "att")
                        dve.wait_ge(S("att_taken"), u + 1)
                        ts(amax[:, u:u + 1], arec[:, u:u + 1], -1.0, None, ALU.mult).then_inc(S("logits_max"), 1)
                    if 1 <= s < units + 1:
                        u = s - 1
                        w = P * (u // FH + 1)
                        dve.wait_ge(S("exped"), u + 1)
                        dve.wait_ge(S("logits_max"), u + 1)
                        go(v.reciprocal(arec[:, u:u + 1], asum[:, u:u + 1]))
                        ts(prob[:, u % 4, 0:w], prob[:, u % 4, 0:w], arec[:, u:u + 1], None, ALU.mult).then_inc(S("probs_ready"), 1)
                    if s >= 4 and s % 2 == 0:
                        i = (s - 4) // 2
                        t, b = i % 8, i // 8
                        c = slice(b * P, (b + 1) * P)
                        taken(tt(oT[:, t, c], full(dve, "att_out", i)[:, 0:P], ogT[:, t, c], ALU.mult), "att_out")
                for i in range((units + 4 - 4) // 2 + (1 if (units + 4) % 2 else 0), 16):
                    t, b = i % 8, i // 8
                    c = slice(b * P, (b + 1) * P)
                    taken(tt(oT[:, t, c], full(dve, "att_out", i)[:, 0:P], ogT[:, t, c], ALU.mult), "att_out")
                dve.wait_ge(S("att_out_taken"), 16)
                dve.sem_inc(S("mixed"), 1)
                residual(1)

            dve.sem_inc(S("u_rows_done"), RING)
            dve.sem_inc(S("dots_kept"), 2)
            mixer0()
            if stop != "mix0":
                peer(0)
            if stop is None:
                mixer1()
                peer(1)


_SHAPES = None


def kernel(**inputs):
    import numpy as _np
    import concourse.bacc as _bacc
    from concourse.bass_utils import run_bass_kernel_spmd as _run

    nc = _bacc.Bacc("TRN2", target_bir_lowering=False, num_devices=1)
    arrays, T = {}, {}
    for name, value in inputs.items():
        a = _np.ascontiguousarray(value)
        arrays[name] = a
        T[name] = nc.dram_tensor(name, a.shape, mybir.dt.from_np(a.dtype), kind="ExternalInput").ap()
    out = nc.dram_tensor("out", (1, SEQ, D), F32, kind="ExternalOutput").ap()
    build(nc, T, out)
    r = _run(nc, [arrays], core_ids=[0])
    return r.results[0]["out"]
```

```python
from contextlib import ExitStack

import concourse.bass as bass
from concourse import mybir

F32 = mybir.dt.float32
U32 = mybir.dt.uint32
ALU = mybir.AluOpType
ACT = mybir.ActivationFunctionType
AX_X = mybir.AxisListType.X

P = 128
D = 1024
SEQ = 256
NB = SEQ // P
KT = D // P
ALPHA = 4.0 ** 0.25
LN_EPS = 1e-5

RW = 512
RH, RN = 8, 64
RT = RW // P
CH = 64
NCH = SEQ // CH
RWKV_COLS = 3 * RW + 64 + 64 + 128
MW = 512
MH, MN = 4, 128
LEVELS = [2, 4, 8, 16, 32]

FH, FN = 16, 64

EH = 8
NK = 128
TOPK = 16
SLOTS = EH * TOPK
RING = 8
UNROLL = 16
DIAGS = 4
PE_ROWS = 80
DVE_ROWS = SLOTS - PE_ROWS

STRIP = 256
WRING = 3
BIG = 3.0e38


def unit_heads():
    return [(b, 2 * q + odd) for b in range(NB) for odd in range(2) for q in range(RH // 2)]


UNITS = unit_heads()
UNIT = {bh: u for u, bh in enumerate(UNITS)}


def parameter_rows():
    rows, at = {}, 0
    for name, n in (("mu", RWKV_COLS // P), ("w0", RT), ("a0", RT), ("k_k", RT), ("k_a", RT), ("r_k", RT),
                    ("ln_g", RT), ("ln_b", RT), ("conv_w", 4 * 8), ("conv_b", 8), ("hn_g", MH), ("hn_b", MH),
                    ("qn_g", 8), ("kn_g", 8)):
        rows[name] = (at, n)
        at += n
    return rows, at


def attention_plan(b):
    order = []
    for s in range(FH + 3):
        if s < FH:
            order.append(("att", FH * b + s))
        if 2 <= s < FH + 2:
            order.append(("att_turn", FH * b + s - 2))
        if s >= 3 and (s - 3) % 2:
            order.append(("att_out", (FH * b + s - 3) // 2))
    return order


NORMS = [(0, 0), (0, 1), (1, 0), (2, 0), (1, 1), (2, 1), (3, 0), (3, 1)]
NORM_LOADS = [sum(NORMS[i][0] != NORMS[i - 1][0] for i in range(1, e + 1)) + 1 for e in range(len(NORMS))]


def bank_plan():
    plan = [("x_turn", 4), ("params", 1), ("rwkv_in", 14), ("lora_w", 2), ("lora_a", 2), ("lora_g", 2), ("kk_norm", 2),
            ("conv_in", 8), ("bonus", 2), ("token_turn", 6), ("scores", 16), ("ab", 4), ("vo_in", 4), ("gates_in", 1)]
    for m in LEVELS:
        plan.append(("inv_t", 4))
        plan.append(("inv_d", 4 if m == LEVELS[-1] else 8))
    plan += [("mrow_turn", 1), ("mv_turn", 2), ("mx_row", 2), ("qk", 4)]
    for c in range(NCH):
        plan += [("seq_x", 1), ("seq_u", 1)] + ([("seq_s", 1)] if c < NCH - 1 else []) + [("seq_y", 1)]
        if c < NB:
            plan.append(("hnum", 2))
    plan += [("y_turn", 4), ("mix_out", 4)]
    plan += [("x_turn", 4), ("key_turn", 4), ("peer_q", 8), ("peer_s", 8), ("experts", 2)]
    for b in range(NB):
        if b == 0:
            plan.append(("key_turn", 4))
        plan += [("x_turn", 2), ("fox_qk", 4), ("fox_v", 2), ("fox_og", 2), ("fox_f", 1), ("fox_rms", 4)]
        plan += [(name, 1) for name, _ in attention_plan(b)]
        plan += [("mix_out", 2), ("x_turn", 2), ("peer_q", 4), ("peer_s", 4), ("experts", 2)]
    plan += [("experts", 2)]
    return plan


def build(nc, T, out):
    ROWS, NROWS = parameter_rows()
    ctx = ExitStack()
    with ctx:
        def sb(name, shape, dt=F32):
            return ctx.enter_context(nc.sbuf_tensor(name, shape, dt))

        sems = {}

        def S(name):
            if name not in sems:
                sems[name] = ctx.enter_context(nc.semaphore(name))
            return sems[name]

        psum = ctx.enter_context(nc.psum_tensor("psum", [P, 8, 512], F32))
        order, ticket, seen, fills = [], {}, {}, {}
        for name, n in bank_plan():
            for _ in range(n):
                k = seen.get(name, 0)
                seen[name] = k + 1
                ticket[(name, k)] = len(order)
                fills[(name, k)] = max(fills.values(), default=0) + (name != "experts")
                order.append((name, k))

        def bank(name, k):
            return psum[:, ticket[(name, k)] % 8, :]

        def claim(pe, name, k):
            n = ticket[(name, k)]
            if n >= 8:
                before, i = order[n - 8]
                pe.wait_ge(S(before + "_taken"), i + 1)
            return bank(name, k)

        def await_filled(eng, name, k):
            eng.wait_ge(S("banks_filled"), fills[(name, k)])

        def full(eng, name, k):
            await_filled(eng, name, k)
            return bank(name, k)

        ident = sb("ident", [P, P])
        pair_ones = sb("pair_ones", [P, P])
        ones = sb("ones", [P, SEQ])
        score_mask = sb("score_mask", [P, 2, P])
        level_mask = sb("level_mask", [P, 6, P])
        level_one = sb("level_one", [P, P])
        causal_st = sb("causal_st", [P, 3 * P])
        causal_ts = sb("causal_ts", [P, SEQ + P])
        iota16 = sb("iota16", [P, TOPK])
        pars = sb("pars", [P, P])
        one_mu = sb("one_mu", [P, RWKV_COLS // P])
        kn8 = sb("kn8", [P, 8])
        small = sb("small", [P, 4])
        cexp = sb("cexp", [P, 6])

        def par(name, i=0):
            at, n = ROWS[name]
            return pars[:, at + i:at + i + 1]

        xres = sb("xres", [P, NB, D])
        xT = sb("xT", [P, KT, SEQ])
        ln_par = sb("ln_par", [P, 2, D])
        lnst = sb("lnst", [P, NB, 12])
        lnmv = sb("lnmv", [P, NB, 2])
        lnrs = sb("lnrs", [P, NB])
        wring = sb("wring", [P, WRING, KT, STRIP])
        ARENA = 36352
        A = sb("arena", [P, ARENA])

        def cut(at, n):
            assert at + n <= ARENA, (at, n)
            return A[:, at:at + n]

        strips = []

        def add_strips(w, c0, c1, name, first, per):
            for i, c in enumerate(range(c0, c1, STRIP)):
                strips.append((T[w][:, c:min(c + STRIP, c1)].rearrange("(k p) n -> p k n", p=P),
                               min(STRIP, c1 - c), name, first + (int(i * per) if per < 1 else (i + 1) * per - 1)))

        M0 = RWKV_COLS
        add_strips("l0_w_in", 0, M0, "rwkv_in", 0, 2)
        add_strips("l0_w_in", M0, M0 + 2 * MW, "conv_in", 0, 2)
        add_strips("l0_w_in", M0 + 2 * MW, M0 + 4 * MW, "vo_in", 0, 1)
        add_strips("l0_w_in", M0 + 4 * MW, M0 + 4 * MW + 2 * MH, "gates_in", 0, 1)
        add_strips("l0_w_out", 0, D, "mix_out", 0, 1)
        add_strips("l0_peer_wq", 0, 2048, "peer_q", 0, 1)
        strips_before_f = []
        for b in range(NB):
            add_strips("l1_w_in", 0, 2 * D, "fox_qk", 4 * b, 0.5)
            add_strips("l1_w_in", 2 * D, 3 * D, "fox_v", 2 * b, 0.5)
            add_strips("l1_w_in", 3 * D, 4 * D, "fox_og", 2 * b, 0.5)
            strips_before_f.append(len(strips))
            add_strips("l1_w_in", 4 * D, 4 * D + FH, "fox_f", b, 1)
            add_strips("l1_w_out", 0, D, "mix_out", 4 + 2 * b, 0.5)
            add_strips("l1_peer_wq", 0, 2048, "peer_q", 8 + 4 * b, 0.5)

        strip_at = [0]

        def next_strip(pe):
            n = strip_at[0]
            strip_at[0] += 1
            pe.wait_ge(S(f"strip_loaded{n % WRING}"), 16 * (n // WRING + 1))
            return wring[:, n % WRING]

        prows = cut(24064, P)
        R = cut(0, 14 * SEQ)
        r_all, k_all, v_all = cut(0, 1024), cut(1024, 1024), cut(2048, 1024)
        xwa, xg = cut(3072, SEQ), cut(3328, SEQ)
        waup, gup = cut(3584, RW), cut(4096, RW)
        mq_all, mk_all, mv_all, mo_all = (cut(4608 + 1024 * i, 1024) for i in range(4))
        AR = cut(8704, 2048).rearrange("p (t b two n) -> p t b two n", t=RT, b=NB, two=2)
        beta_all, kappa_all, g_all, bonus_all = (cut(10752 + 1024 * i, 1024) for i in range(4))
        v_tok = cut(14848, 1024).rearrange("p (b c) -> p b c", b=NB)
        beta_tok = cut(0, 1024).rearrange("p (b c) -> p b c", b=NB)
        kappa_tok = cut(1024, 1024).rearrange("p (b c) -> p b c", b=NB)
        y_tok = cut(2048, 1024)
        SC = cut(15872, 8192).rearrange("p (u f n) -> p u f n", u=16, f=4)
        a_all, logw, cumw, pinv, pprev, pfull, kk_all, tmp = (cut(24064 + 1024 * i, 1024) for i in range(8))
        Dm, DT, Tm, LM = (cut(24064 + 2048 * i, 2048).rearrange("p (u n) -> p u n", u=16) for i in range(4))
        vaug = cut(32256, NB * MH * 132).rearrange("p (b h n) -> p b h n", b=NB, h=MH)
        scT = cut(33312, MH * 384).rearrange("p (h n) -> p h n", h=MH)
        seq_x, seq_u = cut(34848, RW), cut(35360, RW)
        conv_sig = lambda t: cut(33312 + 1024 * t, 1024)
        states = [cut(at, RT * RN).rearrange("p (t n) -> p t n", t=RT) for at in (35872, 30208)]
        h_tok = mq_all
        yT = cut(8704, 2048).rearrange("p (k n) -> p k n", k=KT)
        mr = sb("mrows", [P, 6, SEQ])
        pend = sb("pend", [P, RT, NCH])
        gcol = sb("gcol", [P, 4 * MH])
        stat = sb("stat", [P, 4, 16])
        dcol = sb("dcol", [P, 8])

        ring_u = cut(0, RING * D).rearrange("p (j n) -> p j n", j=RING)
        ring_v = cut(8192, RING * D).rearrange("p (j n) -> p j n", j=RING)
        keyT = cut(16384, 2048).rearrange("p (i n) -> p i n", i=16)
        keys = cut(18432, 2048).rearrange("p (i n) -> p i n", i=16)
        cand = cut(18432, 2048).rearrange("p (h n) -> p h n", h=EH)
        qT = cut(20480, 4096).rearrange("p (i n) -> p i n", i=16)
        sc = cut(24576, 4096).rearrange("p (b i n) -> p b i n", b=NB, i=16)
        scr = cut(28672, 2048)
        onehot = cut(30720, 2048).rearrange("p (h k j) -> p h k j", h=EH, k=TOPK)
        v16 = cut(32768, 256).rearrange("p (i k) -> p i k", i=16)
        i16f = cut(33024, 256).rearrange("p (h two k) -> p h two k", h=EH, two=2)
        csc = cut(33280, SLOTS).rearrange("p (h k) -> p h k", h=EH)
        hilo = cut(33408, 2 * SLOTS).rearrange("p (w h k) -> p w h k", w=2, h=EH)
        e12 = cut(33664, 2 * SLOTS).rearrange("p (w h k) -> p w h k", w=2, h=EH)
        eidf = cut(33920, SLOTS)
        gate = cut(34048, NB * SLOTS).rearrange("p (b s) -> p b s", b=NB)
        hid = cut(34304, NB * SLOTS).rearrange("p (b s) -> p b s", b=NB)
        ga = cut(34560, NB * SLOTS).rearrange("p (b s) -> p b s", b=NB)
        diag = cut(34816, DIAGS * P).rearrange("p (j n) -> p j n", j=DIAGS)
        gsum = cut(35328, 2 * EH)
        qT1 = cut(20480, 2048).rearrange("p (i n) -> p i n", i=16)
        hstage = cut(35344, 2 * RING).rearrange("p (k j) -> p k j", k=2)
        gstage = cut(35360, 2 * RING).rearrange("p (k j) -> p k j", k=2)
        uints = cut(35376, 944).bitcast(U32)
        i16 = uints[:, 0:256].rearrange("p (i k) -> p i k", k=TOPK)
        pos = uints[:, 256:384].rearrange("p (h k) -> p h k", k=TOPK)
        hilo_u = uints[:, 384:640].rearrange("p (w s) -> p w s", w=2)
        eid = uints[:, 640:896].rearrange("p (b s) -> p b s", b=NB)
        ustage = uints[:, 896:912].rearrange("p (k j) -> p k j", k=2)
        vstage = uints[:, 912:928].rearrange("p (k j) -> p k j", k=2)

        kc = cut(22528, 2048).rearrange("p (t n) -> p t n", t=8)
        fv = cut(26624, 2048).rearrange("p (b n) -> p b n", b=NB)
        qc = cut(25600, 1024).rearrange("p (t n) -> p t n", t=8)
        fw = cut(24576, KT * P).rearrange("p (k n) -> p k n", k=KT)
        SQ = cut(28672, 2048).rearrange("p (t n) -> p t n", t=16)
        RS = cut(30720, 2048).rearrange("p (t n) -> p t n", t=16)
        lg = cut(28672, 4 * SEQ).rearrange("p (j n) -> p j n", j=4)
        prob = cut(29696, 4 * SEQ).rearrange("p (j n) -> p j n", j=4)
        probT = cut(30720, 4 * SEQ).rearrange("p (j s n) -> p j s n", j=4, s=2)
        ogT = cut(18432, 1024).rearrange("p (t n) -> p t n", t=KT)
        oT = cut(19456, 1024).rearrange("p (t n) -> p t n", t=KT)
        fz, fl, fc, fneg = mr[:, 0, 0:P], mr[:, 0, P:SEQ], mr[:, 1, :], mr[:, 2, :]
        amax, asum, arec = mr[:, 3, 0:32], mr[:, 3, 32:64], mr[:, 3, 64:96]

        class Steps:

            def __init__(self, eng, name):
                self.eng, self.sem, self.n = eng, S(name), 0

            def then(self, ins):
                ins.then_inc(self.sem, 1)
                self.n += 1

            def settle(self):
                self.eng.wait_ge(self.sem, self.n)

        block = ctx.enter_context(nc.Block())
        R2 = lambda ap: ap.rearrange("(r c) -> r c", c=P)

        @block.sync
        def _(sp):
            used = [0]

            def load_strips(n):
                for _ in range(n):
                    i = used[0]
                    used[0] += 1
                    src, w, _, _ = strips[i]
                    if i >= WRING:
                        await_filled(sp, strips[i - WRING][2], strips[i - WRING][3])
                    sp.dma_start(wring[:, i % WRING, :, 0:w], src).then_inc(S(f"strip_loaded{i % WRING}"), 16)

            sp.dma_start(xres[:], T["x"].rearrange("o (b p) d -> p (o b) d", p=P)).then_inc(S("x_loaded"), 16)
            load_strips(2)
            srcs = [("mu", T["l0_rwkv_mu"]), ("w0", T["l0_rwkv_w0"]), ("a0", T["l0_rwkv_a0"]), ("k_k", T["l0_rwkv_k_k"]),
                    ("k_a", T["l0_rwkv_k_a"])]
            for name, src in srcs:
                at, n = ROWS[name]
                sp.dma_start(prows[at:at + n, :], R2(src)).then_inc(S("params_loaded"), 16)
            for name, src in (("r_k", "l0_rwkv_r_k"), ("ln_g", "l0_rwkv_ln_g"), ("ln_b", "l0_rwkv_ln_b"),
                              ("qn_g", "l1_fox_qn_g"), ("kn_g", "l1_fox_kn_g")):
                at, n = ROWS[name]
                sp.dma_start(prows[at:at + n, :], T[src].rearrange("(t h) n -> t (h n)", h=2)).then_inc(S("params_loaded"), 16)
            at, n = ROWS["conv_w"]
            sp.dma_start(prows[at:at + n, :], T["l0_mlstm_conv_w"].rearrange("j (t c) -> (j t) c", c=P)).then_inc(S("params_loaded"), 16)
            at, n = ROWS["conv_b"]
            sp.dma_start(prows[at:at + n, :], R2(T["l0_mlstm_conv_b"])).then_inc(S("params_loaded"), 16)
            for name in ("hn_g", "hn_b"):
                at, n = ROWS[name]
                sp.dma_start(prows[at:at + n, :], T["l0_mlstm_" + name]).then_inc(S("params_loaded"), 16)
            sp.wait_ge(S("constants"), 1)
            for i, lo, name, n in ((0, 0, "l0_mlstm_ig_b", MH), (1, 0, "l0_mlstm_fg_b", MH), (2, 0, "l1_fox_f_b", FH),
                                   (2, 64, "l1_fox_f_b", FH)):
                sp.dma_start(small[lo:lo + n, i:i + 1], T[name].rearrange("(h o) -> h o", o=1)).then_inc(S("small_loaded"), 16)
            sp.dma_start(waup[0:64, :], T["l0_rwkv_w_up"]).then_inc(S("ups_loaded"), 16)
            sp.dma_start(waup[64:128, :], T["l0_rwkv_a_up"]).then_inc(S("ups_loaded"), 16)
            sp.dma_start(gup, T["l0_rwkv_g_up"]).then_inc(S("ups_loaded"), 16)

            def load_ln(e):
                name = ("l0_ln1", "l0_ln2", "l1_ln1", "l1_ln2")[NORMS[e][0]]
                if e:
                    sp.wait_ge(S("x_normed"), e)
                sp.dma_start(ln_par[:, 0, :], T[name + "_g"].partition_broadcast(P)).then_inc(S("ln_loaded"), 16)
                sp.dma_start(ln_par[:, 1, :], T[name + "_b"].partition_broadcast(P)).then_inc(S("ln_loaded"), 16)

            def load_keys(l):
                for half in range(2):
                    sp.dma_start(keys[:, half * EH:half * EH + EH, :],
                                 T[f"l{l}_peer_k{half + 1}"].rearrange("h n d -> n h d")).then_inc(S("keys_loaded"), 16)

            load_ln(0)
            load_strips(16 - 2 + 4)
            sp.wait_ge(S("x_normed"), 2)
            load_keys(0)
            load_ln(2)
            load_strips(8)
            sp.wait_ge(S("experts_chosen"), 2)
            load_keys(1)
            for b in range(NB):
                load_strips(17)
                load_ln(3 + 2 * b)
                load_strips(4 + 8)
                load_ln(4 + 2 * b)
            for b in range(NB):
                sp.wait_ge(S("x_normed"), 7 + b)
                sp.dma_start(out[0, b * P:(b + 1) * P, :], xres[:, b, :]).then_inc(S("stored"), 16)
            sp.wait_ge(S("stored"), 16 * NB)

        @block.gpsimd
        def _(pool):
            st = Steps(pool, "pool_step")
            st.then(pool.memset(ident[:], 1.0))
            st.settle()
            pool.affine_select(out=ident[:], in_=ident[:], compare_op=ALU.is_equal, fill=0.0, base=0, pattern=[[1, P]],
                               channel_multiplier=-1).then_inc(S("ident_ready"), 1)
            for t, v in ((pair_ones, 1.0), (ones, 1.0), (score_mask, 1.0),
                         (level_mask, 1.0), (level_one, 1.0), (small, 0.0), (causal_st, 1.0), (causal_ts, 0.0), (cexp, 1.0)):
                st.then(pool.memset(t[:], v))
            st.then(pool.memset(vaug, 1.0))
            st.settle()
            for i, eps in enumerate((LN_EPS, 1e-5 * RN, FN * 1e-6)):
                st.then(pool.memset(cexp[:, 2 + i:3 + i], eps))
            st.then(pool.iota(iota16[:], pattern=[[1, TOPK]], base=0, channel_multiplier=0,
                              allow_small_or_imprecise_dtypes=True))
            st.settle()

            def keep(ap, pattern, base, mult, op=ALU.is_ge, fill=0.0):
                st.then(pool.affine_select(out=ap, in_=ap, compare_op=op, fill=fill, base=base, pattern=pattern,
                                           channel_multiplier=mult))

            keep(pair_ones[:, 0:64], [[0, 64]], 63, -1)
            keep(pair_ones[:, 64:128], [[0, 64]], -64, 1)
            for i in range(2):
                keep(score_mask[:, i, :], [[1, P]], -1 if i % 2 == 0 else 0, -1)
            keep(causal_st[:, 0:P], [[1, P]], 0, -1)
            keep(causal_st[:, 2 * P:3 * P], [[1, P]], 0, -1)
            keep(causal_ts[:, SEQ:SEQ + P], [[-1, P]], 0, 1, ALU.is_ge, -1e30)
            keep(cexp[:, 0:1], [[0, 1]], -1000, 1)
            for i, m in enumerate([1] + LEVELS):
                v = level_mask[:, i, :].rearrange("p (g two m) -> p g two m", two=2, m=m)
                st.then(pool.memset(v[:, :, 0, :], 0.0))
            v = level_one[:].rearrange("p (g two) -> p g two", two=2)
            st.then(pool.memset(v[:, :, 1], 0.0))
            st.settle()
            for i in range(2):
                keep(score_mask[:, i, CH:P], [[0, CH]], -CH, 1)
            for i, m in enumerate([1] + LEVELS):
                v = level_mask[:, i, :].rearrange("p (g two m) -> p g two m", two=2, m=m)[:, :, 1, :]
                keep(v, [[-2 * m, P // (2 * m)], [0, m]], 0, 1)
            v = level_one[:].rearrange("p (g two) -> p g two", two=2)[:, :, 0]
            keep(v, [[-2, P // 2]], -1, 1)
            st.settle()
            for i, m in enumerate([1] + LEVELS):
                v = level_mask[:, i, :].rearrange("p (g two m) -> p g two m", two=2, m=m)[:, :, 1, :]
                keep(v, [[2 * m, P // (2 * m)], [0, m]], m - 1, -1)
            v = level_one[:].rearrange("p (g two) -> p g two", two=2)[:, :, 0]
            keep(v, [[2, P // 2]], 1, -1)
            st.settle()
            pool.sem_inc(S("constants"), 1)

            def gather(tab, ring, stage, j, k, row, free, value):
                pool.wait_ge(free, value)
                pool.sem_inc(S("gathers_issued"), 1)
                pool.indirect_dma_start(out=ring[:, j, :], out_offset=None, in_=tab,
                                        in_offset=bass.IndirectOffsetOnAxis(ap=stage[:, k, j:j + 1], axis=0)
                                        ).then_inc(S(f"{row}{j}"), 16)

            staged = [0]

            def gathers(b, tab, ring, stage, row, first, turns, slot_free):
                base = staged[0]
                staged[0] += turns * (UNROLL // RING)

                def turn(i):
                    for k in range(UNROLL // RING):
                        s0 = first + RING * k
                        free, value, step = slot_free(s0)
                        if free is not None:
                            pool.wait_ge(free, i * (UNROLL * step) + value)
                        pool.tensor_copy(stage[:, k, :], eid[:, b, bass.ds(i * UNROLL + s0, RING)]
                                         ).then_inc(S("indices_staged"), 1)
                        pool.wait_ge(S("indices_staged"), i * (UNROLL // RING) + (base + k + 1))
                        for j in range(RING):
                            free, value, step = slot_free(s0 + j)
                            if free is None:
                                free, value, step = S("indices_staged"), base + k + 1, 0
                            gather(tab, ring, stage, j, k, row, free, i * (UNROLL * step) + value if step else value)

                if turns > 1:
                    with pool.Fori(0, turns) as i:
                        turn(i)
                else:
                    turn(0)

            def gather_u(l, b):
                pool.wait_ge(S("experts_chosen"), 2 * l + b + 1)
                gathers(b, T[f"l{l}_peer_u"], ring_u, ustage, "u_row", 0, SLOTS // UNROLL,
                        lambda s: (S("u_rows_done"), SLOTS * (2 * l + b) + s + 1, 1))

            def gather_v(l, b):
                n = 2 * l + b
                after_pe = lambda s: (S("v_rows_done"), PE_ROWS * n + s + 1, 1)
                after_dve = lambda s: (S("sum_steps"), (2 + 2 * DVE_ROWS) * n + 2 * (s - RING - PE_ROWS) + 4, 2)
                last_call = lambda s: (S("sum_steps"), (2 + 2 * DVE_ROWS) * (n - 1) + 2 * (s - RING + DVE_ROWS) + 4, 2) if n else (None, 0, 0)
                args = (b, T[f"l{l}_peer_v"], ring_v, vstage, "v_row")
                gathers(*args, 0, 1, lambda s: last_call(s) if s < RING else after_pe(s))
                gathers(*args, UNROLL, PE_ROWS // UNROLL - 1, after_pe)
                gathers(*args, PE_ROWS, 1, lambda s: after_pe(s) if s < PE_ROWS + RING else after_dve(s))
                gathers(*args, PE_ROWS + UNROLL, DVE_ROWS // UNROLL - 1, after_dve)

            for l in range(2):
                for b in range(NB):
                    gather_u(l, b)
                    gather_v(l, b)

        @block.tensor
        def _(pe):
            mm, tp = nc.tensor.matmul, nc.tensor.transpose

            filled, nth = [0], {}

            def done(ins, name):
                assert fills[(name, nth.get(name, 0))] == filled[0] + 1
                nth[name] = nth.get(name, 0) + 1
                filled[0] += 1
                ins.then_inc(S("banks_filled"), 1)

            def turn_x(first, b, i):
                for half in range(2):
                    ps = claim(pe, "x_turn", first + half).rearrange("p (k n) -> p k n", k=4)
                    for q in range(4):
                        c = (4 * half + q) * P
                        last = tp(ps[:, q, :], xres[:, b, c:c + P], ident[:])
                    done(last, "x_turn")

            def project(ps, w, c0, cols, tok=slice(0, SEQ)):
                for k in range(KT):
                    last = mm(ps, w[:, k, c0:c0 + cols], xT[:, k, tok], start=(k == 0), stop=(k == KT - 1))
                return last

            def mixer0():
                pe.wait_ge(S("ident_ready"), 1)
                pe.wait_ge(S("x_loaded"), 16)
                for b in range(NB):
                    turn_x(2 * b, b, 0)
                pe.wait_ge(S("params_loaded"), 16 * 14)
                done(tp(claim(pe, "params", 0)[:, 0:NROWS], prows[0:NROWS, :], ident[0:NROWS, 0:NROWS]), "params")
                pe.wait_ge(S("x_turn_taken"), 4)

                def two_tiles_a_strip(name, n):
                    for t in range(n):
                        if t % 2 == 0:
                            w = next_strip(pe)
                        done(project(claim(pe, name, t)[:, 0:SEQ], w, P * (t % 2), P), name)

                two_tiles_a_strip("rwkv_in", 14)
                pe.wait_ge(S("constants"), 1)
                pe.wait_ge(S("ups_loaded"), 48)
                pe.wait_ge(S("lora_squashed"), 1)
                for name, lo, hi, up, low in (("lora_w", 0, 64, waup, xwa), ("lora_a", 64, 128, waup, xwa),
                                              ("lora_g", 0, 128, gup, xg)):
                    for half in range(2):
                        ps = claim(pe, name, half)
                        for q in range(2):
                            t = 2 * half + q
                            last = mm(ps[:, q * SEQ:(q + 1) * SEQ], up[lo:hi, t * P:(t + 1) * P], low[lo:hi, :],
                                      start=True, stop=True)
                        done(last, name)
                def head_sums(name, ready):
                    pe.wait_ge(S("head_products"), ready)
                    for half in range(2):
                        done(mm(claim(pe, name, half), pair_ones[:], tmp[:, half * 512:(half + 1) * 512],
                                start=True, stop=True), name)

                head_sums("kk_norm", 1)
                two_tiles_a_strip("conv_in", 8)
                head_sums("bonus", 2)
                pe.wait_ge(S("scan_operands"), 1)
                for i, src in enumerate((v_all, beta_all, kappa_all)):
                    for b in range(NB):
                        ps = claim(pe, "token_turn", NB * i + b).rearrange("p (t n) -> p t n", t=RT)
                        for t in range(RT):
                            last = tp(ps[:, t, :], src[:, t * SEQ + b * P:t * SEQ + (b + 1) * P], ident[:])
                        done(last, "token_turn")
                for u in range(16):
                    b, h = UNITS[u]
                    t, lo = h // 2, 64 * (h % 2)
                    ps = claim(pe, "scores", u)
                    ar = AR[lo:lo + 64, t, b, :, :].rearrange("p two n -> p (two n)")
                    c = t * SEQ + b * P
                    mm(ps[:, 0:256], beta_all[lo:lo + 64, c:c + P], ar, start=True, stop=True)
                    done(mm(ps[:, 256:512], kappa_all[lo:lo + 64, c:c + P], ar, start=True, stop=True), "scores")
                for g in range(4):
                    ps = claim(pe, "ab", g).rearrange("p (u n) -> p u n", u=4)
                    for q in range(4):
                        u = 4 * g + q
                        b, h = UNITS[u]
                        t, lo = h // 2, 64 * (h % 2)
                        c = t * SEQ + b * P
                        last = mm(ps[:, q, :], AR[lo:lo + 64, t, b, 0, :], beta_all[lo:lo + 64, c:c + P],
                                  start=True, stop=True)
                    done(last, "ab")
                for t in range(4):
                    w = next_strip(pe)
                    ps = claim(pe, "vo_in", t)
                    for q in range(2):
                        last = project(ps[:, q * SEQ:(q + 1) * SEQ], w, P * q, P)
                    done(last, "vo_in")
                w = next_strip(pe)
                ps = claim(pe, "gates_in", 0)
                project(ps[0:MH, 0:SEQ], w, 0, MH)
                done(project(ps[0:MH, SEQ:2 * SEQ], w, MH, MH), "gates_in")
                nt = nd = 0
                for i, m in enumerate(LEVELS):
                    last_level = m == LEVELS[-1]
                    for g in range(4):
                        pe.wait_ge(S("merge_ready"), 4 * i + g + 1)
                        ps = claim(pe, "inv_t", nt).rearrange("p (u n) -> p u n", u=4)
                        for q in range(4):
                            last = mm(ps[:, q, :], LM[:, 4 * g + q, :], Dm[:, 4 * g + q, :], start=True, stop=True)
                        done(last, "inv_t")
                        nt += 1
                    for g in range(4):
                        pe.wait_ge(S("inv_t_taken"), 4 * i + g + 1)
                        if not last_level:
                            ps = claim(pe, "inv_d", nd).rearrange("p (u n) -> p u n", u=4)
                            for q in range(4):
                                last = mm(ps[:, q, :], DT[:, 4 * g + q, :], Tm[:, 4 * g + q, :], start=True, stop=True)
                            done(last, "inv_d")
                            nd += 1
                        ps = claim(pe, "inv_d", nd).rearrange("p (u n) -> p u n", u=4)
                        for q in range(4):
                            last = mm(ps[:, q, :], Tm[:, 4 * g + q, :], DT[:, 4 * g + q, :], start=True, stop=True)
                        done(last, "inv_d")
                        nd += 1

                pe.wait_ge(S("m_rows"), 1)
                ps = claim(pe, "mrow_turn", 0)
                for i, row in enumerate((2, 5)):
                    for b in range(NB):
                        c = (2 * i + b) * MH
                        last = tp(ps[:, c:c + MH], mr[0:MH, row, b * P:(b + 1) * P], ident[0:MH, 0:MH])
                done(last, "mrow_turn")
                for b in range(NB):
                    ps = claim(pe, "mv_turn", b).rearrange("p (h n) -> p h n", h=MH)
                    for h in range(MH):
                        last = tp(ps[:, h, :], mv_all[:, h * SEQ + b * P:h * SEQ + (b + 1) * P], ident[:])
                    done(last, "mv_turn")
                for i in range(2):
                    ps = claim(pe, "mx_row", i)
                    for q in range(2):
                        h = 2 * i + q
                        last = mm(ps[:, q * SEQ:(q + 1) * SEQ], ident[0:MH, h:h + 1].to_broadcast([MH, P]),
                                  mr[0:MH, 4, :], start=True, stop=True)
                    done(last, "mx_row")
                for h in range(MH):
                    ps = claim(pe, "qk", h)
                    q, k = mq_all[:, h * SEQ:(h + 1) * SEQ], mk_all[:, h * SEQ:(h + 1) * SEQ]
                    mm(ps[:, 0:SEQ], k[:, 0:P], q, start=True, stop=True)
                    done(mm(ps[:, SEQ:SEQ + P], k[:, P:SEQ], q[:, P:SEQ], start=True, stop=True), "qk")
                def values(b):
                    for i in range(2):
                        pe.wait_ge(S("qk_taken"), 2 * i + 2)
                        ps = claim(pe, "hnum", 2 * b + i).rearrange("p (q n) -> p q n", q=2)
                        for q in range(2):
                            h = 2 * i + q
                            for s in range(b + 1):
                                c = b * P if s == 0 else SEQ
                                last = mm(ps[:, q, 0:MN + 1], scT[:, h, c:c + P], vaug[:, s, h, 0:MN + 1],
                                          start=(s == 0), stop=(s == b))
                        done(last, "hnum")

                pe.wait_ge(S("inv_d_taken"), nd)
                for c in range(NCH):
                    b, lo = c // 2, CH * (c % 2)
                    rows = slice(lo, lo + CH)
                    if c:
                        pe.wait_ge(S("state_ready"), c)
                    ps = claim(pe, "seq_x", c)
                    chunk_rows(c, ps, 0, [(2, v_tok[:, b, :])], "seq_x")
                    ps = claim(pe, "seq_u", c)
                    pe.wait_ge(S("seq_x_taken"), c + 1)
                    for h in range(RH):
                        last = mm(ps[rows, h * RN:(h + 1) * RN], DT[rows, UNIT[(b, h)], rows],
                                  seq_x[rows, h * RN:(h + 1) * RN], start=True, stop=True)
                    done(last, "seq_u")
                    pe.wait_ge(S("seq_u_taken"), c + 1)
                    if c < NCH - 1:
                        ps = claim(pe, "seq_s", c).rearrange("p (t n) -> p t n", n=RN)
                        for h in range(RH):
                            t, hp = h // 2, 64 * (h % 2)
                            cols = slice(h * RN, (h + 1) * RN)
                            mm(ps[hp:hp + 64, t, :], kappa_tok[rows, b, cols], v_tok[rows, b, cols], start=True, stop=False)
                            last = mm(ps[hp:hp + 64, t, :], beta_tok[rows, b, cols], seq_u[rows, cols], start=False, stop=True)
                        done(last, "seq_s")
                    ps = claim(pe, "seq_y", c)
                    chunk_rows(c, ps, 1, [(3, v_tok[:, b, :]), (1, seq_u)], "seq_y")
                    if c < NB:
                        values(c)
                for i, (src, sem) in enumerate(((y_tok, "y_normed"), (h_tok, "h_normed"))):
                    pe.wait_ge(S(sem), 1)
                    for b in range(NB):
                        ps = claim(pe, "y_turn", NB * i + b).rearrange("p (t n) -> p t n", t=RT)
                        for t in range(RT):
                            last = tp(ps[:, t, :], src[:, b * 512 + t * P:b * 512 + (t + 1) * P], ident[:])
                        done(last, "y_turn")
                pe.wait_ge(S("mixed"), 1)
                for i in range(4):
                    w = next_strip(pe)
                    ps = claim(pe, "mix_out", i)
                    for b in range(NB):
                        for k in range(KT):
                            last = mm(ps[:, b * STRIP:(b + 1) * STRIP], yT[:, k, b * P:(b + 1) * P], w[:, k, :],
                                      start=(k == 0), stop=(k == KT - 1))
                    done(last, "mix_out")

            def chunk_rows(c, ps, which, products, name):
                b, lo = c // 2, CH * (c % 2)
                rows = slice(lo, lo + CH)

                def on_state(h, start, stop):
                    hp = 64 * (h % 2)
                    return mm(ps[rows, h * RN:(h + 1) * RN], AR[hp:hp + 64, h // 2, b, which, rows],
                              states[(c - 1) % 2][hp:hp + 64, h // 2, :], start=start, stop=stop, skip_group_check=True)

                last_far = max(h for h in range(RH) if 64 * (h % 2) != lo)
                opened = False

                for h in range(RH):
                    near = c > 0 and 64 * (h % 2) == lo
                    if near:
                        on_state(h, not opened, False)
                        opened = True
                    for i, (f, rhs) in enumerate(products):
                        last = mm(ps[rows, h * RN:(h + 1) * RN], SC[rows, UNIT[(b, h)], f, rows],
                                  rhs[rows, h * RN:(h + 1) * RN], start=not opened,
                                  stop=(c == 0 and h == RH - 1 and i == len(products) - 1), skip_group_check=True)
                        opened = True
                if c:
                    last.then_inc(S("row_tile_done"), 1)
                    far_waits[0] += 1
                    pe.wait_ge(S("row_tile_done"), far_waits[0])
                    for h in range(RH):
                        if 64 * (h % 2) != lo:
                            last = on_state(h, False, h == last_far)
                done(last, name)

            far_waits = [0]

            def turn_keys(l):
                pe.wait_ge(S("keys_loaded"), 32 * (l + 1))
                for i in range(4):
                    ps = claim(pe, "key_turn", 4 * l + i).rearrange("p (q n) -> p q n", q=4)
                    for q in range(4):
                        last = tp(ps[:, q, :], keys[:, 4 * i + q, :], ident[:])
                    done(last, "key_turn")

            def score_keys(first, l, queries):
                pe.wait_ge(S("key_turn_taken"), 4 * (l + 1))
                for i in range(4):
                    ps = claim(pe, "peer_s", first + i).rearrange("p (q n) -> p q n", q=4)
                    for q in range(4):
                        j = 4 * i + q
                        last = mm(ps[:, q, :], queries(j), keyT[:, (j % 2) * EH + j // 2, :], start=True, stop=True)
                    done(last, "peer_s")

            def peer_scores0():
                for b in range(NB):
                    pe.wait_ge(S("x_normed"), 1 + b)
                    turn_x(4 + 2 * b, b, 0)
                turn_keys(0)
                pe.wait_ge(S("x_turn_taken"), 8)
                for i in range(8):
                    w = next_strip(pe)
                    ps = claim(pe, "peer_q", i)
                    for q in range(2):
                        last = project(ps[:, q * SEQ:(q + 1) * SEQ], w, P * q, P)
                    done(last, "peer_q")
                pe.wait_ge(S("peer_q_taken"), 8)
                for b in range(NB):
                    score_keys(4 * b, 0, lambda j: qT[:, j, b * P:(b + 1) * P])

            def peer_scores1(b):
                pe.wait_ge(S("x_normed"), 4 + 2 * b)
                turn_x(10 + 4 * b, b, 0)
                pe.wait_ge(S("x_turn_taken"), 12 + 4 * b)
                for i in range(4):
                    feature_strips("peer_q", 8 + 4 * b + i, b)
                pe.wait_ge(S("peer_q_taken"), 12 + 4 * b)
                score_keys(8 + 4 * b, 1, lambda j: qT1[:, j, :])

            def feature_strips(name, k, b):
                ps = claim(pe, name, k)
                for i in range(2):
                    w = next_strip(pe)
                    for q in range(2):
                        c = (2 * i + q) * P
                        last = project(ps[:, c:c + P], w, P * q, P, slice(b * P, (b + 1) * P))
                done(last, name)

            def token_strips(name, k, lhs):
                ps = claim(pe, name, k)
                for i in range(2):
                    w = next_strip(pe)
                    for kt in range(KT):
                        last = mm(ps[:, i * STRIP:(i + 1) * STRIP], lhs(kt), w[:, kt, :], start=(kt == 0), stop=(kt == KT - 1))
                done(last, name)

            def experts(l, b):
                n = 2 * l + b
                ps = [claim(pe, "experts", 2 * n + c) for c in range(2)]

                def rows(i):
                    for s in range(UNROLL):
                        j = s % RING
                        first = isinstance(i, int) and s == 0
                        pe.wait_ge(S("diags_made"), i * UNROLL + (PE_ROWS * n + s + 1))
                        pe.wait_ge(S(f"v_row{j}"), i * (16 * UNROLL // RING) + 16 * (SLOTS // RING * n + s // RING + 1))
                        mm(ps[0], diag[:, s % DIAGS, :], ring_v[:, j, 0:512], start=first, stop=True, skip_group_check=True)
                        mm(ps[1], diag[:, s % DIAGS, :], ring_v[:, j, 512:1024], start=first, stop=True, skip_group_check=True
                           ).then_inc(S("v_rows_done"), 1)

                rows(0)
                with pe.Fori(1, PE_ROWS // UNROLL) as i:
                    rows(i)

            def mixer1(b):
                tok = slice(b * P, (b + 1) * P)
                pe.wait_ge(S("x_normed"), 3 + 2 * b)
                turn_x(8 + 4 * b, b, 0)
                pe.wait_ge(S("x_turn_taken"), 10 + 4 * b)
                for i in range(4):
                    feature_strips("fox_qk", 4 * b + i, b)
                for i in range(2):
                    token_strips("fox_v", 2 * b + i, lambda kt: xT[:, kt, tok])
                for i in range(2):
                    feature_strips("fox_og", 2 * b + i, b)
                strip_at[0] += 1
                pe.wait_ge(S("f_weights"), b + 1)
                done(project(claim(pe, "fox_f", b)[:, 0:P], fw, 0, P, tok), "fox_f")
                for i in range(4):
                    pe.wait_ge(S("squares"), 4 * b + i + 1)
                    done(mm(claim(pe, "fox_rms", 4 * b + i), pair_ones[:], SQ[:, 4 * i:4 * i + 4, :].rearrange("p t n -> p (t n)"),
                            start=True, stop=True), "fox_rms")
                pe.wait_ge(S("qk_normed"), b + 1)
                pe.wait_ge(S("decay_rows"), b + 1)
                w = P * (b + 1)
                for name, u in attention_plan(b):
                    if name == "att":
                        h = u % FH
                        t, lo = h // 2, 64 * (h % 2)
                        ps = claim(pe, "att", u)[:, 0:w]
                        mm(ps, qc[lo:lo + 64, t, :], kc[lo:lo + 64, t, 0:w], start=True, stop=False)
                        done(mm(ps, ident[lo:lo + 64, lo + h:lo + h + 1].to_broadcast([64, P]), fneg[lo:lo + 64, 0:w],
                                start=False, stop=True), "att")
                    elif name == "att_turn":
                        pe.wait_ge(S("probs_ready"), u + 1)
                        ps = claim(pe, "att_turn", u)
                        for s in range(b + 1):
                            last = tp(ps[:, s * P:(s + 1) * P], prob[:, u % 4, s * P:(s + 1) * P], ident[:])
                        done(last, "att_turn")
                    else:
                        ps = claim(pe, "att_out", u)
                        for q in range(2):
                            n = 2 * u + q
                            h = n % FH
                            lo = 64 * (h % 2)
                            pe.wait_ge(S("att_turn_taken"), n + 1)
                            for s in range(b + 1):
                                last = mm(ps[lo:lo + 64, 0:P], fv[:, s, h * FN:(h + 1) * FN], probT[:, n % 4, s, :],
                                          start=(s == 0), stop=(s == b))
                        done(last, "att_out")
                pe.wait_ge(S("mixed"), b + 2)
                for i in range(2):
                    token_strips("mix_out", 4 + 2 * b + i, lambda kt: oT[:, kt, :])

            pe.sem_inc(S("v_rows_done"), RING)
            mixer0()
            peer_scores0()
            experts(0, 0)
            turn_keys(1)
            mixer1(0)
            peer_scores1(0)
            experts(0, 1)
            mixer1(1)
            peer_scores1(1)
            experts(1, 0)
            experts(1, 1)

        @block.scalar
        def _(act):
            st = Steps(act, "scalar_step")
            af = nc.scalar.activation

            def taken(ins, name):
                ins.then_inc(S(name + "_taken"), 1)

            def copy(out_, in_):
                return nc.scalar.copy(out_, in_)

            ZERO, ONE, EPS_LN, EPS_RWKV, EPS_FOX = (cexp[:, i:i + 1] for i in range(5))

            def root(ready, n, ap, bias, scale, sem):
                act.wait_ge(S(ready), n)
                af(ap, ap, ACT.Sqrt, bias=bias, scale=scale).then_inc(S(sem), 1)

            def ln_root(e):
                root("ln_var", e + 1, lnmv[:, NORMS[e][1], 1:2], EPS_LN, 1.0, "ln_std")

            def take_x(first, b):
                for half in range(2):
                    ps = full(act, "x_turn", first + half)
                    taken(copy(xT[:, 4 * half:4 * half + 4, b * P:(b + 1) * P], ps.rearrange("p (k n) -> p k n", k=4)),
                          "x_turn")

            def mixer0():
                for b in range(NB):
                    take_x(2 * b, b)
                act.wait_ge(S("constants"), 1)
                act.wait_ge(S("params_taken"), 1)
                act.wait_ge(S("one_mu"), 1)
                for t in range(14):
                    ps = full(act, "rwkv_in", t)[:, 0:SEQ]
                    af(R[:, t * SEQ:(t + 1) * SEQ], ps, ACT.Identity, bias=ZERO, scale=one_mu[:, t:t + 1]
                       ).then_inc(S("rwkv_scaled"), 1)
                act.wait_ge(S("rwkv_in_taken"), 14)
                af(xg, xg, ACT.Sigmoid)
                af(xwa[0:64, :], xwa[0:64, :], ACT.Tanh).then_inc(S("lora_squashed"), 1)
                for name, dst, bias in (("lora_w", logw, "w0"), ("lora_a", a_all, "a0")):
                    for half in range(2):
                        ps = full(act, name, half)
                        for q in range(2):
                            t = 2 * half + q
                            last = af(dst[:, t * SEQ:(t + 1) * SEQ], ps[:, q * SEQ:(q + 1) * SEQ], ACT.Sigmoid,
                                      bias=par(bias, t), scale=1.0)
                        taken(last, name)
                for half in range(2):
                    taken(copy(g_all[:, half * 512:(half + 1) * 512], full(act, "lora_g", half)), "lora_g")
                for half in range(2):
                    taken(af(tmp[:, half * 512:(half + 1) * 512], full(act, "kk_norm", half), ACT.Sqrt, bias=ZERO), "kk_norm")
                act.wait_ge(S("cum_ready"), 1)
                af(pfull, cumw, ACT.Exp)
                af(pinv, cumw, ACT.Exp, scale=-1.0)
                act.wait_ge(S("cum_ready"), 2)
                af(pprev, pprev, ACT.Exp).then_inc(S("decays"), 1)
                for t in range(8):
                    ps = full(act, "conv_in", t)[:, 0:SEQ]
                    dst = cut(4608 + t * SEQ, SEQ)
                    af(dst, ps, ACT.Identity, bias=par("conv_b", t), scale=par("conv_w", 24 + t)).then_inc(S("conv_scaled"), 1)
                for i, dst in enumerate((v_tok, beta_tok, kappa_tok)):
                    for b in range(NB):
                        taken(copy(dst[:, b, :], full(act, "token_turn", NB * i + b)), "token_turn")
                act.wait_ge(S("conv_in_taken"), 8)
                for t in range(2):
                    af(conv_sig(t), cut(4608 + t * 1024, 1024), ACT.Sigmoid).then_inc(S("conv_sigmoid"), 1)
                for t in range(2):
                    taken(copy(mv_all[:, t * 512:(t + 1) * 512], full(act, "vo_in", t)), "vo_in")
                for t in range(2):
                    taken(af(mo_all[:, t * 512:(t + 1) * 512], full(act, "vo_in", 2 + t), ACT.Sigmoid), "vo_in")
                act.wait_ge(S("small_loaded"), 64)
                ps = full(act, "gates_in", 0)
                af(mr[0:MH, 0, :], ps[0:MH, 0:SEQ], ACT.Identity, bias=small[0:MH, 0:1], scale=1.0)
                taken(af(mr[0:MH, 1, :], ps[0:MH, SEQ:2 * SEQ], ACT.Identity, bias=small[0:MH, 1:2], scale=1.0), "gates_in")
                for i in range(len(LEVELS)):
                    for g in range(4):
                        taken(copy(Tm[:, 4 * g:4 * g + 4, :], full(act, "inv_t", 4 * i + g).rearrange("p (u n) -> p u n", u=4)),
                              "inv_t")
                    if i == 1:
                        act.wait_ge(S("m_abs"), 1)
                        st.then(af(mr[0:MH, 3, :], mr[0:MH, 3, :], ACT.Exp, scale=-1.0))
                        st.settle()
                        af(mr[0:MH, 3, :], mr[0:MH, 3, :], ACT.Ln, bias=ONE[0:MH]).then_inc(S("m_log"), 1)
                        act.wait_ge(S("m_neg"), 1)
                        af(mr[0:MH, 5, :], mr[0:MH, 5, :], ACT.Exp).then_inc(S("m_rows"), 1)
                for b in range(NB):
                    taken(copy(vaug[:, b, :, 0:MN], full(act, "mv_turn", b).rearrange("p (h n) -> p h n", h=MH)), "mv_turn")
                for h in range(MH):
                    act.wait_ge(S("mx_clamped"), h + 1)
                    af(scT[:, h, :], scT[:, h, :], ACT.Exp).then_inc(S("m_weights"), 1)
                for c in range(NCH):
                    if c == NB:
                        root("head_var", 1, stat[:, 1, 0:NB * MH], EPS_LN, 1.0 / MN, "head_std")
                    rows = slice(CH * (c % 2), CH * (c % 2) + CH)
                    taken(copy(seq_x[rows, :], full(act, "seq_x", c)[rows, :]), "seq_x")
                    taken(af(seq_u[rows, :], full(act, "seq_u", c)[rows, :], ACT.Copy, scale=-1.0), "seq_u")
                root("head_var", 2, stat[:, 1, 0:NB * RH], EPS_RWKV, 1.0 / RN, "head_std")
                for i, (g, bb) in enumerate((("ln_g", "ln_b"), ("hn_g", "hn_b"))):
                    for b in range(NB):
                        ps = full(act, "y_turn", NB * i + b)
                        for t in range(RT):
                            last = af(yT[:, 4 * i + t, b * P:(b + 1) * P], ps[:, t * P:(t + 1) * P], ACT.Identity,
                                      bias=par(bb, t), scale=par(g, t))
                        taken(last, "y_turn")
                ln_root(0)
                ln_root(1)

            def take_keys(l):
                for i in range(4):
                    taken(copy(keyT[:, 4 * i:4 * i + 4, :], full(act, "key_turn", 4 * l + i).rearrange("p (q n) -> p q n", q=4)),
                          "key_turn")

            def peer_scores0():
                for b in range(NB):
                    take_x(4 + 2 * b, b)
                take_keys(0)
                for i in range(8):
                    taken(copy(qT[:, 2 * i:2 * i + 2, :], full(act, "peer_q", i).rearrange("p (q n) -> p q n", q=2)), "peer_q")
                for b in range(NB):
                    for i in range(4):
                        ps = full(act, "peer_s", 4 * b + i).rearrange("p (q n) -> p q n", q=4)
                        taken(copy(sc[:, b, 4 * i:4 * i + 4, :], ps), "peer_s")

            def peer_scores1(b):
                take_x(10 + 4 * b, b)
                for i in range(4):
                    taken(copy(qT1[:, 4 * i:4 * i + 4, :], full(act, "peer_q", 8 + 4 * b + i).rearrange("p (q n) -> p q n", q=4)),
                          "peer_q")
                for i in range(4):
                    ps = full(act, "peer_s", 8 + 4 * b + i).rearrange("p (q n) -> p q n", q=4)
                    taken(copy(sc[:, 0, 4 * i:4 * i + 4, :], ps), "peer_s")

            def activate(l, b):
                n = 2 * l + b
                act.wait_ge(S("gate_shifted"), n + 1)
                g = gate[:, b, :]
                af(g, g, ACT.Exp).then_inc(S("gate_exp"), 1)
                act.wait_ge(S("hidden"), n + 1)
                af(ga[:, b, :], hid[:, b, :], ACT.Gelu).then_inc(S("gelued"), 1)

            def diags(l, b):
                n = 2 * l + b
                act.wait_ge(S("weights"), n + 1)
                with act.Fori(0, PE_ROWS // UNROLL) as i:
                    for k in range(UNROLL // RING):
                        act.wait_ge(S("v_rows_done"), i * UNROLL + (PE_ROWS * n + RING * k + 1))
                        copy(gstage[:, k, :], ga[:, b, bass.ds(i * UNROLL + RING * k, RING)]).then_inc(S("weights_staged"), 1)
                        act.wait_ge(S("weights_staged"), i * (UNROLL // RING) + (PE_ROWS // RING * n + k + 1))
                        for j in range(RING):
                            s = RING * k + j
                            act.wait_ge(S("v_rows_done"), i * UNROLL + (PE_ROWS * n + s + 1 + RING - DIAGS))
                            af(diag[:, s % DIAGS, :], ident[:], ACT.Copy, scale=gstage[:, k, j:j + 1]
                               ).then_inc(S("diags_made"), 1)

            def mixer1(b):
                tok = slice(b * P, (b + 1) * P)
                wide = lambda ps: ps.rearrange("p (t n) -> p t n", n=P)
                take_x(8 + 4 * b, b)
                for i in range(4):
                    dst = qc[:, 4 * i:4 * i + 4, :] if i < 2 else kc[:, 4 * i - 8:4 * i - 4, tok]
                    taken(copy(dst, wide(full(act, "fox_qk", 4 * b + i))), "fox_qk")
                for i in range(2):
                    taken(copy(fv[:, b, i * 512:(i + 1) * 512], full(act, "fox_v", 2 * b + i)), "fox_v")
                for i in range(2):
                    taken(af(ogT[:, 4 * i:4 * i + 4, :], wide(full(act, "fox_og", 2 * b + i)), ACT.Sigmoid), "fox_og")
                n = strips_before_f[b]
                act.wait_ge(S(f"strip_loaded{n % WRING}"), 16 * (n // WRING + 1))
                act.wait_ge(S("f_zeroed"), b + 1)
                copy(fw[:, :, 0:FH], wring[:, n % WRING, :, 0:FH])
                copy(fw[:, :, 64:64 + FH], wring[:, n % WRING, :, 0:FH]).then_inc(S("f_weights"), 1)
                taken(af(fz, full(act, "fox_f", b)[:, 0:P], ACT.Identity, bias=small[:, 2:3], scale=1.0), "fox_f")
                act.wait_ge(S("f_abs"), b + 1)
                st.then(af(fl, fl, ACT.Exp, scale=-1.0))
                st.settle()
                af(fl, fl, ACT.Ln, bias=ONE).then_inc(S("f_log"), 1)
                for i in range(4):
                    taken(af(RS[:, 4 * i:4 * i + 4, :], wide(full(act, "fox_rms", 4 * b + i)), ACT.Sqrt, bias=EPS_FOX), "fox_rms")
                w = P * (b + 1)
                for s in range(FH + 2):
                    if s < FH:
                        u = FH * b + s
                        act.wait_ge(S("logits_max"), u + 1)
                        if s >= 4:
                            await_filled(act, "att_turn", u - 4)
                        af(prob[:, u % 4, 0:w], lg[:, u % 4, 0:w], ACT.Exp, bias=amax[:, u:u + 1], scale=1.0,
                           accum_out=asum[:, u:u + 1]).then_inc(S("exped"), 1)
                    if s >= 2:
                        u = FH * b + s - 2
                        ps = full(act, "att_turn", u)
                        if s - 2 >= 4:
                            await_filled(act, "att_out", (u - 4) // 2)
                        taken(copy(probT[:, u % 4, 0:b + 1, :], wide(ps[:, 0:w])), "att_turn")
                ln_root(3 + 2 * b)

            mixer0()
            peer_scores0()
            activate(0, 0)
            diags(0, 0)
            ln_root(2)
            take_keys(1)
            mixer1(0)
            peer_scores1(0)
            activate(0, 1)
            diags(0, 1)
            ln_root(4)
            mixer1(1)
            peer_scores1(1)
            activate(1, 0)
            diags(1, 0)
            ln_root(6)
            activate(1, 1)
            diags(1, 1)
            ln_root(7)

        @block.vector
        def _(dve):
            v = nc.vector
            st = Steps(dve, "vector_step")
            tt, ts, stt = v.tensor_tensor, v.tensor_scalar, v.scalar_tensor_tensor

            def go(ins):
                st.then(ins)
                st.settle()

            def taken(ins, name):
                ins.then_inc(S(name + "_taken"), 1)

            def layer_norm(e):
                b = NORMS[e][1]
                parts = halves(b)
                dve.wait_ge(S("ln_loaded"), 32 * NORM_LOADS[e])
                for c, part in enumerate(parts):
                    st.then(v.bn_stats(lnst[:, b, 6 * c:6 * c + 6], part))
                st.settle()
                v.bn_aggr(lnmv[:, b, :], lnst[:, b, :]).then_inc(S("ln_var"), 1)
                dve.wait_ge(S("ln_std"), e + 1)
                go(v.reciprocal(lnrs[:, b:b + 1], lnmv[:, b, 1:2]))
                for c, part in enumerate(parts):
                    st.then(ts(part, part, lnmv[:, b, 0:1], lnrs[:, b:b + 1], ALU.subtract, ALU.mult))
                st.settle()
                go(tt(xres[:, b, :], xres[:, b, :], ln_par[:, 0, :], ALU.mult))
                tt(xres[:, b, :], xres[:, b, :], ln_par[:, 1, :], ALU.add).then_inc(S("x_normed"), 1)
                dve.wait_ge(S("x_normed"), e + 1)

            def head_norm(x, scratch, groups, n, norms, sem):
                g = x.rearrange("p (g n) -> p g n", n=n)
                q = scratch.rearrange("p (g n) -> p g n", n=n)
                mean, ss = stat[:, 0, 0:groups], stat[:, 1, 0:groups]
                wide = lambda s: s.rearrange("p (g o) -> p g o", o=1).to_broadcast([P, groups, n])
                go(v.tensor_reduce(mean, g, AX_X, ALU.add))
                go(ts(mean, mean, 1.0 / n, None, ALU.mult))
                go(tt(g, g, wide(mean), ALU.subtract))
                go(tt(q, g, g, ALU.mult))
                v.tensor_reduce(ss, q, AX_X, ALU.add).then_inc(S("head_var"), 1)
                dve.wait_ge(S("head_std"), norms)
                go(v.reciprocal(ss, ss))
                tt(g, g, wide(ss), ALU.mult).then_inc(S(sem), 1)

            def log_sigmoid(z, t, o, ready, logged, n=1):
                stt(t, z, -1.0, z, ALU.mult, ALU.max).then_inc(S(ready), 1)
                dve.wait_ge(S(logged), n)
                go(stt(o, z, 0.0, t, ALU.min, ALU.subtract))

            def mlstm_values(b):
                for i in range(2):
                    n = 2 * b + i
                    ps = full(dve, "hnum", n).rearrange("p (q n) -> p q n", q=2)
                    d = dcol[:, 2 * n:2 * n + 2]
                    go(v.tensor_copy(d, ps[:, :, MN]))
                    go(stt(d, d, -1.0, d, ALU.mult, ALU.max))
                    go(tt(d, d, gcol[:, 2 * MH + MH * b + 2 * i:2 * MH + MH * b + 2 * i + 2], ALU.max))
                    go(v.reciprocal(d, d))
                    for q in range(2):
                        c = b * 512 + (2 * i + q) * MN
                        ins = ts(h_tok[:, c:c + MN], ps[:, q, 0:MN], d[:, q:q + 1], None, ALU.mult)
                        if q == 0:
                            st.then(ins)
                    taken(ins, "hnum")

            def mlstm_rows():
                dve.wait_ge(S("gates_in_taken"), 1)
                rows = [mr[0:MH, i, :] for i in range(6)]
                log_sigmoid(rows[1], rows[3], rows[1], "m_abs", "m_log")
                go(v.tensor_tensor_scan(rows[3], ones[0:MH, :], rows[1], 0.0, ALU.mult, ALU.add))
                go(tt(rows[2], rows[0], rows[3], ALU.subtract))
                go(v.tensor_tensor_scan(rows[4], rows[2], rows[2], 0.0, ALU.max, ALU.max))
                go(tt(rows[5], rows[3], rows[4], ALU.add))
                go(ts(rows[5], rows[5], -1.0, None, ALU.mult))
                ts(rows[4], rows[4], -1.0, None, ALU.mult).then_inc(S("m_neg"), 1)
                dve.wait_ge(S("conv_sigmoid"), 1)
                stt(mq_all, mq_all, float(MN) ** -0.5, conv_sig(0), ALU.mult, ALU.mult).then_inc(S("silu"), 1)
                dve.wait_ge(S("conv_sigmoid"), 2)
                tt(mk_all, mk_all, conv_sig(1), ALU.mult).then_inc(S("silu"), 1)
                dve.wait_ge(S("silu"), 2)

            def mixer0():
                dve.wait_ge(S("constants"), 1)
                taken(v.tensor_copy(pars[:, 0:NROWS], full(dve, "params", 0)[:, 0:NROWS]), "params")
                dve.wait_ge(S("params_taken"), 1)
                st.then(ts(kn8[:], pars[:, ROWS["kn_g"][0]:ROWS["kn_g"][0] + 8], float(FN) ** 0.5, None, ALU.mult))
                ts(one_mu[:], pars[:, 0:14], -1.0, 1.0, ALU.mult, ALU.add).then_inc(S("one_mu"), 1)
                for t in range(14):
                    dve.wait_ge(S("rwkv_scaled"), t + 1)
                    ps = full(dve, "rwkv_in", t)
                    dst = R[:, t * SEQ + 1:(t + 1) * SEQ]
                    taken(stt(dst, ps[:, 0:SEQ - 1], par("mu", t), dst, ALU.mult, ALU.add), "rwkv_in")
                dve.wait_ge(S("rwkv_in_taken"), 14)
                for t in range(RT):
                    st.then(ts(kk_all[:, t * SEQ:(t + 1) * SEQ], k_all[:, t * SEQ:(t + 1) * SEQ], par("k_k", t), None, ALU.mult))
                st.settle()
                tt(tmp, kk_all, kk_all, ALU.mult).then_inc(S("head_products"), 1)
                dve.wait_ge(S("lora_w_taken"), 2)
                go(ts(logw, logw, -float(2.718281828459045 ** -0.5), None, ALU.mult))
                for i in range(RT * NCH):
                    ins = v.tensor_tensor_scan(cumw[:, i * CH:(i + 1) * CH], ones[:, 0:CH], logw[:, i * CH:(i + 1) * CH], 0.0,
                                               ALU.mult, ALU.add)
                    if i < RT * NCH - 1:
                        st.then(ins)
                ins.then_inc(S("cum_ready"), 1)
                dve.wait_ge(S("cum_ready"), 1)
                tt(pprev, cumw, logw, ALU.subtract).then_inc(S("cum_ready"), 1)
                dve.wait_ge(S("kk_norm_taken"), 2)
                go(ts(tmp, tmp, 1e-12, None, ALU.max))
                go(v.reciprocal(tmp, tmp))
                go(tt(kk_all, kk_all, tmp, ALU.mult))
                dve.wait_ge(S("lora_a_taken"), 2)
                for t in range(RT):
                    c = slice(t * SEQ, (t + 1) * SEQ)
                    st.then(ts(tmp[:, c], a_all[:, c], 1.0, par("k_a", t), ALU.subtract, ALU.mult))
                st.settle()
                go(stt(k_all, tmp, 1.0, k_all, ALU.add, ALU.mult))
                for t in range(RT):
                    c = slice(t * SEQ, (t + 1) * SEQ)
                    ins = stt(tmp[:, c], r_all[:, c], par("r_k", t), k_all[:, c], ALU.mult, ALU.mult)
                ins.then_inc(S("head_products"), 1)
                dve.wait_ge(S("decays"), 1)
                view = lambda x: x.rearrange("p (t b n) -> p t b n", t=RT, b=NB)
                st.then(v.tensor_copy(pend[:], pfull.rearrange("p (t c n) -> p t c n", t=RT, c=NCH)[:, :, :, CH - 1]))
                st.then(tt(AR[:, :, :, 0, :], view(kk_all), view(pprev), ALU.mult))
                st.then(tt(AR[:, :, :, 1, :], view(r_all), view(pfull), ALU.mult))
                go(tt(beta_all, kk_all, a_all, ALU.mult))
                st.then(tt(beta_all, beta_all, pinv, ALU.mult))
                tt(kappa_all, k_all, pinv, ALU.mult).then_inc(S("scan_operands"), 1)
                for t in range(8):
                    dve.wait_ge(S("conv_scaled"), t + 1)
                    ps = full(dve, "conv_in", t)
                    for back in (1, 2, 3):
                        dst = cut(4608 + t * SEQ, SEQ)[:, back:SEQ]
                        ins = stt(dst, ps[:, 0:SEQ - back], par("conv_w", 8 * (3 - back) + t), dst, ALU.mult, ALU.add)
                        if back < 3:
                            go(ins)
                        else:
                            taken(ins, "conv_in")
                for half in range(2):
                    c = slice(half * 512, (half + 1) * 512)
                    taken(tt(bonus_all[:, c], full(dve, "bonus", half), v_all[:, c], ALU.mult), "bonus")
                for u in range(16):
                    ps = full(dve, "scores", u).rearrange("p (f n) -> p f n", f=2)
                    taken(tt(SC[:, u, :, :].rearrange("p (f g) n -> p f (g n)", f=2), ps,
                             score_mask[:].rearrange("p g n -> p (g n)").unsqueeze(1).to_broadcast([P, 2, 2 * P]), ALU.mult),
                          "scores")
                dve.wait_ge(S("scores_taken"), 16)
                wide = lambda m: m.unsqueeze(1).to_broadcast([P, 4, P])
                for g in range(4):
                    us = slice(4 * g, 4 * g + 4)
                    ps = full(dve, "ab", g).rearrange("p (u n) -> p u n", u=4)
                    taken(stt(Dm[:, us, :], ps, -1.0, wide(level_one[:]), ALU.mult, ALU.mult), "ab")
                    st.then(stt(DT[:, us, :], SC[:, us, 0, :], -1.0, wide(level_mask[:, 0, :]), ALU.mult, ALU.mult))
                dve.wait_ge(S("ab_taken"), 4)
                st.settle()
                nd = 0
                for g in range(4):
                    us = slice(4 * g, 4 * g + 4)
                    st.then(tt(Dm[:, us, :], Dm[:, us, :], wide(ident[:]), ALU.add))
                    st.then(tt(DT[:, us, :], DT[:, us, :], wide(ident[:]), ALU.add))
                for i, m in enumerate(LEVELS):
                    for g in range(4):
                        us = slice(4 * g, 4 * g + 4)
                        if i:
                            await_filled(dve, "inv_t", 4 * (i - 1) + g)
                        tt(LM[:, us, :], SC[:, us, 0, :], wide(level_mask[:, i + 1, :]), ALU.mult).then_inc(S("merge_ready"), 1)
                    for g in range(4):
                        us = slice(4 * g, 4 * g + 4)
                        for which in ((DT,) if m == LEVELS[-1] else (Dm, DT)):
                            if which is Dm:
                                await_filled(dve, "inv_d", nd + 1)
                            ps = full(dve, "inv_d", nd).rearrange("p (u n) -> p u n", u=4)
                            if i == 0:
                                st.settle()
                            taken(tt(which[:, us, :], which[:, us, :], ps, ALU.subtract), "inv_d")
                            nd += 1
                    dve.wait_ge(S("inv_d_taken"), nd)
                    if i == 1:
                        mlstm_rows()
                taken(v.tensor_copy(gcol[:], full(dve, "mrow_turn", 0)[:, 0:16]), "mrow_turn")
                dve.wait_ge(S("mrow_turn_taken"), 1)
                for i in range(2):
                    ps = full(dve, "mx_row", i)
                    for q in range(2):
                        h = 2 * i + q
                        st.then(ts(scT[:, h, 0:SEQ], ps[:, q * SEQ:(q + 1) * SEQ], gcol[:, h:h + 1], 0.0, ALU.add, ALU.min))
                        ins = ts(scT[:, h, SEQ:SEQ + P], ps[:, q * SEQ + P:(q + 1) * SEQ], gcol[:, MH + h:MH + h + 1], 0.0,
                                 ALU.add, ALU.min)
                        if q == 0:
                            st.then(ins)
                    taken(ins, "mx_row")
                    dve.wait_ge(S("mx_row_taken"), i + 1)
                    dve.sem_inc(S("mx_clamped"), 2)
                for h in range(MH):
                    dve.wait_ge(S("m_weights"), h + 1)
                    go(tt(scT[:, h, :], scT[:, h, :], causal_st[:], ALU.mult))
                    taken(tt(scT[:, h, :], full(dve, "qk", h)[:, 0:384], scT[:, h, :], ALU.mult), "qk")
                for c in range(NCH):
                    b, rows = c // 2, slice(CH * (c % 2), CH * (c % 2) + CH)
                    if c < NCH - 1:
                        ps = full(dve, "seq_s", c).rearrange("p (t n) -> p t n", n=RN)
                        state, before = states[c % 2], states[(c - 1) % 2]
                        if c == 0:
                            taken(v.tensor_copy(state, ps[:, 0:RT, :]), "seq_s")
                        else:
                            taken(tt(state, before, ps[:, 0:RT, :], ALU.add), "seq_s")
                        dve.wait_ge(S("seq_s_taken"), c + 1)
                        tt(state, state, pend[:, :, c:c + 1].to_broadcast([P, RT, RN]), ALU.mult).then_inc(S("state_ready"), 1)
                        dve.wait_ge(S("state_ready"), c + 1)
                    taken(v.tensor_copy(y_tok[rows, b * 512:(b + 1) * 512], full(dve, "seq_y", c)[rows, :]), "seq_y")
                    if c < NB:
                        mlstm_values(c)
                    if c == NB - 1:
                        dve.wait_ge(S("hnum_taken"), 4)
                        head_norm(h_tok, mk_all, NB * MH, MN, 1, "h_normed")
                dve.wait_ge(S("seq_y_taken"), NCH)
                head_norm(y_tok, kk2, NB * RH, RN, 2, "y_normed")
                yr = cut(8704, 1024)
                dve.wait_ge(S("y_turn_taken"), 2)
                go(tt(yr, yr, bonus_all, ALU.add))
                go(tt(yr, yr, g_all, ALU.mult))
                dve.wait_ge(S("y_turn_taken"), 4)
                ym = cut(9728, 1024)
                tt(ym, ym, mo_all, ALU.mult).then_inc(S("mixed"), 1)
                for i in range(4):
                    ps = full(dve, "mix_out", i).rearrange("p (b n) -> p b n", b=NB)
                    x = xres[:, :, i * STRIP:(i + 1) * STRIP]
                    taken(stt(x, x, ALPHA, ps, ALU.mult, ALU.add), "mix_out")
                dve.wait_ge(S("mix_out_taken"), 4)
                for b in range(NB):
                    layer_norm(b)

            kk2 = cut(24064, 1024)

            def halves(b):
                return [xres[:, b, c * 512:(c + 1) * 512] for c in range(2)]

            def top16(src, scratch, vals, idx, n):
                for i in range(n):
                    st.then(v.max(vals[:, i, 0:8], src[:, i, :]))
                st.settle()
                for i in range(n):
                    st.then(v.max_index(idx[:, i, 0:8], vals[:, i, 0:8], src[:, i, :]))
                    st.then(v.match_replace(scratch[:, i, :], vals[:, i, 0:8], src[:, i, :], -BIG))
                st.settle()
                for i in range(n):
                    st.then(v.max(vals[:, i, 8:16], scratch[:, i, :]))
                st.settle()
                for i in range(n):
                    st.then(v.max_index(idx[:, i, 8:16], vals[:, i, 8:16], scratch[:, i, :]))
                st.settle()

            def route(l, b):
                dve.wait_ge(S("peer_s_taken"), 8 * l + 4 * b + 4)
                top16(sc[:, 0 if l else b, :, :], scr.rearrange("p (i n) -> p i n", i=16), v16, i16, 16)
                vv = v16.rearrange("p (h two) k -> p h two k", two=2)
                cv = cand.rearrange("p h (i j) -> p h i j", i=TOPK)
                go(v.tensor_copy(i16f, i16.rearrange("p (h two) k -> p h two k", two=2)))
                for h in range(EH):
                    st.then(tt(cv[:, h], vv[:, h, 0, :].unsqueeze(2).to_broadcast([P, TOPK, TOPK]),
                               vv[:, h, 1, :].unsqueeze(1).to_broadcast([P, TOPK, TOPK]), ALU.add))
                st.settle()
                top16(cand, scr.rearrange("p (h n) -> p h n", h=EH), csc, pos, EH)
                pf = pos.rearrange("p h k -> p (h k)")
                st.then(ts(hilo_u[:, 0, :], pf, 4, None, ALU.logical_shift_right))
                go(ts(hilo_u[:, 1, :], pf, 15, None, ALU.bitwise_and))
                go(v.tensor_copy(hilo.rearrange("p w h k -> p w (h k)"), hilo_u))
                for w in range(2):
                    for h in range(EH):
                        st.then(tt(onehot[:, h], hilo[:, w, h, :].unsqueeze(2).to_broadcast([P, TOPK, TOPK]),
                                   iota16[:].unsqueeze(1).to_broadcast([P, TOPK, TOPK]), ALU.is_equal))
                    st.settle()
                    for h in range(EH):
                        st.then(tt(onehot[:, h], onehot[:, h], i16f[:, h, w, :].unsqueeze(1).to_broadcast([P, TOPK, TOPK]),
                                   ALU.mult))
                    st.settle()
                    go(v.tensor_reduce(e12[:, w].rearrange("p h k -> p (h k)"), onehot.rearrange("p h k j -> p (h k) j"),
                                       AX_X, ALU.add))
                ef = e12.rearrange("p w h k -> p w (h k)")
                go(stt(eidf, ef[:, 0, :], float(NK), ef[:, 1, :], ALU.mult, ALU.add))
                v.tensor_copy(eid[:, b, :], eidf).then_inc(S("experts_chosen"), 1)
                g = gate[:, b, :].rearrange("p (h k) -> p h k", h=EH)
                tt(g, csc, csc[:, :, 0:1].to_broadcast([P, EH, TOPK]), ALU.subtract).then_inc(S("gate_shifted"), 1)

            def weigh(l, b):
                g = gate[:, b, :].rearrange("p (h k) -> p h k", h=EH)
                dve.wait_ge(S("gate_exp"), 2 * l + b + 1)
                go(v.tensor_reduce(gsum[:, 0:EH], g, AX_X, ALU.add))
                go(v.reciprocal(gsum[:, EH:2 * EH], gsum[:, 0:EH]))
                go(tt(g, g, gsum[:, EH:2 * EH].unsqueeze(2).to_broadcast([P, EH, TOPK]), ALU.mult))
                dve.wait_ge(S("gelued"), 2 * l + b + 1)
                tt(ga[:, b, :], ga[:, b, :], gate[:, b, :], ALU.mult).then_inc(S("weights"), 1)

            def scale_x(l, b):
                for x in halves(b):
                    ts(x, x, ALPHA, None, ALU.mult).then_inc(S("sum_steps"), 1)

            def add_rows(l, b):
                n = 2 * l + b
                base = (2 + 2 * DVE_ROWS) * n
                with dve.Fori(0, DVE_ROWS // RING) as i:
                    for j in range(RING):
                        dve.wait_ge(S(f"v_row{j}"), i * 16 + 16 * (SLOTS // RING * n + PE_ROWS // RING + 1))
                        for c, x in enumerate(halves(b)):
                            dve.wait_ge(S("sum_steps"), i * (2 * RING) + (base + 2 * j + c + 1))
                            stt(x, ring_v[:, j, c * 512:(c + 1) * 512], ga[:, b, bass.ds(i * RING + (PE_ROWS + j), 1)], x,
                                ALU.mult, ALU.add).then_inc(S("sum_steps"), 1)
                dve.wait_ge(S("v_rows_done"), PE_ROWS * (n + 1) + RING)
                dve.wait_ge(S("sum_steps"), base + 2 + 2 * DVE_ROWS)
                for c, x in enumerate(halves(b)):
                    taken(tt(x, x, bank("experts", 2 * n + c), ALU.add), "experts")
                dve.wait_ge(S("experts_taken"), 2 * n + 2)

            kept = [0]

            def dots(l, b):
                n, k0 = 2 * l + b, kept[0]
                kept[0] += SLOTS // RING
                with dve.Fori(0, SLOTS // UNROLL) as i:
                    for k in range(UNROLL // RING):
                        dve.wait_ge(S("dots_kept"), i * (UNROLL // RING) + (k0 + k + 1))
                        for j in range(RING):
                            dve.wait_ge(S(f"u_row{j}"), i * (16 * UNROLL // RING) + 16 * (SLOTS // RING * n + k + 1))
                            v.tensor_tensor_reduce(out=ring_u[:, j, :], in0=ring_u[:, j, :], in1=xres[:, b, :], scale=1.0,
                                                   scalar=0.0, op0=ALU.mult, op1=ALU.add, accum_out=hstage[:, k, j:j + 1]
                                                   ).then_inc(S("u_rows_done"), 1)
                        dve.wait_ge(S("u_rows_done"), i * UNROLL + (SLOTS * n + RING * (k + 1) + RING))
                        v.tensor_copy(hid[:, b, bass.ds(i * UNROLL + RING * k, RING)], hstage[:, k, :]
                                      ).then_inc(S("dots_kept"), 1)
                dve.wait_ge(S("dots_kept"), kept[0] + 2)
                dve.sem_inc(S("hidden"), 1)

            class Dots:

                def __init__(self, l, b):
                    self.n, self.b, self.s = 2 * l + b, b, 0

                def rows(self, count):
                    for s in range(self.s, min(self.s + count, SLOTS)):
                        j = s % RING
                        dve.wait_ge(S(f"u_row{j}"), 16 * (SLOTS // RING * self.n + s // RING + 1))
                        v.tensor_tensor_reduce(out=ring_u[:, j, :], in0=ring_u[:, j, :], in1=xres[:, self.b, :], scale=1.0,
                                               scalar=0.0, op0=ALU.mult, op1=ALU.add, accum_out=hid[:, self.b, s:s + 1]
                                               ).then_inc(S("u_rows_done"), 1)
                    self.s = min(self.s + count, SLOTS)

                def finish(self):
                    self.rows(SLOTS)
                    dve.wait_ge(S("u_rows_done"), SLOTS * (self.n + 1) + RING)
                    dve.sem_inc(S("hidden"), 1)

            def mixer1(b, dot):
                v.memset(fw, 0.0).then_inc(S("f_zeroed"), 1)
                dot.rows(40)
                for i in range(4):
                    dve.wait_ge(S("fox_qk_taken"), 4 * b + i + 1)
                    src = qc[:, 4 * i:4 * i + 4, :] if i < 2 else kc[:, 4 * i - 8:4 * i - 4, b * P:(b + 1) * P]
                    tt(SQ[:, 4 * i:4 * i + 4, :], src, src, ALU.mult).then_inc(S("squares"), 1)
                dot.rows(20)
                dve.wait_ge(S("fox_f_taken"), b + 1)
                log_sigmoid(fz, fl, fz, "f_abs", "f_log", b + 1)
                c = fc[:, b * P:(b + 1) * P]
                go(v.tensor_tensor_scan(c, ones[:, 0:P], fz, fc[:, P - 1:P] if b else 0.0, ALU.mult, ALU.add))
                ts(fneg[:, b * P:(b + 1) * P], c, -1.0, None, ALU.mult).then_inc(S("decay_rows"), 1)
                dve.wait_ge(S("fox_rms_taken"), 4 * b + 4)
                for i in range(4):
                    st.then(v.reciprocal(RS[:, 4 * i:4 * i + 4, :], RS[:, 4 * i:4 * i + 4, :]))
                st.settle()
                for t in range(16):
                    gain = par("qn_g", t) if t < 8 else kn8[:, t - 8:t - 7]
                    x = qc[:, t, :] if t < 8 else kc[:, t - 8, b * P:(b + 1) * P]
                    ins = stt(x, x, gain, RS[:, t, :], ALU.mult, ALU.mult)
                    if t < 15:
                        st.then(ins)
                ins.then_inc(S("qk_normed"), 1)
                dot.rows(4)
                w = P * (b + 1)
                for s in range(FH + 4):
                    if s < FH:
                        u = FH * b + s
                        ps = full(dve, "att", u)[:, 0:w]
                        if s >= 4:
                            dve.wait_ge(S("exped"), u - 3)
                        taken(v.tensor_tensor_reduce(out=lg[:, u % 4, 0:w], in0=ps, in1=causal_ts[:, SEQ + P - w:SEQ + P],
                                                     scale=1.0, scalar=-BIG, op0=ALU.add, op1=ALU.max,
                                                     accum_out=arec[:, u:u + 1]), "att")
                        dve.wait_ge(S("att_taken"), u + 1)
                        ts(amax[:, u:u + 1], arec[:, u:u + 1], -1.0, None, ALU.mult).then_inc(S("logits_max"), 1)
                    if 1 <= s < FH + 1:
                        u = FH * b + s - 1
                        dve.wait_ge(S("exped"), u + 1)
                        dve.wait_ge(S("logits_max"), u + 1)
                        go(v.reciprocal(arec[:, u:u + 1], asum[:, u:u + 1]))
                        ts(prob[:, u % 4, 0:w], prob[:, u % 4, 0:w], arec[:, u:u + 1], None, ALU.mult).then_inc(S("probs_ready"), 1)
                    if s >= 4 and s % 2 == 0:
                        i = (FH * b + s - 4) // 2
                        t = i % 8
                        taken(tt(oT[:, t, :], full(dve, "att_out", i)[:, 0:P], ogT[:, t, :], ALU.mult), "att_out")
                    dot.rows(2)
                dve.wait_ge(S("att_out_taken"), 8 * b + 8)
                dve.sem_inc(S("mixed"), 1)
                dot.rows(8)
                for i in range(2):
                    x = xres[:, b, i * 512:(i + 1) * 512]
                    taken(stt(x, x, ALPHA, full(dve, "mix_out", 4 + 2 * b + i), ALU.mult, ALU.add), "mix_out")
                dve.wait_ge(S("mix_out_taken"), 6 + 2 * b)
                layer_norm(3 + 2 * b)
                dot.finish()

            dve.sem_inc(S("u_rows_done"), RING)
            dve.sem_inc(S("dots_kept"), 2)
            mixer0()
            route(0, 0)
            dots(0, 0)
            weigh(0, 0)
            scale_x(0, 0)
            route(0, 1)
            add_rows(0, 0)
            layer_norm(2)
            mixer1(0, Dots(0, 1))
            weigh(0, 1)
            scale_x(0, 1)
            route(1, 0)
            add_rows(0, 1)
            layer_norm(4)
            mixer1(1, Dots(1, 0))
            weigh(1, 0)
            scale_x(1, 0)
            route(1, 1)
            add_rows(1, 0)
            layer_norm(6)
            dots(1, 1)
            weigh(1, 1)
            scale_x(1, 1)
            add_rows(1, 1)
            layer_norm(7)


def kernel(**inputs):
    import numpy as _np
    import concourse.bacc as _bacc
    from concourse.bass_utils import run_bass_kernel_spmd as _run

    nc = _bacc.Bacc("TRN2", target_bir_lowering=False, num_devices=1)
    arrays, T = {}, {}
    for name, value in inputs.items():
        a = _np.ascontiguousarray(value)
        arrays[name] = a
        T[name] = nc.dram_tensor(name, a.shape, mybir.dt.from_np(a.dtype), kind="ExternalInput").ap()
    out = nc.dram_tensor("out", (1, SEQ, D), F32, kind="ExternalOutput").ap()
    build(nc, T, out)
    r = _run(nc, [arrays], core_ids=[0])
    return r.results[0]["out"]
```

```python
from contextlib import ExitStack

import concourse.bass as bass
from concourse import mybir

F32 = mybir.dt.float32
U32 = mybir.dt.uint32
ALU = mybir.AluOpType
ACT = mybir.ActivationFunctionType
AX_X = mybir.AxisListType.X

P = 128
D = 1024
SEQ = 256
NB = SEQ // P
KT = D // P
ALPHA = 4.0 ** 0.25
LN_EPS = 1e-5

RW = 512
RH, RN = 8, 64
RT = RW // P
CH = 64
NCH = SEQ // CH
RWKV_COLS = 3 * RW + 64 + 64 + 128
MW = 512
MH, MN = 4, 128
LEVELS = [2, 4, 8, 16, 32]

FH, FN = 16, 64

EH = 8
NK = 128
TOPK = 16
SLOTS = EH * TOPK
GROUPS = 4
PAIRS = tuple((2 * g, 2 * g + 2) for g in range(GROUPS))
FIRST_GROUPS = ((0, 1), (1, 2)) + PAIRS[1:]
FIRST_DOTS = (0, 1, 2, 3, 3)
RING = 8
UNROLL = 16
DIAGS = 4
HALF_RING = RING // 2
HALF_ROWS = SLOTS // 2

DOT_ROWS = (40, 30, 4, 3)
ROUTE_ROWS = 1
EARLY_ROWS = 4
NORM_ROWS = 6
TAIL_ROWS = 4
STRIP = 256
WRING = 3
BIG = 3.0e38


def unit_heads():
    return [(b, 2 * q + odd) for b in range(NB) for odd in range(2) for q in range(RH // 2)]


UNITS = unit_heads()
UNIT = {bh: u for u, bh in enumerate(UNITS)}


def parameter_rows():
    rows, at = {}, 0
    for name, n in (("mu", RWKV_COLS // P), ("w0", RT), ("a0", RT), ("k_k", RT), ("k_a", RT), ("r_k", RT),
                    ("ln_g", RT), ("ln_b", RT), ("conv_w", 4 * 8), ("conv_b", 8), ("hn_g", MH), ("hn_b", MH),
                    ("qn_g", 8), ("kn_g", 8)):
        rows[name] = (at, n)
        at += n
    return rows, at


def attention_plan(b):
    order = []
    for s in range(FH + 3):
        if s < FH:
            order.append(("att", FH * b + s))
        if 2 <= s < FH + 2:
            order.append(("att_turn", FH * b + s - 2))
        if s >= 3 and (s - 3) % 2:
            order.append(("att_out", (FH * b + s - 3) // 2))
    return order


NORMS = [(0, 0), (0, 1), (1, 0), (2, 0), (1, 1), (2, 1), (3, 0), (3, 1)]
NORM_LOADS = [sum(NORMS[i][0] != NORMS[i - 1][0] for i in range(1, e + 1)) + 1 for e in range(len(NORMS))]


def bank_plan():
    plan = [("x_turn", 4), ("params", 1), ("rwkv_in", 14), ("lora_w", 2), ("lora_a", 2), ("lora_g", 2), ("kk_norm", 2),
            ("conv_in", 8), ("bonus", 2), ("token_turn", 6), ("scores", 16), ("ab", 4), ("gates_in", 1), ("vo_in", 4)]
    for m in LEVELS:
        plan.append(("inv_t", 4))
        plan.append(("inv_d", 4))
    plan += [("mrow_turn", 1), ("mv_turn", 2), ("mx_row", 2), ("qk", 4)]
    for c in range(NCH):
        plan += [("y_turn", NB)] * (c == NCH - 1)
        plan += [("seq_x", 1), ("seq_u", 1)] + ([("seq_s", 1)] if c < NCH - 1 else []) + [("seq_y", 1)]
        if c < NB:
            plan.append(("hnum", 2))
    plan += [("y_turn", NB), ("mix_out", 4)]
    plan += [("x_turn", 2), ("peer_q", 1), ("x_turn", 2), ("key_turn", 4), ("peer_s", 1), ("peer_q", 2), ("peer_s", 1)]
    for h in range(1, EH):
        plan += [("peer_q", 1)] * (h < EH - 1) + [("peer_s", 1)]
    plan.append(("experts", 2))
    for b in range(NB):
        if b == 0:
            plan.append(("key_turn", 4))
        plan += [("x_turn", 2), ("fox_qk", 4), ("fox_v", 2), ("fox_og", 2), ("fox_f", 1), ("fox_rms", 4)]
        plan += [(name, 1) for name, _ in attention_plan(b)]
        plan += [("mix_out", 2), ("x_turn", 2)] + [("peer_q", 1), ("peer_s", 1)] * GROUPS + [("experts", 2)]
    plan += [("experts", 2)]
    return plan


def build(nc, T, out):
    ROWS, NROWS = parameter_rows()
    ctx = ExitStack()
    with ctx:
        def sb(name, shape, dt=F32):
            return ctx.enter_context(nc.sbuf_tensor(name, shape, dt))

        sems = {}

        def S(name):
            if name not in sems:
                sems[name] = ctx.enter_context(nc.semaphore(name))
            return sems[name]

        psum = ctx.enter_context(nc.psum_tensor("psum", [P, 8, 512], F32))
        order, ticket, seen, fills = [], {}, {}, {}
        for name, n in bank_plan():
            for _ in range(n):
                k = seen.get(name, 0)
                seen[name] = k + 1
                ticket[(name, k)] = len(order)
                fills[(name, k)] = max(fills.values(), default=0) + (name != "experts")
                order.append((name, k))

        bank_of, former, holder = {}, {}, {}
        turn, shared = 0, 8
        for name, k in order:
            if name == "experts":
                shared, at = 6, 6 + k % 2
            else:
                at = turn % shared
                turn += 1
            bank_of[(name, k)] = at
            former[(name, k)] = holder.get(at)
            holder[at] = (name, k)

        def bank(name, k):
            return psum[:, bank_of[(name, k)], :]

        def claim(pe, name, k):
            if former[(name, k)]:
                before, i = former[(name, k)]
                pe.wait_ge(S(before + "_taken"), i + 1)
            return bank(name, k)

        def await_filled(eng, name, k):
            eng.wait_ge(S("banks_filled"), fills[(name, k)])

        def full(eng, name, k):
            await_filled(eng, name, k)
            return bank(name, k)

        ident = sb("ident", [P, P])
        pair_ones = sb("pair_ones", [P, P])
        ones = sb("ones", [P, SEQ])
        score_mask = sb("score_mask", [P, 2, P])
        level_mask = sb("level_mask", [P, 6, P])
        level_one = sb("level_one", [P, P])
        causal_st = sb("causal_st", [P, 3 * P])
        causal_ts = sb("causal_ts", [P, SEQ + P])
        iota16 = sb("iota16", [P, TOPK])
        pars = sb("pars", [P, P])
        one_mu = sb("one_mu", [P, RWKV_COLS // P])
        kn8 = sb("kn8", [P, 8])
        small = sb("small", [P, 4])
        cexp = sb("cexp", [P, 6])

        def par(name, i=0):
            at, n = ROWS[name]
            return pars[:, at + i:at + i + 1]

        xres = sb("xres", [P, NB, D])
        xT = sb("xT", [P, KT, SEQ])
        ln_par = sb("ln_par", [P, 2, D])
        lnst = sb("lnst", [P, NB, 12])
        lnmv = sb("lnmv", [P, NB, 2])
        lnrs = sb("lnrs", [P, NB])
        wring = sb("wring", [P, WRING, KT, STRIP])
        ARENA = 36352
        A = sb("arena", [P, ARENA])

        def cut(at, n):
            assert at + n <= ARENA, (at, n)
            return A[:, at:at + n]

        strips = []

        def add_strips(w, c0, c1, name, first, per):
            for i, c in enumerate(range(c0, c1, STRIP)):
                strips.append((T[w][:, c:min(c + STRIP, c1)].rearrange("(k p) n -> p k n", p=P),
                               min(STRIP, c1 - c), name, first + (int(i * per) if per < 1 else (i + 1) * per - 1)))

        M0 = RWKV_COLS
        add_strips("l0_w_in", 0, M0, "rwkv_in", 0, 2)
        add_strips("l0_w_in", M0, M0 + 2 * MW, "conv_in", 0, 2)
        add_strips("l0_w_in", M0 + 4 * MW, M0 + 4 * MW + 2 * MH, "gates_in", 0, 1)
        add_strips("l0_w_in", M0 + 2 * MW, M0 + 4 * MW, "vo_in", 0, 1)
        add_strips("l0_w_out", 0, D, "mix_out", 0, 1)
        add_strips("l0_peer_wq", 0, 2048, "peer_q", 1, 1)
        strips_before_f = []
        for b in range(NB):
            add_strips("l1_w_in", 0, 2 * D, "fox_qk", 4 * b, 0.5)
            add_strips("l1_w_in", 2 * D, 3 * D, "fox_v", 2 * b, 0.5)
            add_strips("l1_w_in", 3 * D, 4 * D, "fox_og", 2 * b, 0.5)
            strips_before_f.append(len(strips))
            add_strips("l1_w_in", 4 * D, 4 * D + FH, "fox_f", b, 1)
            add_strips("l1_w_out", 0, D, "mix_out", 4 + 2 * b, 0.5)
            add_strips("l1_peer_wq", 0, 2048, "peer_q", EH + 1 + 4 * b, 0.5)

        strip_at = [0]

        def next_strip(pe):
            n = strip_at[0]
            strip_at[0] += 1
            pe.wait_ge(S(f"strip_loaded{n % WRING}"), 16 * (n // WRING + 1))
            return wring[:, n % WRING]

        prows = cut(24064, P)
        R = cut(0, 14 * SEQ)
        r_all, k_all, v_all = cut(0, 1024), cut(1024, 1024), cut(2048, 1024)
        xwa, xg = cut(3072, SEQ), cut(3328, SEQ)
        waup, gup = cut(3584, RW), cut(4096, RW)
        mq_all, mk_all, mv_all, mo_all = (cut(4608 + 1024 * i, 1024) for i in range(4))
        AR = cut(8704, 2048).rearrange("p (t b two n) -> p t b two n", t=RT, b=NB, two=2)
        beta_all, kappa_all, g_all, bonus_all = (cut(10752 + 1024 * i, 1024) for i in range(4))
        v_tok = cut(14848, 1024).rearrange("p (b c) -> p b c", b=NB)
        beta_tok = cut(0, 1024).rearrange("p (b c) -> p b c", b=NB)
        kappa_tok = cut(1024, 1024).rearrange("p (b c) -> p b c", b=NB)
        y_tok = cut(2048, 1024)
        SC = cut(15872, 8192).rearrange("p (u f n) -> p u f n", u=16, f=4)
        a_all, logw, cumw, pinv, pprev, pfull, kk_all, tmp = (cut(24064 + 1024 * i, 1024) for i in range(8))
        DT, Tm, LM = (cut(26112 + 2048 * i, 2048).rearrange("p (u n) -> p u n", u=16) for i in range(3))
        DC = cut(24064, 2048).rearrange("p (two u n) -> p two u n", two=2, u=16)
        Tc = cut(34848, 1024).rearrange("p (u n) -> p u n", u=16)
        vaug = cut(32256, NB * MH * 132).rearrange("p (b h n) -> p b h n", b=NB, h=MH)
        scT = cut(33312, MH * 384).rearrange("p (h n) -> p h n", h=MH)
        seq_x, seq_u = cut(34848, RW), cut(35360, RW)
        conv_sig = lambda t: cut(33312 + 1024 * t, 1024)
        states = [cut(at, RT * RN).rearrange("p (t n) -> p t n", t=RT) for at in (35872, 30208)]
        h_tok = mq_all
        yT = cut(28160, 2048).rearrange("p (k n) -> p k n", k=KT)
        mr = sb("mrows", [P, 6, SEQ])
        pend = sb("pend", [P, RT, NCH])
        gcol = sb("gcol", [P, 4 * MH])
        stat = sb("stat", [P, 4, 16])
        dcol = sb("dcol", [P, 8])

        ring_u = cut(0, RING * D).rearrange("p (j n) -> p j n", j=RING)
        ring_v = cut(8192, RING * D).rearrange("p (j n) -> p j n", j=RING)
        keyT = cut(16384, 2048).rearrange("p (i n) -> p i n", i=16)
        keys = cut(18432, 2048).rearrange("p (i n) -> p i n", i=16)
        cand = cut(18432, 2048).rearrange("p (h n) -> p h n", h=EH)
        qT = cut(20480, 4096).rearrange("p (i n) -> p i n", i=16)
        sc = cut(24576, 4096).rearrange("p (b i n) -> p b i n", b=NB, i=16)
        scr = cut(28672, 2048)
        onehot = cut(30720, 2048).rearrange("p (h k j) -> p h k j", h=EH, k=TOPK)
        v16 = cut(32768, 256).rearrange("p (i k) -> p i k", i=16)
        i16f = cut(33024, 256).rearrange("p (h two k) -> p h two k", h=EH, two=2)
        csc = cut(33280, SLOTS).rearrange("p (h k) -> p h k", h=EH)
        hilo = cut(33408, 2 * SLOTS).rearrange("p (w h k) -> p w h k", w=2, h=EH)
        e12 = cut(33664, 2 * SLOTS).rearrange("p (w h k) -> p w h k", w=2, h=EH)
        eidf = cut(33920, SLOTS)
        gate = cut(34048, NB * SLOTS).rearrange("p (b s) -> p b s", b=NB)
        hid = cut(34304, NB * SLOTS).rearrange("p (b s) -> p b s", b=NB)
        ga = cut(34560, NB * SLOTS).rearrange("p (b s) -> p b s", b=NB)
        diag = cut(34816, DIAGS * P).rearrange("p (j n) -> p j n", j=DIAGS)
        gsum = cut(35328, 2 * EH)
        qT1 = cut(20480, 2048).rearrange("p (i n) -> p i n", i=16)
        hstage = cut(35344, 2 * RING).rearrange("p (k j) -> p k j", k=2)
        gstage = cut(35360, 2 * RING).rearrange("p (k j) -> p k j", k=2)
        uints = cut(35376, 944).bitcast(U32)
        i16 = uints[:, 0:256].rearrange("p (i k) -> p i k", k=TOPK)
        pos = uints[:, 256:384].rearrange("p (h k) -> p h k", k=TOPK)
        hilo_u = uints[:, 384:640].rearrange("p (w s) -> p w s", w=2)
        eid = uints[:, 640:896].rearrange("p (b s) -> p b s", b=NB)
        ustage = uints[:, 896:912].rearrange("p (k j) -> p k j", k=2)
        vstage = uints[:, 912:928].rearrange("p (k j) -> p k j", k=2)

        kc = cut(22528, 2048).rearrange("p (t n) -> p t n", t=8)
        fv = cut(26624, 2048).rearrange("p (b n) -> p b n", b=NB)
        qc = cut(25600, 1024).rearrange("p (t n) -> p t n", t=8)
        fw = cut(24576, KT * P).rearrange("p (k n) -> p k n", k=KT)
        SQ = cut(28672, 2048).rearrange("p (t n) -> p t n", t=16)
        RS = cut(30720, 2048).rearrange("p (t n) -> p t n", t=16)
        lg = cut(28672, 4 * SEQ).rearrange("p (j n) -> p j n", j=4)
        prob = cut(29696, 4 * SEQ).rearrange("p (j n) -> p j n", j=4)
        probT = cut(30720, 4 * SEQ).rearrange("p (j s n) -> p j s n", j=4, s=2)
        ogT = cut(18432, 1024).rearrange("p (t n) -> p t n", t=KT)
        oT = cut(19456, 1024).rearrange("p (t n) -> p t n", t=KT)
        fz, fl, fc, fneg = mr[:, 0, 0:P], mr[:, 0, P:SEQ], mr[:, 1, :], mr[:, 2, :]
        amax, asum, arec = mr[:, 3, 0:32], mr[:, 3, 32:64], mr[:, 3, 64:96]

        class Steps:

            def __init__(self, eng, name):
                self.eng, self.sem, self.n = eng, S(name), 0

            def then(self, ins):
                ins.then_inc(self.sem, 1)
                self.n += 1

            def settle(self):
                self.eng.wait_ge(self.sem, self.n)

        block = ctx.enter_context(nc.Block())
        R2 = lambda ap: ap.rearrange("(r c) -> r c", c=P)

        @block.sync
        def _(sp):
            used = [0]

            def load_strips(n):
                for _ in range(n):
                    i = used[0]
                    used[0] += 1
                    src, w, _, _ = strips[i]
                    if i >= WRING:
                        await_filled(sp, strips[i - WRING][2], strips[i - WRING][3])
                    sp.dma_start(wring[:, i % WRING, :, 0:w], src).then_inc(S(f"strip_loaded{i % WRING}"), 16)

            sp.dma_start(xres[:], T["x"].rearrange("o (b p) d -> p (o b) d", p=P)).then_inc(S("x_loaded"), 16)
            load_strips(2)
            srcs = [("mu", T["l0_rwkv_mu"]), ("w0", T["l0_rwkv_w0"]), ("a0", T["l0_rwkv_a0"]), ("k_k", T["l0_rwkv_k_k"]),
                    ("k_a", T["l0_rwkv_k_a"])]
            for name, src in srcs:
                at, n = ROWS[name]
                sp.dma_start(prows[at:at + n, :], R2(src)).then_inc(S("params_loaded"), 16)
            for name, src in (("r_k", "l0_rwkv_r_k"), ("ln_g", "l0_rwkv_ln_g"), ("ln_b", "l0_rwkv_ln_b"),
                              ("qn_g", "l1_fox_qn_g"), ("kn_g", "l1_fox_kn_g")):
                at, n = ROWS[name]
                sp.dma_start(prows[at:at + n, :], T[src].rearrange("(t h) n -> t (h n)", h=2)).then_inc(S("params_loaded"), 16)
            at, n = ROWS["conv_w"]
            sp.dma_start(prows[at:at + n, :], T["l0_mlstm_conv_w"].rearrange("j (t c) -> (j t) c", c=P)).then_inc(S("params_loaded"), 16)
            at, n = ROWS["conv_b"]
            sp.dma_start(prows[at:at + n, :], R2(T["l0_mlstm_conv_b"])).then_inc(S("params_loaded"), 16)
            for name in ("hn_g", "hn_b"):
                at, n = ROWS[name]
                sp.dma_start(prows[at:at + n, :], T["l0_mlstm_" + name]).then_inc(S("params_loaded"), 16)
            sp.wait_ge(S("constants"), 1)
            for i, lo, name, n in ((0, 0, "l0_mlstm_ig_b", MH), (1, 0, "l0_mlstm_fg_b", MH), (2, 0, "l1_fox_f_b", FH),
                                   (2, 64, "l1_fox_f_b", FH)):
                sp.dma_start(small[lo:lo + n, i:i + 1], T[name].rearrange("(h o) -> h o", o=1)).then_inc(S("small_loaded"), 16)
            sp.dma_start(waup[0:64, :], T["l0_rwkv_w_up"]).then_inc(S("ups_loaded"), 16)
            sp.dma_start(waup[64:128, :], T["l0_rwkv_a_up"]).then_inc(S("ups_loaded"), 16)
            sp.dma_start(gup, T["l0_rwkv_g_up"]).then_inc(S("ups_loaded"), 16)

            def load_ln(e):
                name = ("l0_ln1", "l0_ln2", "l1_ln1", "l1_ln2")[NORMS[e][0]]
                if e:
                    sp.wait_ge(S("x_normed"), e)
                sp.dma_start(ln_par[:, 0, :], T[name + "_g"].partition_broadcast(P)).then_inc(S("ln_loaded"), 16)
                sp.dma_start(ln_par[:, 1, :], T[name + "_b"].partition_broadcast(P)).then_inc(S("ln_loaded"), 16)

            def load_keys(l):
                for half in range(2):
                    sp.dma_start(keys[:, half * EH:half * EH + EH, :],
                                 T[f"l{l}_peer_k{half + 1}"].rearrange("h n d -> n h d")).then_inc(S("keys_loaded"), 16)

            load_ln(0)
            load_strips(16 - 2 + 4 + 2)
            sp.wait_ge(S("x_normed"), 1)
            load_keys(0)
            load_ln(2)
            load_strips(8 - 2)
            sp.wait_ge(S("experts_chosen"), NB * EH)
            load_keys(1)
            for b in range(NB):
                load_strips(17)
                load_ln(3 + 2 * b)
                load_strips(4 + 8)
                load_ln(4 + 2 * b)
            for b in range(NB):
                sp.wait_ge(S("x_normed"), 7 + b)
                sp.dma_start(out[0, b * P:(b + 1) * P, :], xres[:, b, :]).then_inc(S("stored"), 16)
            sp.wait_ge(S("stored"), 16 * NB)

        @block.gpsimd
        def _(pool):
            st = Steps(pool, "pool_step")
            st.then(pool.memset(ident[:], 1.0))
            st.settle()
            pool.affine_select(out=ident[:], in_=ident[:], compare_op=ALU.is_equal, fill=0.0, base=0, pattern=[[1, P]],
                               channel_multiplier=-1).then_inc(S("ident_ready"), 1)
            for t, v in ((pair_ones, 1.0), (ones, 1.0), (score_mask, 1.0),
                         (level_mask, 1.0), (level_one, 1.0), (small, 0.0), (causal_st, 1.0), (causal_ts, 0.0), (cexp, 1.0)):
                st.then(pool.memset(t[:], v))
            st.then(pool.memset(vaug, 1.0))
            st.settle()
            for i, eps in enumerate((LN_EPS, 1e-5 * RN, FN * 1e-6)):
                st.then(pool.memset(cexp[:, 2 + i:3 + i], eps))
            st.then(pool.iota(iota16[:], pattern=[[1, TOPK]], base=0, channel_multiplier=0,
                              allow_small_or_imprecise_dtypes=True))
            st.settle()

            def keep(ap, pattern, base, mult, op=ALU.is_ge, fill=0.0):
                st.then(pool.affine_select(out=ap, in_=ap, compare_op=op, fill=fill, base=base, pattern=pattern,
                                           channel_multiplier=mult))

            keep(pair_ones[:, 0:64], [[0, 64]], 63, -1)
            keep(pair_ones[:, 64:128], [[0, 64]], -64, 1)
            for i in range(2):
                keep(score_mask[:, i, :], [[1, P]], -1 if i % 2 == 0 else 0, -1)
            keep(causal_st[:, 0:P], [[1, P]], 0, -1)
            keep(causal_st[:, 2 * P:3 * P], [[1, P]], 0, -1)
            keep(causal_ts[:, SEQ:SEQ + P], [[-1, P]], 0, 1, ALU.is_ge, -1e30)
            keep(cexp[:, 0:1], [[0, 1]], -1000, 1)
            for i, m in enumerate([1] + LEVELS):
                v = level_mask[:, i, :].rearrange("p (g two m) -> p g two m", two=2, m=m)
                st.then(pool.memset(v[:, :, 0, :], 0.0))
            v = level_one[:].rearrange("p (g two) -> p g two", two=2)
            st.then(pool.memset(v[:, :, 1], 0.0))
            st.settle()
            for i in range(2):
                keep(score_mask[:, i, CH:P], [[0, CH]], -CH, 1)
            for i, m in enumerate([1] + LEVELS):
                v = level_mask[:, i, :].rearrange("p (g two m) -> p g two m", two=2, m=m)[:, :, 1, :]
                keep(v, [[-2 * m, P // (2 * m)], [0, m]], 0, 1)
            v = level_one[:].rearrange("p (g two) -> p g two", two=2)[:, :, 0]
            keep(v, [[-2, P // 2]], -1, 1)
            st.settle()
            for i, m in enumerate([1] + LEVELS):
                v = level_mask[:, i, :].rearrange("p (g two m) -> p g two m", two=2, m=m)[:, :, 1, :]
                keep(v, [[2 * m, P // (2 * m)], [0, m]], m - 1, -1)
            v = level_one[:].rearrange("p (g two) -> p g two", two=2)[:, :, 0]
            keep(v, [[2, P // 2]], 1, -1)
            st.settle()
            pool.sem_inc(S("constants"), 1)
            pool.wait_ge(S("scan_operands"), 1)
            pool.memset(Tm, 0.0).then_inc(S("t_zeroed"), 1)

            def gather(tab, ring, stage, j, k, row, free, value):
                pool.wait_ge(free, value)
                pool.sem_inc(S("gathers_issued"), 1)
                pool.indirect_dma_start(out=ring[:, j, :], out_offset=None, in_=tab,
                                        in_offset=bass.IndirectOffsetOnAxis(ap=stage[:, k, j:j + 1], axis=0)
                                        ).then_inc(S(f"{row}{j}"), 16)

            def gathers(b, n, tab, ring, stage, row, per_turn, slot_free, chosen=None):
                with pool.Fori(0, SLOTS // UNROLL) as i:
                    if chosen is not None:
                        pool.wait_ge(S("experts_chosen"), i + (chosen + 1))
                    for k in range(UNROLL // RING):
                        free, value = slot_free(RING * k)
                        pool.wait_ge(free, i * per_turn + value)
                        pool.tensor_copy(stage[:, k, :], eid[:, b, bass.ds(i * UNROLL + RING * k, RING)]
                                         ).then_inc(S("indices_staged"), 1)
                        pool.wait_ge(S("indices_staged"), i * (UNROLL // RING) + (SLOTS // RING * n + k + 1))
                        for j in range(RING):
                            free, value = slot_free(RING * k + j)
                            gather(tab, ring, stage, j, k, row, free, i * per_turn + value)

            def gather_u(l, b):
                n = 2 * l + b
                gathers(b, 2 * n, T[f"l{l}_peer_u"], ring_u, ustage, "u_row", UNROLL,
                        lambda s: (S("u_rows_done"), SLOTS * n + s + 1), chosen=EH * n)

            def gather_v(l, b):
                n = 2 * l + b
                gathers(b, 2 * n + 1, T[f"l{l}_peer_v"], ring_v, vstage, "v_row", UNROLL // 2,
                        lambda s: (S("half_sums1" if s % 2 else "v_rows_done"), HALF_ROWS * n + s // 2 + 1))

            for l in range(2):
                for b in range(NB):
                    gather_u(l, b)
                    gather_v(l, b)

        @block.tensor
        def _(pe):
            mm, tp = nc.tensor.matmul, nc.tensor.transpose

            filled, nth = [0], {}

            def done(ins, name):
                assert fills[(name, nth.get(name, 0))] == filled[0] + 1
                nth[name] = nth.get(name, 0) + 1
                filled[0] += 1
                ins.then_inc(S("banks_filled"), 1)

            def turn_x(first, b):
                for half in range(2):
                    ps = claim(pe, "x_turn", first + half).rearrange("p (k n) -> p k n", k=4)
                    for q in range(4):
                        c = (4 * half + q) * P
                        last = tp(ps[:, q, :], xres[:, b, c:c + P], ident[:])
                    done(last, "x_turn")

            def project(ps, w, c0, cols, tok=slice(0, SEQ)):
                for k in range(KT):
                    last = mm(ps, w[:, k, c0:c0 + cols], xT[:, k, tok], start=(k == 0), stop=(k == KT - 1))
                return last

            def mixer0():
                pe.wait_ge(S("ident_ready"), 1)
                pe.wait_ge(S("x_loaded"), 16)
                for b in range(NB):
                    turn_x(2 * b, b)
                pe.wait_ge(S("params_loaded"), 16 * 14)
                done(tp(claim(pe, "params", 0)[:, 0:NROWS], prows[0:NROWS, :], ident[0:NROWS, 0:NROWS]), "params")
                pe.wait_ge(S("x_turn_taken"), 4)

                def two_tiles_a_strip(name, n):
                    for t in range(n):
                        if t % 2 == 0:
                            w = next_strip(pe)
                        done(project(claim(pe, name, t)[:, 0:SEQ], w, P * (t % 2), P), name)

                two_tiles_a_strip("rwkv_in", 14)
                pe.wait_ge(S("constants"), 1)
                pe.wait_ge(S("ups_loaded"), 48)
                pe.wait_ge(S("lora_squashed"), 1)
                for name, lo, hi, up, low in (("lora_w", 0, 64, waup, xwa), ("lora_a", 64, 128, waup, xwa),
                                              ("lora_g", 0, 128, gup, xg)):
                    for half in range(2):
                        ps = claim(pe, name, half)
                        for q in range(2):
                            t = 2 * half + q
                            last = mm(ps[:, q * SEQ:(q + 1) * SEQ], up[lo:hi, t * P:(t + 1) * P], low[lo:hi, :],
                                      start=True, stop=True)
                        done(last, name)
                def head_sums(name, ready):
                    pe.wait_ge(S("head_products"), ready)
                    for half in range(2):
                        done(mm(claim(pe, name, half), pair_ones[:], tmp[:, half * 512:(half + 1) * 512],
                                start=True, stop=True), name)

                head_sums("kk_norm", 1)
                two_tiles_a_strip("conv_in", 8)
                head_sums("bonus", 2)
                pe.wait_ge(S("scan_operands"), 1)
                for i, src in enumerate((v_all, beta_all, kappa_all)):
                    for b in range(NB):
                        ps = claim(pe, "token_turn", NB * i + b).rearrange("p (t n) -> p t n", t=RT)
                        for t in range(RT):
                            last = tp(ps[:, t, :], src[:, t * SEQ + b * P:t * SEQ + (b + 1) * P], ident[:])
                        done(last, "token_turn")
                for u in range(16):
                    b, h = UNITS[u]
                    t, lo = h // 2, 64 * (h % 2)
                    ps = claim(pe, "scores", u)
                    ar = AR[lo:lo + 64, t, b, :, :].rearrange("p two n -> p (two n)")
                    c = t * SEQ + b * P
                    mm(ps[:, 0:256], beta_all[lo:lo + 64, c:c + P], ar, start=True, stop=True)
                    done(mm(ps[:, 256:512], kappa_all[lo:lo + 64, c:c + P], ar, start=True, stop=True), "scores")
                for g in range(4):
                    ps = claim(pe, "ab", g).rearrange("p (u n) -> p u n", u=4)
                    for q in range(4):
                        u = 4 * g + q
                        b, h = UNITS[u]
                        t, lo = h // 2, 64 * (h % 2)
                        c = t * SEQ + b * P
                        last = mm(ps[:, q, :], AR[lo:lo + 64, t, b, 0, :], beta_all[lo:lo + 64, c:c + P],
                                  start=True, stop=True)
                    done(last, "ab")
                w = next_strip(pe)
                ps = claim(pe, "gates_in", 0)
                project(ps[0:MH, 0:SEQ], w, 0, MH)
                done(project(ps[0:MH, SEQ:2 * SEQ], w, MH, MH), "gates_in")
                for t in range(4):
                    w = next_strip(pe)
                    ps = claim(pe, "vo_in", t)
                    for q in range(2):
                        last = project(ps[:, q * SEQ:(q + 1) * SEQ], w, P * q, P)
                    done(last, "vo_in")
                for i, m in enumerate(LEVELS):
                    last_level = m == LEVELS[-1]
                    for g in range(4):
                        pe.wait_ge(S("merge_ready"), 4 * i + g + 1)
                        ps = claim(pe, "inv_t", 4 * i + g)[:, 0:4 * CH].rearrange("p (u n) -> p u n", u=4)
                        for q in range(4):
                            last = mm(ps[:, q, :], LM[:, 4 * g + q, :], DC[:, 0, 4 * g + q, :], start=True, stop=True)
                        done(last, "inv_t")
                    for g in range(4):
                        pe.wait_ge(S("inv_t_taken"), 4 * i + g + 1)
                        pe.wait_ge(S("d_copied"), 4 * (i - 1) + g + 3 if i else 2)
                        ps = claim(pe, "inv_d", 4 * i + g).rearrange("p (two u n) -> p two u n", two=2, u=4)
                        for q in range(4):
                            u = 4 * g + q
                            if not last_level:
                                mm(ps[:, 0, q, :], DT[:, u, :], Tc[:, u, :], start=True, stop=True)
                            last = mm(ps[:, 1, q, :], Tm[:, u, :], DC[:, 1, u, :], start=True, stop=True)
                        done(last, "inv_d")

                pe.wait_ge(S("m_rows"), 1)
                ps = claim(pe, "mrow_turn", 0)
                for i, row in enumerate((2, 5)):
                    for b in range(NB):
                        c = (2 * i + b) * MH
                        last = tp(ps[:, c:c + MH], mr[0:MH, row, b * P:(b + 1) * P], ident[0:MH, 0:MH])
                done(last, "mrow_turn")
                for b in range(NB):
                    ps = claim(pe, "mv_turn", b).rearrange("p (h n) -> p h n", h=MH)
                    for h in range(MH):
                        last = tp(ps[:, h, :], mv_all[:, h * SEQ + b * P:h * SEQ + (b + 1) * P], ident[:])
                    done(last, "mv_turn")
                for i in range(2):
                    ps = claim(pe, "mx_row", i)
                    for q in range(2):
                        h = 2 * i + q
                        last = mm(ps[:, q * SEQ:(q + 1) * SEQ], ident[0:MH, h:h + 1].to_broadcast([MH, P]),
                                  mr[0:MH, 4, :], start=True, stop=True)
                    done(last, "mx_row")
                for h in range(MH):
                    ps = claim(pe, "qk", h)
                    q, k = mq_all[:, h * SEQ:(h + 1) * SEQ], mk_all[:, h * SEQ:(h + 1) * SEQ]
                    mm(ps[:, 0:SEQ], k[:, 0:P], q, start=True, stop=True)
                    done(mm(ps[:, SEQ:SEQ + P], k[:, P:SEQ], q[:, P:SEQ], start=True, stop=True), "qk")
                def values(b):
                    for i in range(2):
                        pe.wait_ge(S("qk_taken"), 2 * i + 2)
                        ps = claim(pe, "hnum", 2 * b + i).rearrange("p (q n) -> p q n", q=2)
                        for q in range(2):
                            h = 2 * i + q
                            for s in range(b + 1):
                                c = b * P if s == 0 else SEQ
                                last = mm(ps[:, q, 0:MN + 1], scT[:, h, c:c + P], vaug[:, s, h, 0:MN + 1],
                                          start=(s == 0), stop=(s == b))
                        done(last, "hnum")

                def turn_heads(k, src, b, sem, n):
                    pe.wait_ge(S(sem), n)
                    ps = claim(pe, "y_turn", k).rearrange("p (t n) -> p t n", t=RT)
                    for t in range(RT):
                        last = tp(ps[:, t, :], src[:, b * 512 + t * P:b * 512 + (t + 1) * P], ident[:])
                    done(last, "y_turn")

                pe.wait_ge(S("inv_d_taken"), 4 * len(LEVELS))
                for c in range(NCH):
                    b, lo = c // 2, CH * (c % 2)
                    rows = slice(lo, lo + CH)
                    if c == NCH - 1:
                        turn_heads(0, h_tok, 0, "h_normed", 1)
                        turn_heads(1, h_tok, 1, "h_normed", 1)
                    if c:
                        pe.wait_ge(S("state_ready"), c)
                    ps = claim(pe, "seq_x", c)
                    chunk_rows(c, ps, 0, [(2, v_tok[:, b, :])], "seq_x")
                    ps = claim(pe, "seq_u", c)
                    pe.wait_ge(S("seq_x_taken"), c + 1)
                    for h in range(RH):
                        last = mm(ps[rows, h * RN:(h + 1) * RN], DT[rows, UNIT[(b, h)], rows],
                                  seq_x[rows, h * RN:(h + 1) * RN], start=True, stop=True)
                    done(last, "seq_u")
                    pe.wait_ge(S("seq_u_taken"), c + 1)
                    if c < NCH - 1:
                        ps = claim(pe, "seq_s", c).rearrange("p (t n) -> p t n", n=RN)
                        for h in range(RH):
                            t, hp = h // 2, 64 * (h % 2)
                            cols = slice(h * RN, (h + 1) * RN)
                            mm(ps[hp:hp + 64, t, :], kappa_tok[rows, b, cols], v_tok[rows, b, cols], start=True, stop=False)
                            last = mm(ps[hp:hp + 64, t, :], beta_tok[rows, b, cols], seq_u[rows, cols], start=False, stop=True)
                        done(last, "seq_s")
                    ps = claim(pe, "seq_y", c)
                    chunk_rows(c, ps, 1, [(3, v_tok[:, b, :]), (1, seq_u)], "seq_y")
                    if c < NB:
                        values(c)
                def project_out(ps, w, ks, first, end):
                    for b in range(NB):
                        for k in ks:
                            last = mm(ps[:, b * STRIP:(b + 1) * STRIP], yT[:, k, b * P:(b + 1) * P], w[:, k, :],
                                      start=first and (b, k) == (0, ks[0]), stop=end and (b, k) == (NB - 1, ks[-1]),
                                      skip_group_check=True)
                    return last

                pe.wait_ge(S("h_mixed"), 1)
                begun = []
                for i in range(WRING):
                    if i == WRING - 1:
                        for b in range(NB):
                            turn_heads(2 + b, y_tok, b, "y_normed", 1 + b)
                    w = next_strip(pe)
                    ps = claim(pe, "mix_out", i)
                    project_out(ps, w, range(RT, KT), True, False)
                    begun.append((ps, w))
                pe.wait_ge(S("mixed"), 1)
                for ps, w in begun:
                    done(project_out(ps, w, range(0, RT), False, True), "mix_out")
                w = next_strip(pe)
                done(project_out(claim(pe, "mix_out", WRING), w, range(0, KT), True, True), "mix_out")

            def chunk_rows(c, ps, which, products, name):
                b, lo = c // 2, CH * (c % 2)
                rows = slice(lo, lo + CH)

                def on_state(h, start, stop):
                    hp = 64 * (h % 2)
                    return mm(ps[rows, h * RN:(h + 1) * RN], AR[hp:hp + 64, h // 2, b, which, rows],
                              states[(c - 1) % 2][hp:hp + 64, h // 2, :], start=start, stop=stop, skip_group_check=True)

                last_far = max(h for h in range(RH) if 64 * (h % 2) != lo)
                opened = False

                for h in range(RH):
                    near = c > 0 and 64 * (h % 2) == lo
                    if near:
                        on_state(h, not opened, False)
                        opened = True
                    for i, (f, rhs) in enumerate(products):
                        last = mm(ps[rows, h * RN:(h + 1) * RN], SC[rows, UNIT[(b, h)], f, rows],
                                  rhs[rows, h * RN:(h + 1) * RN], start=not opened,
                                  stop=(c == 0 and h == RH - 1 and i == len(products) - 1), skip_group_check=True)
                        opened = True
                if c:
                    last.then_inc(S("row_tile_done"), 1)
                    far_waits[0] += 1
                    pe.wait_ge(S("row_tile_done"), far_waits[0])
                    for h in range(RH):
                        if 64 * (h % 2) != lo:
                            last = on_state(h, False, h == last_far)
                done(last, name)

            far_waits = [0]

            def turn_keys(l):
                pe.wait_ge(S("keys_loaded"), 32 * (l + 1))
                for i in range(4):
                    ps = claim(pe, "key_turn", 4 * l + i).rearrange("p (q n) -> p q n", q=4)
                    for q in range(4):
                        last = tp(ps[:, q, :], keys[:, 4 * i + q, :], ident[:])
                    done(last, "key_turn")

            def score_keys(ps, q0, js, queries):
                for i, j in enumerate(js):
                    last = mm(ps[:, q0 + i, :], queries(j), keyT[:, (j % 2) * EH + j // 2, :], start=True, stop=True)
                return last

            def peer_scores0():
                def queries(k, w, tok):
                    ps = claim(pe, "peer_q", k)
                    n = tok.stop - tok.start
                    for q in range(2):
                        last = project(ps[:, q * n:(q + 1) * n], w, P * q, P, tok)
                    done(last, "peer_q")

                def scores(k, h, blocks):
                    ps = claim(pe, "peer_s", k).rearrange("p (q n) -> p q n", q=4)
                    for i, b in enumerate(blocks):
                        last = score_keys(ps, 2 * i, (2 * h, 2 * h + 1), lambda j: qT[:, j, b * P:(b + 1) * P])
                    done(last, "peer_s")

                w = next_strip(pe)
                for b in range(NB):
                    pe.wait_ge(S("x_normed"), 1 + b)
                    turn_x(4 + 2 * b, b)
                    if b == 0:
                        pe.wait_ge(S("x_turn_taken"), 6)
                        queries(0, w, slice(0, P))
                turn_keys(0)
                pe.wait_ge(S("key_turn_taken"), 4)
                pe.wait_ge(S("peer_q_taken"), 1)
                scores(0, 0, [0])
                pe.wait_ge(S("x_turn_taken"), 8)
                queries(1, w, slice(P, SEQ))
                queries(2, next_strip(pe), slice(0, SEQ))
                pe.wait_ge(S("peer_q_taken"), 2)
                scores(1, 0, [1])
                for h in range(1, EH):
                    if h < EH - 1:
                        queries(h + 2, next_strip(pe), slice(0, SEQ))
                    pe.wait_ge(S("peer_q_taken"), h + 2)
                    scores(h + 1, h, range(NB))

            def feature_strips(name, k, b):
                ps = claim(pe, name, k)
                for i in range(2):
                    w = next_strip(pe)
                    for q in range(2):
                        c = (2 * i + q) * P
                        last = project(ps[:, c:c + P], w, P * q, P, slice(b * P, (b + 1) * P))
                done(last, name)

            def token_strips(name, k, lhs):
                ps = claim(pe, name, k)
                for i in range(2):
                    w = next_strip(pe)
                    for kt in range(KT):
                        last = mm(ps[:, i * STRIP:(i + 1) * STRIP], lhs(kt), w[:, kt, :], start=(kt == 0), stop=(kt == KT - 1))
                done(last, name)

            class Experts:

                def __init__(self, l, b):
                    self.n, self.done = 2 * l + b, 0
                    self.ps = [claim(pe, "experts", 2 * self.n + c) for c in range(2)]

                def row(self, r, turn=0):
                    g = HALF_ROWS * self.n + r
                    j = 2 * (r % HALF_RING)
                    pe.wait_ge(S("diags_made"), turn * (UNROLL // 2) + (g + 1))
                    pe.wait_ge(S(f"v_row{j}"), turn * (16 * UNROLL // RING) + 16 * (g // HALF_RING + 1))
                    for c in range(2):
                        last = mm(self.ps[c], diag[:, r % DIAGS, :], ring_v[:, j, c * 512:(c + 1) * 512],
                                  start=self.done == 0, stop=True, skip_group_check=True)
                    last.then_inc(S("v_rows_done"), 1)
                    self.done += 1

                def rows(self, count):
                    for r in range(self.done, min(self.done + count, HALF_ROWS)):
                        self.row(r)

                def all_rows(self):
                    self.rows(UNROLL // 2)
                    with pe.Fori(1, SLOTS // UNROLL) as i:
                        for r in range(UNROLL // 2):
                            self.row(r, i)

            def mixer1(b):
                tok = slice(b * P, (b + 1) * P)
                pe.wait_ge(S("x_normed"), 3 + 2 * b)
                turn_x(8 + 4 * b, b)
                pe.wait_ge(S("x_turn_taken"), 10 + 4 * b)
                for i in range(4):
                    feature_strips("fox_qk", 4 * b + i, b)
                for i in range(2):
                    token_strips("fox_v", 2 * b + i, lambda kt: xT[:, kt, tok])
                for i in range(2):
                    feature_strips("fox_og", 2 * b + i, b)
                strip_at[0] += 1
                pe.wait_ge(S("f_weights"), b + 1)
                done(project(claim(pe, "fox_f", b)[:, 0:P], fw, 0, P, tok), "fox_f")
                for i in range(4):
                    pe.wait_ge(S("squares"), 4 * b + i + 1)
                    done(mm(claim(pe, "fox_rms", 4 * b + i), pair_ones[:], SQ[:, 4 * i:4 * i + 4, :].rearrange("p t n -> p (t n)"),
                            start=True, stop=True), "fox_rms")
                pe.wait_ge(S("qk_normed"), b + 1)
                pe.wait_ge(S("decay_rows"), b + 1)
                w = P * (b + 1)
                for name, u in attention_plan(b):
                    if name == "att":
                        h = u % FH
                        t, lo = h // 2, 64 * (h % 2)
                        ps = claim(pe, "att", u)[:, 0:w]
                        mm(ps, qc[lo:lo + 64, t, :], kc[lo:lo + 64, t, 0:w], start=True, stop=False)
                        done(mm(ps, ident[lo:lo + 64, lo + h:lo + h + 1].to_broadcast([64, P]), fneg[lo:lo + 64, 0:w],
                                start=False, stop=True), "att")
                    elif name == "att_turn":
                        pe.wait_ge(S("probs_ready"), u + 1)
                        ps = claim(pe, "att_turn", u)
                        for s in range(b + 1):
                            last = tp(ps[:, s * P:(s + 1) * P], prob[:, u % 4, s * P:(s + 1) * P], ident[:])
                        done(last, "att_turn")
                    else:
                        ps = claim(pe, "att_out", u)
                        for q in range(2):
                            n = 2 * u + q
                            h = n % FH
                            lo = 64 * (h % 2)
                            pe.wait_ge(S("att_turn_taken"), n + 1)
                            for s in range(b + 1):
                                last = mm(ps[lo:lo + 64, 0:P], fv[:, s, h * FN:(h + 1) * FN], probT[:, n % 4, s, :],
                                          start=(s == 0), stop=(s == b))
                        done(last, "att_out")

            def mixer1_tail(b):
                ex = Experts(b, 1 - b)
                pe.wait_ge(S("mixed"), b + 2)
                for i in range(2):
                    ex.rows(EARLY_ROWS)
                    token_strips("mix_out", 4 + 2 * b + i, lambda kt: oT[:, kt, :])
                ex.rows(TAIL_ROWS)
                pe.wait_ge(S("x_normed"), 4 + 2 * b)
                turn_x(10 + 4 * b, b)
                pe.wait_ge(S("x_turn_taken"), 12 + 4 * b)
                pe.wait_ge(S("key_turn_taken"), 8)
                for g in range(GROUPS):
                    feature_strips("peer_q", EH + 1 + 4 * b + g, b)
                    ex.rows(TAIL_ROWS)
                    pe.wait_ge(S("peer_q_taken"), EH + 2 + 4 * b + g)
                    ps = claim(pe, "peer_s", EH + 1 + 4 * b + g).rearrange("p (q n) -> p q n", q=4)
                    done(score_keys(ps, 0, range(4 * g, 4 * g + 4), lambda j: qT1[:, j, :]), "peer_s")
                ex.rows(HALF_ROWS)

            pe.sem_inc(S("v_rows_done"), HALF_RING)
            mixer0()
            peer_scores0()
            Experts(0, 0).all_rows()
            turn_keys(1)
            for b in range(NB):
                mixer1(b)
                mixer1_tail(b)
            Experts(1, 1).all_rows()

        @block.scalar
        def _(act):
            st = Steps(act, "scalar_step")
            af = nc.scalar.activation

            def taken(ins, name):
                ins.then_inc(S(name + "_taken"), 1)

            def copy(out_, in_):
                return nc.scalar.copy(out_, in_)

            ZERO, ONE, EPS_LN, EPS_RWKV, EPS_FOX = (cexp[:, i:i + 1] for i in range(5))

            def root(ready, n, ap, bias, scale, sem):
                act.wait_ge(S(ready), n)
                af(ap, ap, ACT.Sqrt, bias=bias, scale=scale).then_inc(S(sem), 1)

            def ln_root(e):
                root("ln_var", e + 1, lnmv[:, NORMS[e][1], 1:2], EPS_LN, 1.0, "ln_std")

            def take_x(first, b):
                for half in range(2):
                    ps = full(act, "x_turn", first + half)
                    taken(copy(xT[:, 4 * half:4 * half + 4, b * P:(b + 1) * P], ps.rearrange("p (k n) -> p k n", k=4)),
                          "x_turn")

            def mixer0():
                for b in range(NB):
                    take_x(2 * b, b)
                act.wait_ge(S("constants"), 1)
                act.wait_ge(S("params_taken"), 1)
                act.wait_ge(S("one_mu"), 1)
                for t in range(14):
                    ps = full(act, "rwkv_in", t)[:, 0:SEQ]
                    af(R[:, t * SEQ:(t + 1) * SEQ], ps, ACT.Identity, bias=ZERO, scale=one_mu[:, t:t + 1]
                       ).then_inc(S("rwkv_scaled"), 1)
                act.wait_ge(S("rwkv_in_taken"), 14)
                af(xg, xg, ACT.Sigmoid)
                af(xwa[0:64, :], xwa[0:64, :], ACT.Tanh).then_inc(S("lora_squashed"), 1)
                for name, dst, bias in (("lora_w", logw, "w0"), ("lora_a", a_all, "a0")):
                    for half in range(2):
                        ps = full(act, name, half)
                        for q in range(2):
                            t = 2 * half + q
                            last = af(dst[:, t * SEQ:(t + 1) * SEQ], ps[:, q * SEQ:(q + 1) * SEQ], ACT.Sigmoid,
                                      bias=par(bias, t), scale=1.0)
                        taken(last, name)
                for half in range(2):
                    taken(copy(g_all[:, half * 512:(half + 1) * 512], full(act, "lora_g", half)), "lora_g")
                for half in range(2):
                    taken(af(tmp[:, half * 512:(half + 1) * 512], full(act, "kk_norm", half), ACT.Sqrt, bias=ZERO), "kk_norm")
                act.wait_ge(S("cum_ready"), 1)
                af(pfull, cumw, ACT.Exp)
                af(pinv, cumw, ACT.Exp, scale=-1.0)
                act.wait_ge(S("cum_ready"), 2)
                af(pprev, pprev, ACT.Exp).then_inc(S("decays"), 1)
                for t in range(8):
                    ps = full(act, "conv_in", t)[:, 0:SEQ]
                    dst = cut(4608 + t * SEQ, SEQ)
                    af(dst, ps, ACT.Identity, bias=par("conv_b", t), scale=par("conv_w", 24 + t)).then_inc(S("conv_scaled"), 1)
                for i, dst in enumerate((v_tok, beta_tok, kappa_tok)):
                    for b in range(NB):
                        taken(copy(dst[:, b, :], full(act, "token_turn", NB * i + b)), "token_turn")
                act.wait_ge(S("conv_in_taken"), 8)
                for t in range(2):
                    af(conv_sig(t), cut(4608 + t * 1024, 1024), ACT.Sigmoid).then_inc(S("conv_sigmoid"), 1)
                act.wait_ge(S("small_loaded"), 64)
                ps = full(act, "gates_in", 0)
                af(mr[0:MH, 0, :], ps[0:MH, 0:SEQ], ACT.Identity, bias=small[0:MH, 0:1], scale=1.0)
                taken(af(mr[0:MH, 1, :], ps[0:MH, SEQ:2 * SEQ], ACT.Identity, bias=small[0:MH, 1:2], scale=1.0), "gates_in")
                act.wait_ge(S("m_abs"), 1)
                st.then(af(mr[0:MH, 3, :], mr[0:MH, 3, :], ACT.Exp, scale=-1.0))
                st.settle()
                af(mr[0:MH, 3, :], mr[0:MH, 3, :], ACT.Ln, bias=ONE[0:MH]).then_inc(S("m_log"), 1)
                act.wait_ge(S("m_neg"), 1)
                af(mr[0:MH, 5, :], mr[0:MH, 5, :], ACT.Exp).then_inc(S("m_rows"), 1)
                for t in range(2):
                    taken(copy(mv_all[:, t * 512:(t + 1) * 512], full(act, "vo_in", t)), "vo_in")
                for t in range(2):
                    taken(af(mo_all[:, t * 512:(t + 1) * 512], full(act, "vo_in", 2 + t), ACT.Sigmoid), "vo_in")
                act.wait_ge(S("t_zeroed"), 1)
                act.wait_ge(S("d_begun"), 1)
                act.wait_ge(S("silu"), 2)
                for at in (0, CH):
                    copy(DC[at:at + CH, 1, :, :], DT[at:at + CH, :, at:at + CH]).then_inc(S("d_copied"), 1)
                for i in range(len(LEVELS)):
                    for g in range(4):
                        us = slice(4 * g, 4 * g + 4)
                        ps = full(act, "inv_t", 4 * i + g)[:, 0:4 * CH].rearrange("p (u n) -> p u n", u=4)
                        for at in (0, CH):
                            copy(Tm[at:at + CH, us, at:at + CH], ps[at:at + CH])
                        taken(copy(Tc[:, us, :], ps), "inv_t")
                    if i + 1 < len(LEVELS):
                        for g in range(4):
                            us = slice(4 * g, 4 * g + 4)
                            act.wait_ge(S("inv_d_taken"), 4 * i + g + 1)
                            copy(DT[CH:P, us, CH:P], DC[CH:P, 1, us, :]).then_inc(S("d_copied"), 1)
                for b in range(NB):
                    taken(copy(vaug[:, b, :, 0:MN], full(act, "mv_turn", b).rearrange("p (h n) -> p h n", h=MH)), "mv_turn")
                for h in range(MH):
                    act.wait_ge(S("mx_clamped"), h + 1)
                    af(scT[:, h, :], scT[:, h, :], ACT.Exp).then_inc(S("m_weights"), 1)

                def turned(k, half, b):
                    g, bias = (("ln_g", "ln_b"), ("hn_g", "hn_b"))[half]
                    ps = full(act, "y_turn", k)
                    for t in range(RT):
                        last = af(yT[:, 4 * half + t, b * P:(b + 1) * P], ps[:, t * P:(t + 1) * P], ACT.Identity,
                                  bias=par(bias, t), scale=par(g, t))
                    taken(last, "y_turn")

                for c in range(NCH):
                    rows = slice(CH * (c % 2), CH * (c % 2) + CH)
                    taken(copy(seq_x[rows, :], full(act, "seq_x", c)[rows, :]), "seq_x")
                    if c == NB:
                        root("head_var", 1, stat[:, 1, 0:NB * MH], EPS_LN, 1.0 / MN, "head_std")
                    taken(af(seq_u[rows, :], full(act, "seq_u", c)[rows, :], ACT.Copy, scale=-1.0), "seq_u")
                    if c == NB:
                        for b in range(NB):
                            turned(b, 1, b)
                root("head_var", 2, stat[:, 1, 0:RH], EPS_RWKV, 1.0 / RN, "head_std")
                root("head_var", 3, stat[:, 1, RH:2 * RH], EPS_RWKV, 1.0 / RN, "head_std")
                turned(2, 0, 0)
                turned(3, 0, 1)
                ln_root(0)
                ln_root(1)

            def take_keys(l):
                for i in range(4):
                    taken(copy(keyT[:, 4 * i:4 * i + 4, :], full(act, "key_turn", 4 * l + i).rearrange("p (q n) -> p q n", q=4)),
                          "key_turn")

            def peer_scores0():
                def queries(k, h, tok):
                    n = tok.stop - tok.start
                    taken(copy(qT[:, 2 * h:2 * h + 2, tok], full(act, "peer_q", k)[:, 0:2 * n].rearrange("p (q n) -> p q n", q=2)),
                          "peer_q")

                def scores(k, h, b0, b1):
                    nb = b1 - b0
                    ps = full(act, "peer_s", k)[:, 0:2 * nb * P].rearrange("p (b q n) -> p b q n", b=nb, q=2)
                    taken(copy(sc[:, b0:b1, 2 * h:2 * h + 2, :], ps), "peer_s")

                take_x(4, 0)
                queries(0, 0, slice(0, P))
                take_x(6, 1)
                take_keys(0)
                scores(0, 0, 0, 1)
                queries(1, 0, slice(P, SEQ))
                queries(2, 1, slice(0, SEQ))
                scores(1, 0, 1, 2)
                for h in range(1, EH):
                    if h < EH - 1:
                        queries(h + 2, h + 1, slice(0, SEQ))
                    scores(h + 1, h, 0, NB)

            def activate(l, b):
                n = 2 * l + b
                act.wait_ge(S("gate_shifted"), n + 1)
                g = gate[:, b, :]
                af(g, g, ACT.Exp).then_inc(S("gate_exp"), 1)
                act.wait_ge(S("hidden"), n + 1)
                af(ga[:, b, :], hid[:, b, :], ACT.Gelu).then_inc(S("gelued"), 1)

            class Diags:

                def __init__(self, l, b):
                    self.n, self.b, self.done = 2 * l + b, b, 0
                    act.wait_ge(S("weights"), self.n + 1)

                def rows(self, count):
                    for r in range(self.done, min(self.done + count, HALF_ROWS)):
                        act.wait_ge(S("v_rows_done"), HALF_ROWS * self.n + r + 1)
                        af(diag[:, r % DIAGS, :], ident[:], ACT.Copy, scale=ga[:, self.b, 2 * r:2 * r + 1]
                           ).then_inc(S("diags_made"), 1)
                    self.done = min(self.done + count, HALF_ROWS)

                def all_rows(self):
                    first = staged_sets[0]
                    staged_sets[0] += SLOTS // RING
                    with act.Fori(0, SLOTS // UNROLL) as i:
                        for k in range(UNROLL // RING):
                            g = HALF_ROWS * self.n + HALF_RING * k
                            act.wait_ge(S("v_rows_done"), i * (UNROLL // 2) + (g + 1))
                            copy(gstage[:, k, :], ga[:, self.b, bass.ds(i * UNROLL + RING * k, RING)]
                                 ).then_inc(S("weights_staged"), 1)
                            act.wait_ge(S("weights_staged"), i * (UNROLL // RING) + (first + k + 1))
                            for r in range(HALF_RING):
                                act.wait_ge(S("v_rows_done"), i * (UNROLL // 2) + (g + r + 1))
                                af(diag[:, r % DIAGS, :], ident[:], ACT.Copy, scale=gstage[:, k, 2 * r:2 * r + 1]
                                   ).then_inc(S("diags_made"), 1)

            staged_sets = [0]

            def mixer1(b):
                tok = slice(b * P, (b + 1) * P)
                wide = lambda ps: ps.rearrange("p (t n) -> p t n", n=P)
                take_x(8 + 4 * b, b)
                for i in range(4):
                    dst = qc[:, 4 * i:4 * i + 4, :] if i < 2 else kc[:, 4 * i - 8:4 * i - 4, tok]
                    taken(copy(dst, wide(full(act, "fox_qk", 4 * b + i))), "fox_qk")
                for i in range(2):
                    taken(copy(fv[:, b, i * 512:(i + 1) * 512], full(act, "fox_v", 2 * b + i)), "fox_v")
                for i in range(2):
                    taken(af(ogT[:, 4 * i:4 * i + 4, :], wide(full(act, "fox_og", 2 * b + i)), ACT.Sigmoid), "fox_og")
                n = strips_before_f[b]
                act.wait_ge(S(f"strip_loaded{n % WRING}"), 16 * (n // WRING + 1))
                act.wait_ge(S("f_zeroed"), b + 1)
                copy(fw[:, :, 0:FH], wring[:, n % WRING, :, 0:FH])
                copy(fw[:, :, 64:64 + FH], wring[:, n % WRING, :, 0:FH]).then_inc(S("f_weights"), 1)
                taken(af(fz, full(act, "fox_f", b)[:, 0:P], ACT.Identity, bias=small[:, 2:3], scale=1.0), "fox_f")
                act.wait_ge(S("f_abs"), b + 1)
                st.then(af(fl, fl, ACT.Exp, scale=-1.0))
                st.settle()
                af(fl, fl, ACT.Ln, bias=ONE).then_inc(S("f_log"), 1)
                for i in range(4):
                    taken(af(RS[:, 4 * i:4 * i + 4, :], wide(full(act, "fox_rms", 4 * b + i)), ACT.Sqrt, bias=EPS_FOX), "fox_rms")
                w = P * (b + 1)
                for s in range(FH + 2):
                    if s < FH:
                        u = FH * b + s
                        act.wait_ge(S("logits_max"), u + 1)
                        if s >= 4:
                            await_filled(act, "att_turn", u - 4)
                        af(prob[:, u % 4, 0:w], lg[:, u % 4, 0:w], ACT.Exp, bias=amax[:, u:u + 1], scale=1.0,
                           accum_out=asum[:, u:u + 1]).then_inc(S("exped"), 1)
                    if s >= 2:
                        u = FH * b + s - 2
                        ps = full(act, "att_turn", u)
                        if s - 2 >= 4:
                            await_filled(act, "att_out", (u - 4) // 2)
                        taken(copy(probT[:, u % 4, 0:b + 1, :], wide(ps[:, 0:w])), "att_turn")

            def mixer1_tail(b):
                activate(b, 1 - b)
                di = Diags(b, 1 - b)
                di.rows(2 * EARLY_ROWS)
                ln_root(3 + 2 * b)
                di.rows(TAIL_ROWS)
                take_x(10 + 4 * b, b)
                for i in range(4):
                    taken(copy(qT1[:, 4 * i:4 * i + 4, :], full(act, "peer_q", EH + 1 + 4 * b + i).rearrange("p (q n) -> p q n", q=4)),
                          "peer_q")
                    di.rows(TAIL_ROWS)
                    ps = full(act, "peer_s", EH + 1 + 4 * b + i).rearrange("p (q n) -> p q n", q=4)
                    taken(copy(sc[:, 0, 4 * i:4 * i + 4, :], ps), "peer_s")
                di.rows(HALF_ROWS)

            mixer0()
            peer_scores0()
            activate(0, 0)
            Diags(0, 0).all_rows()
            ln_root(2)
            take_keys(1)
            mixer1(0)
            mixer1_tail(0)
            ln_root(4)
            mixer1(1)
            mixer1_tail(1)
            ln_root(6)
            activate(1, 1)
            Diags(1, 1).all_rows()
            ln_root(7)

        @block.vector
        def _(dve):
            v = nc.vector
            st = Steps(dve, "vector_step")
            tt, ts, stt = v.tensor_tensor, v.tensor_scalar, v.scalar_tensor_tensor

            def go(ins):
                st.then(ins)
                st.settle()

            def taken(ins, name):
                ins.then_inc(S(name + "_taken"), 1)

            def half_stats(b, c):
                st.then(v.bn_stats(lnst[:, b, 6 * c:6 * c + 6], halves(b)[c]))

            def layer_norm(e, known=0):
                b = NORMS[e][1]
                parts = halves(b)
                dve.wait_ge(S("ln_loaded"), 32 * NORM_LOADS[e])
                for c in range(known, 2):
                    half_stats(b, c)
                st.settle()
                v.bn_aggr(lnmv[:, b, :], lnst[:, b, :]).then_inc(S("ln_var"), 1)
                dve.wait_ge(S("ln_std"), e + 1)
                go(v.reciprocal(lnrs[:, b:b + 1], lnmv[:, b, 1:2]))
                for c, part in enumerate(parts):
                    st.then(ts(part, part, lnmv[:, b, 0:1], lnrs[:, b:b + 1], ALU.subtract, ALU.mult))
                st.settle()
                go(tt(xres[:, b, :], xres[:, b, :], ln_par[:, 0, :], ALU.mult))
                tt(xres[:, b, :], xres[:, b, :], ln_par[:, 1, :], ALU.add).then_inc(S("x_normed"), 1)
                dve.wait_ge(S("x_normed"), e + 1)

            def head_norm(x, scratch, at, groups, n, norms, sem):
                g = x.rearrange("p (g n) -> p g n", n=n)
                q = scratch.rearrange("p (g n) -> p g n", n=n)
                mean, ss = stat[:, 0, at:at + groups], stat[:, 1, at:at + groups]
                wide = lambda s: s.rearrange("p (g o) -> p g o", o=1).to_broadcast([P, groups, n])
                go(v.tensor_reduce(mean, g, AX_X, ALU.add))
                go(ts(mean, mean, 1.0 / n, None, ALU.mult))
                go(tt(g, g, wide(mean), ALU.subtract))
                go(tt(q, g, g, ALU.mult))
                v.tensor_reduce(ss, q, AX_X, ALU.add).then_inc(S("head_var"), 1)
                dve.wait_ge(S("head_std"), norms)
                go(v.reciprocal(ss, ss))
                tt(g, g, wide(ss), ALU.mult).then_inc(S(sem), 1)

            def log_sigmoid(z, t, o, ready, logged, n=1):
                stt(t, z, -1.0, z, ALU.mult, ALU.max).then_inc(S(ready), 1)
                dve.wait_ge(S(logged), n)
                go(stt(o, z, 0.0, t, ALU.min, ALU.subtract))

            def mlstm_values(b):
                for i in range(2):
                    n = 2 * b + i
                    ps = full(dve, "hnum", n).rearrange("p (q n) -> p q n", q=2)
                    d = dcol[:, 2 * n:2 * n + 2]
                    go(v.tensor_copy(d, ps[:, :, MN]))
                    go(stt(d, d, -1.0, d, ALU.mult, ALU.max))
                    go(tt(d, d, gcol[:, 2 * MH + MH * b + 2 * i:2 * MH + MH * b + 2 * i + 2], ALU.max))
                    go(v.reciprocal(d, d))
                    for q in range(2):
                        c = b * 512 + (2 * i + q) * MN
                        ins = ts(h_tok[:, c:c + MN], ps[:, q, 0:MN], d[:, q:q + 1], None, ALU.mult)
                        if q == 0:
                            st.then(ins)
                    taken(ins, "hnum")

            def mlstm_rows():
                dve.wait_ge(S("gates_in_taken"), 1)
                rows = [mr[0:MH, i, :] for i in range(6)]
                log_sigmoid(rows[1], rows[3], rows[1], "m_abs", "m_log")
                go(v.tensor_tensor_scan(rows[3], ones[0:MH, :], rows[1], 0.0, ALU.mult, ALU.add))
                go(tt(rows[2], rows[0], rows[3], ALU.subtract))
                go(v.tensor_tensor_scan(rows[4], rows[2], rows[2], 0.0, ALU.max, ALU.max))
                go(tt(rows[5], rows[3], rows[4], ALU.add))
                go(ts(rows[5], rows[5], -1.0, None, ALU.mult))
                ts(rows[4], rows[4], -1.0, None, ALU.mult).then_inc(S("m_neg"), 1)
                dve.wait_ge(S("conv_sigmoid"), 1)
                stt(mq_all, mq_all, float(MN) ** -0.5, conv_sig(0), ALU.mult, ALU.mult).then_inc(S("silu"), 1)
                dve.wait_ge(S("conv_sigmoid"), 2)
                tt(mk_all, mk_all, conv_sig(1), ALU.mult).then_inc(S("silu"), 1)
                dve.wait_ge(S("silu"), 2)

            def mixer0():
                dve.wait_ge(S("constants"), 1)
                taken(v.tensor_copy(pars[:, 0:NROWS], full(dve, "params", 0)[:, 0:NROWS]), "params")
                dve.wait_ge(S("params_taken"), 1)
                st.then(ts(kn8[:], pars[:, ROWS["kn_g"][0]:ROWS["kn_g"][0] + 8], float(FN) ** 0.5, None, ALU.mult))
                ts(one_mu[:], pars[:, 0:14], -1.0, 1.0, ALU.mult, ALU.add).then_inc(S("one_mu"), 1)
                for t in range(14):
                    dve.wait_ge(S("rwkv_scaled"), t + 1)
                    ps = full(dve, "rwkv_in", t)
                    dst = R[:, t * SEQ + 1:(t + 1) * SEQ]
                    taken(stt(dst, ps[:, 0:SEQ - 1], par("mu", t), dst, ALU.mult, ALU.add), "rwkv_in")
                dve.wait_ge(S("rwkv_in_taken"), 14)
                for t in range(RT):
                    st.then(ts(kk_all[:, t * SEQ:(t + 1) * SEQ], k_all[:, t * SEQ:(t + 1) * SEQ], par("k_k", t), None, ALU.mult))
                st.settle()
                tt(tmp, kk_all, kk_all, ALU.mult).then_inc(S("head_products"), 1)
                dve.wait_ge(S("lora_w_taken"), 2)
                go(ts(logw, logw, -float(2.718281828459045 ** -0.5), None, ALU.mult))
                for i in range(RT * NCH):
                    ins = v.tensor_tensor_scan(cumw[:, i * CH:(i + 1) * CH], ones[:, 0:CH], logw[:, i * CH:(i + 1) * CH], 0.0,
                                               ALU.mult, ALU.add)
                    if i < RT * NCH - 1:
                        st.then(ins)
                ins.then_inc(S("cum_ready"), 1)
                dve.wait_ge(S("cum_ready"), 1)
                tt(pprev, cumw, logw, ALU.subtract).then_inc(S("cum_ready"), 1)
                dve.wait_ge(S("kk_norm_taken"), 2)
                go(ts(tmp, tmp, 1e-12, None, ALU.max))
                go(v.reciprocal(tmp, tmp))
                go(tt(kk_all, kk_all, tmp, ALU.mult))
                dve.wait_ge(S("lora_a_taken"), 2)
                for t in range(RT):
                    c = slice(t * SEQ, (t + 1) * SEQ)
                    st.then(ts(tmp[:, c], a_all[:, c], 1.0, par("k_a", t), ALU.subtract, ALU.mult))
                st.settle()
                go(stt(k_all, tmp, 1.0, k_all, ALU.add, ALU.mult))
                for t in range(RT):
                    c = slice(t * SEQ, (t + 1) * SEQ)
                    ins = stt(tmp[:, c], r_all[:, c], par("r_k", t), k_all[:, c], ALU.mult, ALU.mult)
                ins.then_inc(S("head_products"), 1)
                dve.wait_ge(S("decays"), 1)
                view = lambda x: x.rearrange("p (t b n) -> p t b n", t=RT, b=NB)
                st.then(v.tensor_copy(pend[:], pfull.rearrange("p (t c n) -> p t c n", t=RT, c=NCH)[:, :, :, CH - 1]))
                st.then(tt(AR[:, :, :, 0, :], view(kk_all), view(pprev), ALU.mult))
                st.then(tt(AR[:, :, :, 1, :], view(r_all), view(pfull), ALU.mult))
                go(tt(beta_all, kk_all, a_all, ALU.mult))
                st.then(tt(beta_all, beta_all, pinv, ALU.mult))
                tt(kappa_all, k_all, pinv, ALU.mult).then_inc(S("scan_operands"), 1)
                for t in range(8):
                    dve.wait_ge(S("conv_scaled"), t + 1)
                    ps = full(dve, "conv_in", t)
                    for back in (1, 2, 3):
                        dst = cut(4608 + t * SEQ, SEQ)[:, back:SEQ]
                        ins = stt(dst, ps[:, 0:SEQ - back], par("conv_w", 8 * (3 - back) + t), dst, ALU.mult, ALU.add)
                        if back < 3:
                            go(ins)
                        else:
                            taken(ins, "conv_in")
                for half in range(2):
                    c = slice(half * 512, (half + 1) * 512)
                    taken(tt(bonus_all[:, c], full(dve, "bonus", half), v_all[:, c], ALU.mult), "bonus")
                for u in range(16):
                    ps = full(dve, "scores", u).rearrange("p (f n) -> p f n", f=2)
                    taken(tt(SC[:, u, :, :].rearrange("p (f g) n -> p f (g n)", f=2), ps,
                             score_mask[:].rearrange("p g n -> p (g n)").unsqueeze(1).to_broadcast([P, 2, 2 * P]), ALU.mult),
                          "scores")
                dve.wait_ge(S("scores_taken"), 16)
                wide = lambda m: m.unsqueeze(1).to_broadcast([P, 4, P])
                for g in range(4):
                    us = slice(4 * g, 4 * g + 4)
                    ps = full(dve, "ab", g).rearrange("p (u n) -> p u n", u=4)
                    for at in (0, CH):
                        own = lambda x: x[at:at + CH, at:at + CH].unsqueeze(1).to_broadcast([CH, 4, CH])
                        ins = stt(DC[at:at + CH, 0, us, :], ps[at:at + CH, :, at:at + CH], -1.0, own(level_one), ALU.mult, ALU.mult)
                        if at == 0:
                            st.then(ins)
                    taken(ins, "ab")
                    st.then(stt(DT[:, us, :], SC[:, us, 0, :], -1.0, wide(level_mask[:, 0, :]), ALU.mult, ALU.mult))
                dve.wait_ge(S("ab_taken"), 4)
                st.settle()
                for g in range(4):
                    us = slice(4 * g, 4 * g + 4)
                    st.then(tt(DT[:, us, :], DT[:, us, :], wide(ident[:]), ALU.add))
                for at in (0, CH):
                    st.then(tt(DC[at:at + CH, 0, :, :], DC[at:at + CH, 0, :, :],
                               ident[at:at + CH, at:at + CH].unsqueeze(1).to_broadcast([CH, 16, CH]), ALU.add))
                st.settle()
                dve.sem_inc(S("d_begun"), 1)

                def merge_operand(i, g):
                    us = slice(4 * g, 4 * g + 4)
                    tt(LM[:, us, :], SC[:, us, 0, :], wide(level_mask[:, i + 1, :]), ALU.mult).then_inc(S("merge_ready"), 1)

                for g in range(4):
                    merge_operand(0, g)
                mlstm_rows()
                dve.wait_ge(S("d_copied"), 2)
                for i, m in enumerate(LEVELS):
                    for g in range(4):
                        us = slice(4 * g, 4 * g + 4)
                        ps = full(dve, "inv_d", 4 * i + g).rearrange("p (two u n) -> p two u n", two=2, u=4)
                        far = DT[0:CH, us, 0:CH]
                        if m == LEVELS[-1]:
                            tt(far, far, ps[0:CH, 1], ALU.subtract)
                            far = DT[CH:P, us, CH:P]
                            taken(tt(far, far, ps[CH:P, 1], ALU.subtract), "inv_d")
                        else:
                            tt(far, far, ps[0:CH, 1], ALU.subtract)
                            taken(tt(DC[:, :, us, :], DC[:, :, us, :], ps, ALU.subtract), "inv_d")
                            merge_operand(i + 1, g)
                dve.wait_ge(S("inv_d_taken"), 4 * len(LEVELS))
                taken(v.tensor_copy(gcol[:], full(dve, "mrow_turn", 0)[:, 0:16]), "mrow_turn")
                dve.wait_ge(S("mrow_turn_taken"), 1)
                for i in range(2):
                    ps = full(dve, "mx_row", i)
                    for q in range(2):
                        h = 2 * i + q
                        st.then(ts(scT[:, h, 0:SEQ], ps[:, q * SEQ:(q + 1) * SEQ], gcol[:, h:h + 1], 0.0, ALU.add, ALU.min))
                        ins = ts(scT[:, h, SEQ:SEQ + P], ps[:, q * SEQ + P:(q + 1) * SEQ], gcol[:, MH + h:MH + h + 1], 0.0,
                                 ALU.add, ALU.min)
                        if q == 0:
                            st.then(ins)
                    taken(ins, "mx_row")
                    dve.wait_ge(S("mx_row_taken"), i + 1)
                    dve.sem_inc(S("mx_clamped"), 2)
                for h in range(MH):
                    dve.wait_ge(S("m_weights"), h + 1)
                    go(tt(scT[:, h, :], scT[:, h, :], causal_st[:], ALU.mult))
                    taken(tt(scT[:, h, :], full(dve, "qk", h)[:, 0:384], scT[:, h, :], ALU.mult), "qk")
                for c in range(NCH):
                    b, rows = c // 2, slice(CH * (c % 2), CH * (c % 2) + CH)
                    if c < NCH - 1:
                        ps = full(dve, "seq_s", c).rearrange("p (t n) -> p t n", n=RN)
                        state, before = states[c % 2], states[(c - 1) % 2]
                        if c == 0:
                            taken(v.tensor_copy(state, ps[:, 0:RT, :]), "seq_s")
                        else:
                            taken(tt(state, before, ps[:, 0:RT, :], ALU.add), "seq_s")
                        dve.wait_ge(S("seq_s_taken"), c + 1)
                        tt(state, state, pend[:, :, c:c + 1].to_broadcast([P, RT, RN]), ALU.mult).then_inc(S("state_ready"), 1)
                        dve.wait_ge(S("state_ready"), c + 1)
                    taken(v.tensor_copy(y_tok[rows, b * 512:(b + 1) * 512], full(dve, "seq_y", c)[rows, :]), "seq_y")
                    if c < NB:
                        mlstm_values(c)
                    if c == NB - 1:
                        dve.wait_ge(S("hnum_taken"), 4)
                        head_norm(h_tok, mk_all, 0, NB * MH, MN, 1, "h_normed")
                    if c == NB:
                        ym = cut(29184, 1024)
                        dve.wait_ge(S("y_turn_taken"), 2)
                        tt(ym, ym, mo_all, ALU.mult).then_inc(S("h_mixed"), 1)
                    if c >= NB:
                        n = c - NB
                        dve.wait_ge(S("seq_y_taken"), NB * (n + 1))
                        head_norm(y_tok[:, n * 512:(n + 1) * 512], y_scratch[:, n * 512:(n + 1) * 512], n * RH, RH, RN, 2 + n,
                                  "y_normed")
                for b in range(NB):
                    block_of = lambda x: x.rearrange("p (t n) -> p t n", t=RT)[:, :, b * P:(b + 1) * P]
                    yr = block_of(cut(28160, 1024))
                    dve.wait_ge(S("y_turn_taken"), 3 + b)
                    go(tt(yr, yr, block_of(bonus_all), ALU.add))
                    go(tt(yr, yr, block_of(g_all), ALU.mult))
                dve.sem_inc(S("mixed"), 1)
                for i in range(4):
                    ps = full(dve, "mix_out", i).rearrange("p (b n) -> p b n", b=NB)
                    x = xres[:, :, i * STRIP:(i + 1) * STRIP]
                    taken(stt(x, x, ALPHA, ps, ALU.mult, ALU.add), "mix_out")
                    if i == 1:
                        dve.wait_ge(S("mix_out_taken"), 2)
                        for b in range(NB):
                            half_stats(b, 0)
                dve.wait_ge(S("mix_out_taken"), 4)
                for b in range(NB):
                    layer_norm(b, 1)

            y_scratch = cut(24064, 1024)

            def halves(b):
                return [xres[:, b, c * 512:(c + 1) * 512] for c in range(2)]

            def top16(src, scratch, vals, idx, n, between):
                for i in range(n):
                    st.then(v.max(vals[:, i, 0:8], src[:, i, :]))
                between()
                st.settle()
                for i in range(n):
                    st.then(v.max_index(idx[:, i, 0:8], vals[:, i, 0:8], src[:, i, :]))
                    st.then(v.match_replace(scratch[:, i, :], vals[:, i, 0:8], src[:, i, :], -BIG))
                between()
                st.settle()
                for i in range(n):
                    st.then(v.max(vals[:, i, 8:16], scratch[:, i, :]))
                between()
                st.settle()
                for i in range(n):
                    st.then(v.max_index(idx[:, i, 8:16], vals[:, i, 8:16], scratch[:, i, :]))
                st.settle()

            def route(l, b, groups, between):
                vv = v16.rearrange("p (h two) k -> p h two k", two=2)
                iv = i16.rearrange("p (h two) k -> p h two k", two=2)
                cv = cand.rearrange("p h (i j) -> p h i j", i=TOPK)
                scratch, cscratch = scr.rearrange("p (i n) -> p i n", i=16), scr.rearrange("p (h n) -> p h n", h=EH)
                iota = iota16[:].unsqueeze(1).unsqueeze(1)
                down = lambda x: x.unsqueeze(3).to_broadcast([P, nh, TOPK, TOPK])
                across = lambda x: x.unsqueeze(2).to_broadcast([P, nh, TOPK, TOPK])
                for g, (h0, h1) in enumerate(groups):
                    nh = h1 - h0
                    meanwhile = lambda: between(g)
                    hs, js, slots = slice(h0, h1), slice(2 * h0, 2 * h1), slice(TOPK * h0, TOPK * h1)
                    dve.wait_ge(S("peer_s_taken"), EH + 1 + GROUPS * b + h1 // 2 if l else 1 if (b, h1) == (0, 1) else h1 + 1)
                    top16(sc[:, 0 if l else b, js, :], scratch[:, js, :], v16[:, js, :], i16[:, js, :], 2 * nh, meanwhile)
                    st.then(v.tensor_copy(i16f[:, hs], iv[:, hs]))
                    go(tt(cv[:, hs], down(vv[:, hs, 0, :]), across(vv[:, hs, 1, :]), ALU.add))
                    top16(cand[:, hs, :], cscratch[:, hs, :], csc[:, hs, :], pos[:, hs, :], nh, meanwhile)
                    pf = pos[:, hs, :].rearrange("p h k -> p (h k)")
                    st.then(ts(hilo_u[:, 0, slots], pf, 4, None, ALU.logical_shift_right))
                    go(ts(hilo_u[:, 1, slots], pf, 15, None, ALU.bitwise_and))
                    go(v.tensor_copy(hilo.rearrange("p w h k -> p w (h k)")[:, :, slots], hilo_u[:, :, slots]))
                    for w in range(2):
                        go(tt(onehot[:, hs], down(hilo[:, w, hs, :]), iota.to_broadcast([P, nh, TOPK, TOPK]), ALU.is_equal))
                        meanwhile()
                        go(tt(onehot[:, hs], onehot[:, hs], across(i16f[:, hs, w, :]), ALU.mult))
                        go(v.tensor_reduce(e12[:, w, hs].rearrange("p h k -> p (h k)"),
                                           onehot[:, hs].rearrange("p h k j -> p (h k) j"), AX_X, ALU.add))
                    ef = e12.rearrange("p w h k -> p w (h k)")
                    go(stt(eidf[:, slots], ef[:, 0, slots], float(NK), ef[:, 1, slots], ALU.mult, ALU.add))
                    v.tensor_copy(eid[:, b, slots], eidf[:, slots]).then_inc(S("experts_chosen"), nh)
                g = gate[:, b, :].rearrange("p (h k) -> p h k", h=EH)
                tt(g, csc, csc[:, :, 0:1].to_broadcast([P, EH, TOPK]), ALU.subtract).then_inc(S("gate_shifted"), 1)

            def weigh(l, b):
                g = gate[:, b, :].rearrange("p (h k) -> p h k", h=EH)
                dve.wait_ge(S("gate_exp"), 2 * l + b + 1)
                go(v.tensor_reduce(gsum[:, 0:EH], g, AX_X, ALU.add))
                go(v.reciprocal(gsum[:, EH:2 * EH], gsum[:, 0:EH]))
                go(tt(g, g, gsum[:, EH:2 * EH].unsqueeze(2).to_broadcast([P, EH, TOPK]), ALU.mult))
                dve.wait_ge(S("gelued"), 2 * l + b + 1)
                tt(ga[:, b, :], ga[:, b, :], gate[:, b, :], ALU.mult).then_inc(S("weights"), 1)

            class Adds:

                def __init__(self, l, b):
                    self.n, self.b, self.done = 2 * l + b, b, 0
                    for x in halves(b):
                        ts(x, x, ALPHA, None, ALU.mult).then_inc(S("x_scaled"), 1)
                    dve.wait_ge(S("x_scaled"), 2 * self.n + 2)

                def row(self, r, turn=0):
                    g = HALF_ROWS * self.n + r
                    j = 2 * (r % HALF_RING) + 1
                    dve.wait_ge(S(f"v_row{j}"), turn * (16 * UNROLL // RING) + 16 * (g // HALF_RING + 1))
                    w = (ga[:, self.b, 2 * r + 1:2 * r + 2] if isinstance(turn, int) else
                         ga[:, self.b, bass.ds(turn * UNROLL + (2 * r + 1), 1)])
                    for c, x in enumerate(halves(self.b)):
                        dve.wait_ge(S(f"half_sums{c}"), turn * (UNROLL // 2) + (g + HALF_RING))
                        stt(x, ring_v[:, j, c * 512:(c + 1) * 512], w, x, ALU.mult, ALU.add).then_inc(S(f"half_sums{c}"), 1)

                def rows(self, count):
                    for r in range(self.done, min(self.done + count, HALF_ROWS)):
                        self.row(r)
                    self.done = min(self.done + count, HALF_ROWS)

                def all_rows(self):
                    with dve.Fori(0, SLOTS // UNROLL) as i:
                        for r in range(UNROLL // 2):
                            self.row(r, i)
                    self.done = HALF_ROWS

                def finish(self):
                    self.rows(HALF_ROWS)
                    g = HALF_ROWS * (self.n + 1) + HALF_RING
                    dve.wait_ge(S("v_rows_done"), g)
                    for c, x in enumerate(halves(self.b)):
                        dve.wait_ge(S(f"half_sums{c}"), g)
                        taken(tt(x, x, bank("experts", 2 * self.n + c), ALU.add), "experts")
                    dve.wait_ge(S("experts_taken"), 2 * self.n + 2)

            kept = [0]

            def dots(l, b):
                n, k0 = 2 * l + b, kept[0]
                kept[0] += SLOTS // RING
                with dve.Fori(0, SLOTS // UNROLL) as i:
                    for k in range(UNROLL // RING):
                        dve.wait_ge(S("dots_kept"), i * (UNROLL // RING) + (k0 + k + 1))
                        for j in range(RING):
                            dve.wait_ge(S(f"u_row{j}"), i * (16 * UNROLL // RING) + 16 * (SLOTS // RING * n + k + 1))
                            v.tensor_tensor_reduce(out=ring_u[:, j, :], in0=ring_u[:, j, :], in1=xres[:, b, :], scale=1.0,
                                                   scalar=0.0, op0=ALU.mult, op1=ALU.add, accum_out=hstage[:, k, j:j + 1]
                                                   ).then_inc(S("u_rows_done"), 1)
                        dve.wait_ge(S("u_rows_done"), i * UNROLL + (SLOTS * n + RING * (k + 1) + RING))
                        v.tensor_copy(hid[:, b, bass.ds(i * UNROLL + RING * k, RING)], hstage[:, k, :]
                                      ).then_inc(S("dots_kept"), 1)
                dve.wait_ge(S("dots_kept"), kept[0] + 2)
                dve.sem_inc(S("hidden"), 1)

            class Dots:

                def __init__(self, l, b):
                    self.n, self.b, self.s = 2 * l + b, b, 0

                def rows(self, count):
                    for s in range(self.s, min(self.s + count, SLOTS)):
                        j = s % RING
                        dve.wait_ge(S(f"u_row{j}"), 16 * (SLOTS // RING * self.n + s // RING + 1))
                        v.tensor_tensor_reduce(out=ring_u[:, j, :], in0=ring_u[:, j, :], in1=xres[:, self.b, :], scale=1.0,
                                               scalar=0.0, op0=ALU.mult, op1=ALU.add, accum_out=hid[:, self.b, s:s + 1]
                                               ).then_inc(S("u_rows_done"), 1)
                    self.s = min(self.s + count, SLOTS)

                def finish(self):
                    self.rows(SLOTS)
                    dve.wait_ge(S("u_rows_done"), SLOTS * (self.n + 1) + RING)
                    dve.sem_inc(S("hidden"), 1)

            def mixer1(b, dot):
                v.memset(fw, 0.0).then_inc(S("f_zeroed"), 1)
                dot.rows(DOT_ROWS[0])
                for i in range(4):
                    dve.wait_ge(S("fox_qk_taken"), 4 * b + i + 1)
                    src = qc[:, 4 * i:4 * i + 4, :] if i < 2 else kc[:, 4 * i - 8:4 * i - 4, b * P:(b + 1) * P]
                    tt(SQ[:, 4 * i:4 * i + 4, :], src, src, ALU.mult).then_inc(S("squares"), 1)
                dot.rows(DOT_ROWS[1])
                dve.wait_ge(S("fox_f_taken"), b + 1)
                log_sigmoid(fz, fl, fz, "f_abs", "f_log", b + 1)
                c = fc[:, b * P:(b + 1) * P]
                go(v.tensor_tensor_scan(c, ones[:, 0:P], fz, fc[:, P - 1:P] if b else 0.0, ALU.mult, ALU.add))
                ts(fneg[:, b * P:(b + 1) * P], c, -1.0, None, ALU.mult).then_inc(S("decay_rows"), 1)
                dve.wait_ge(S("fox_rms_taken"), 4 * b + 4)
                for i in range(4):
                    st.then(v.reciprocal(RS[:, 4 * i:4 * i + 4, :], RS[:, 4 * i:4 * i + 4, :]))
                st.settle()
                for t in range(16):
                    gain = par("qn_g", t) if t < 8 else kn8[:, t - 8:t - 7]
                    x = qc[:, t, :] if t < 8 else kc[:, t - 8, b * P:(b + 1) * P]
                    ins = stt(x, x, gain, RS[:, t, :], ALU.mult, ALU.mult)
                    if t < 15:
                        st.then(ins)
                ins.then_inc(S("qk_normed"), 1)
                dot.rows(DOT_ROWS[2])
                w = P * (b + 1)
                for s in range(FH + 4):
                    if s < FH:
                        u = FH * b + s
                        ps = full(dve, "att", u)[:, 0:w]
                        if s >= 4:
                            dve.wait_ge(S("exped"), u - 3)
                        taken(v.tensor_tensor_reduce(out=lg[:, u % 4, 0:w], in0=ps, in1=causal_ts[:, SEQ + P - w:SEQ + P],
                                                     scale=1.0, scalar=-BIG, op0=ALU.add, op1=ALU.max,
                                                     accum_out=arec[:, u:u + 1]), "att")
                        dve.wait_ge(S("att_taken"), u + 1)
                        ts(amax[:, u:u + 1], arec[:, u:u + 1], -1.0, None, ALU.mult).then_inc(S("logits_max"), 1)
                    if 1 <= s < FH + 1:
                        u = FH * b + s - 1
                        dve.wait_ge(S("exped"), u + 1)
                        dve.wait_ge(S("logits_max"), u + 1)
                        go(v.reciprocal(arec[:, u:u + 1], asum[:, u:u + 1]))
                        ts(prob[:, u % 4, 0:w], prob[:, u % 4, 0:w], arec[:, u:u + 1], None, ALU.mult).then_inc(S("probs_ready"), 1)
                    if s >= 4 and s % 2 == 0:
                        i = (FH * b + s - 4) // 2
                        t = i % 8
                        taken(tt(oT[:, t, :], full(dve, "att_out", i)[:, 0:P], ogT[:, t, :], ALU.mult), "att_out")
                    dot.rows(DOT_ROWS[3])
                dve.wait_ge(S("att_out_taken"), 8 * b + 8)
                dve.sem_inc(S("mixed"), 1)
                dot.finish()

            def mixer1_tail(b):
                weigh(b, 1 - b)
                adds = Adds(b, 1 - b)
                for i in range(2):
                    adds.rows(EARLY_ROWS)
                    x = xres[:, b, i * 512:(i + 1) * 512]
                    taken(stt(x, x, ALPHA, full(dve, "mix_out", 4 + 2 * b + i), ALU.mult, ALU.add), "mix_out")
                dve.wait_ge(S("mix_out_taken"), 6 + 2 * b)
                layer_norm(3 + 2 * b)
                adds.rows(NORM_ROWS)
                route(1, b, PAIRS, lambda g: adds.rows(ROUTE_ROWS))
                adds.finish()

            dve.sem_inc(S("u_rows_done"), RING)
            for c in range(2):
                dve.sem_inc(S(f"half_sums{c}"), HALF_RING)
            dve.sem_inc(S("dots_kept"), 2)
            mixer0()
            dot = Dots(0, 0)
            route(0, 0, FIRST_GROUPS, lambda g: dot.rows(FIRST_DOTS[g]))
            dot.finish()
            weigh(0, 0)
            adds = Adds(0, 0)
            route(0, 1, PAIRS, lambda g: adds.rows(ROUTE_ROWS))
            adds.finish()
            layer_norm(2)
            mixer1(0, Dots(0, 1))
            mixer1_tail(0)
            layer_norm(4)
            mixer1(1, Dots(1, 0))
            mixer1_tail(1)
            layer_norm(6)
            dots(1, 1)
            weigh(1, 1)
            adds = Adds(1, 1)
            adds.all_rows()
            adds.finish()
            layer_norm(7)


def kernel(**inputs):
    import numpy as _np
    import concourse.bacc as _bacc
    from concourse.bass_utils import run_bass_kernel_spmd as _run

    nc = _bacc.Bacc("TRN2", target_bir_lowering=False, num_devices=1)
    arrays, T = {}, {}
    for name, value in inputs.items():
        a = _np.ascontiguousarray(value)
        arrays[name] = a
        T[name] = nc.dram_tensor(name, a.shape, mybir.dt.from_np(a.dtype), kind="ExternalInput").ap()
    out = nc.dram_tensor("out", (1, SEQ, D), F32, kind="ExternalOutput").ap()
    build(nc, T, out)
    r = _run(nc, [arrays], core_ids=[0])
    return r.results[0]["out"]
```
